# Optimizing a Trainium2 kernel written in Bass

```python
import math
import jax
import jax.numpy as jnp
from jax import lax
import numpy as np

D_MODEL = 1024
BATCH = 1
SEQ = 1024
DEPTH = 1
DEC_BATCH = 1
DEC_SEQ = 512
PAST_LEN = 128

D_MIX = 1024
D_CONV = 512
CONV_WIDTH = 31
CONV_PAD = CONV_WIDTH // 2
N_HEADS = 8
N_KV_HEADS = 2
HEAD_DIM = 64
KV_GROUP = N_HEADS // N_KV_HEADS
D_Q = N_HEADS * HEAD_DIM
D_KV = N_KV_HEADS * HEAD_DIM
D_IN = 2 * D_CONV + D_Q + 2 * D_KV
HALF_ROT = HEAD_DIM // 2
ROPE_THETA = 10000.0
GRID_W = 64
Q_BLOCK = 128
N_EXPERTS = 16
CAPACITY_FACTOR = 2
D_FF_EXPERT = 2048
D_PLE = 256
EPS = 1e-6

kernel_name = "hybrid_conv_attn_ec_encoder"

def rms_norm(x, g):
    xf = x.astype(jnp.float32)
    y = xf * lax.rsqrt(jnp.mean(xf * xf, axis=-1, keepdims=True) + EPS)
    return (y * g.astype(jnp.float32)).astype(x.dtype)

def layer_norm(x, g, b):
    xf = x.astype(jnp.float32)
    mu = jnp.mean(xf, axis=-1, keepdims=True)
    var = jnp.mean(jnp.square(xf - mu), axis=-1, keepdims=True)
    y = (xf - mu) * lax.rsqrt(var + EPS) * g.astype(jnp.float32) + b.astype(jnp.float32)
    return y.astype(x.dtype)

def axial_rope_tables(n_tok):
    rows = n_tok // GRID_W
    row_idx = jnp.repeat(jnp.arange(rows, dtype=jnp.float32), GRID_W)
    col_idx = jnp.tile(jnp.arange(GRID_W, dtype=jnp.float32), rows)
    freqs = 1.0 / (ROPE_THETA ** (jnp.arange(0, HALF_ROT, 2, dtype=jnp.float32) / HALF_ROT))
    ang_r = row_idx[:, None] * freqs[None, :]
    ang_c = col_idx[:, None] * freqs[None, :]
    return jnp.cos(ang_r), jnp.sin(ang_r), jnp.cos(ang_c), jnp.sin(ang_c)

def _rotate(x, cos, sin):
    half = x.shape[-1] // 2
    x1, x2 = x[..., :half], x[..., half:]
    c = cos[None, :, None, :].astype(x.dtype)
    s = sin[None, :, None, :].astype(x.dtype)
    return jnp.concatenate([x1 * c - x2 * s, x2 * c + x1 * s], axis=-1)

def apply_axial_rope(x, tables):
    cr, sr, cc, sc = tables
    return jnp.concatenate([_rotate(x[..., :HALF_ROT], cr, sr),
                            _rotate(x[..., HALF_ROT:], cc, sc)], axis=-1)

def conformer_conv(u, dw_w, dw_b, ln_g, ln_b):
    val, gate = u[..., :D_CONV], u[..., D_CONV:]
    g = val * jax.nn.sigmoid(gate)
    kern = dw_w[:, None, :].astype(g.dtype)
    c = lax.conv_general_dilated(g, kern, window_strides=(1,), padding=[(CONV_PAD, CONV_PAD)],
                                 dimension_numbers=('NWC', 'WIO', 'NWC'),
                                 feature_group_count=D_CONV)
    c = layer_norm(c + dw_b, ln_g, ln_b)
    return c * jax.nn.sigmoid(c)

def block_attention(q, k, v):
    B, T = q.shape[0], q.shape[1]
    nb = T // Q_BLOCK
    scale = HEAD_DIM ** -0.5
    qb = q.reshape(B, nb, Q_BLOCK, N_KV_HEADS, KV_GROUP, HEAD_DIM).transpose(1, 0, 2, 3, 4, 5)

    def one_block(qblk):
        s = jnp.einsum('bqkgd,bskd->bkgqs', qblk, k).astype(jnp.float32) * scale
        p = jax.nn.softmax(s, axis=-1).astype(v.dtype)
        return jnp.einsum('bkgqs,bskd->bqkgd', p, v)

    o = lax.map(one_block, qb)
    return o.transpose(1, 0, 2, 3, 4, 5).reshape(B, T, D_Q)

def expert_choice_ffn(h, w_router, w_gate, w_up, w_down):
    B, T, D = h.shape
    n_tok = B * T
    cap = CAPACITY_FACTOR * n_tok // N_EXPERTS
    xt = h.reshape(n_tok, D)
    aff = jax.nn.softmax((xt @ w_router).astype(jnp.float32), axis=-1)
    gates, idx = lax.top_k(aff.T, cap)
    xe = xt[idx]
    hid = jax.nn.silu(jnp.einsum('ecd,edf->ecf', xe, w_gate)) * jnp.einsum('ecd,edf->ecf', xe, w_up)
    ye = jnp.einsum('ecf,efd->ecd', hid, w_down) * gates[..., None].astype(h.dtype)
    out = jnp.zeros_like(xt).at[idx.reshape(-1)].add(ye.reshape(-1, D))
    return out.reshape(B, T, D)

def run_trunk(x, p, norm1_g, w_in, conv_dw_w, conv_dw_b, conv_ln_g, conv_ln_b, q_norm_g, k_norm_g,
              conv_out_g, attn_out_g, w_out, norm2_g, w_router, w_gate, w_up, w_down,
              ple_proj, ple_norm_g, ple_gate_w, ple_gate_b):
    B, T, _ = x.shape
    rope = axial_rope_tables(T)
    h = x
    for i in range(DEPTH):
        a = rms_norm(h, norm1_g[i])
        z = a @ w_in[i]
        o0 = 2 * D_CONV
        u = z[..., :o0]
        q = z[..., o0:o0 + D_Q].reshape(B, T, N_HEADS, HEAD_DIM)
        k = z[..., o0 + D_Q:o0 + D_Q + D_KV].reshape(B, T, N_KV_HEADS, HEAD_DIM)
        v = z[..., o0 + D_Q + D_KV:].reshape(B, T, N_KV_HEADS, HEAD_DIM)
        c_out = conformer_conv(u, conv_dw_w[i], conv_dw_b[i], conv_ln_g[i], conv_ln_b[i])
        q = apply_axial_rope(rms_norm(q, q_norm_g[i]), rope)
        k = apply_axial_rope(rms_norm(k, k_norm_g[i]), rope)
        a_out = block_attention(q, k, v)
        mix = jnp.concatenate([rms_norm(c_out, conv_out_g[i]), rms_norm(a_out, attn_out_g[i])], axis=-1)
        h = h + mix @ w_out[i]
        h = h + expert_choice_ffn(rms_norm(h, norm2_g[i]), w_router[i], w_gate[i], w_up[i], w_down[i])
        e = p[i] @ ple_proj[i]
        gate = jax.nn.sigmoid(rms_norm(h, ple_norm_g[i]) @ ple_gate_w[i] + ple_gate_b[i])
        h = h + gate * e
    return h

def setup_inputs(seed: int = 0) -> dict:
    key = jax.random.key(seed)
    ks = jax.random.split(key, 24)
    f32 = jnp.float32

    def nrm(k, shape, scale):
        return jax.random.normal(k, shape, f32) * scale

    def gain(k, shape):
        return 1.0 + 0.02 * jax.random.normal(k, shape, f32)

    return {
        "x_prompt": nrm(ks[0], (BATCH, SEQ, D_MODEL), 1.0),
        "x_sample": nrm(ks[1], (DEC_BATCH, DEC_SEQ, D_MODEL), 1.0),
        "p_prompt": nrm(ks[2], (DEPTH, BATCH, SEQ, D_PLE), 1.0),
        "p_sample": nrm(ks[3], (DEPTH, DEC_BATCH, DEC_SEQ, D_PLE), 1.0),
        "norm1_g": gain(ks[4], (DEPTH, D_MODEL)),
        "w_in": nrm(ks[5], (DEPTH, D_MODEL, D_IN), D_MODEL ** -0.5),
        "conv_dw_w": nrm(ks[6], (DEPTH, CONV_WIDTH, D_CONV), CONV_WIDTH ** -0.5),
        "conv_dw_b": nrm(ks[7], (DEPTH, D_CONV), 0.02),
        "conv_ln_g": gain(ks[8], (DEPTH, D_CONV)),
        "conv_ln_b": nrm(ks[9], (DEPTH, D_CONV), 0.02),
        "q_norm_g": gain(ks[10], (DEPTH, HEAD_DIM)),
        "k_norm_g": gain(ks[11], (DEPTH, HEAD_DIM)),
        "conv_out_g": gain(ks[12], (DEPTH, D_CONV)),
        "attn_out_g": gain(ks[13], (DEPTH, D_Q)),
        "w_out": nrm(ks[14], (DEPTH, D_MIX, D_MODEL), D_MIX ** -0.5),
        "norm2_g": gain(ks[15], (DEPTH, D_MODEL)),
        "w_router": nrm(ks[16], (DEPTH, D_MODEL, N_EXPERTS), D_MODEL ** -0.5),
        "w_gate": nrm(ks[17], (DEPTH, N_EXPERTS, D_MODEL, D_FF_EXPERT), D_MODEL ** -0.5),
        "w_up": nrm(ks[18], (DEPTH, N_EXPERTS, D_MODEL, D_FF_EXPERT), D_MODEL ** -0.5),
        "w_down": nrm(ks[19], (DEPTH, N_EXPERTS, D_FF_EXPERT, D_MODEL), D_FF_EXPERT ** -0.5),
        "ple_proj": nrm(ks[20], (DEPTH, D_PLE, D_MODEL), D_PLE ** -0.5),
        "ple_norm_g": gain(ks[21], (DEPTH, D_MODEL)),
        "ple_gate_w": nrm(ks[22], (DEPTH, D_MODEL, D_MODEL), D_MODEL ** -0.5),
        "ple_gate_b": nrm(ks[23], (DEPTH, D_MODEL), 0.02),
    }

def reference(x_prompt, x_sample, p_prompt, p_sample, norm1_g, w_in, conv_dw_w, conv_dw_b, conv_ln_g,
              conv_ln_b, q_norm_g, k_norm_g, conv_out_g, attn_out_g, w_out, norm2_g, w_router, w_gate,
              w_up, w_down, ple_proj, ple_norm_g, ple_gate_w, ple_gate_b):
    y_prompt = run_trunk(x_prompt, p_prompt, norm1_g, w_in, conv_dw_w, conv_dw_b, conv_ln_g, conv_ln_b,
                         q_norm_g, k_norm_g, conv_out_g, attn_out_g, w_out, norm2_g, w_router, w_gate,
                         w_up, w_down, ple_proj, ple_norm_g, ple_gate_w, ple_gate_b)
    y_sample = run_trunk(x_sample, p_sample, norm1_g, w_in, conv_dw_w, conv_dw_b, conv_ln_g, conv_ln_b,
                         q_norm_g, k_norm_g, conv_out_g, attn_out_g, w_out, norm2_g, w_router, w_gate,
                         w_up, w_down, ple_proj, ple_norm_g, ple_gate_w, ple_gate_b)
    return (y_prompt, y_sample)


_drawn_inputs = setup_inputs


def setup_inputs(seed=0):
    import zlib

    import numpy as np

    out = dict(_drawn_inputs(seed))
    spreads = {}
    factors = {'conv_dw_b': 2.814,
     'conv_ln_g': 4.361,
     'conv_ln_b': 4.934,
     'q_norm_g': 4.521,
     'k_norm_g': 4.664,
     'conv_out_g': 4.783,
     'attn_out_g': 4.619,
     'norm2_g': 4.944,
     'ple_norm_g': 8.0,
     'ple_gate_b': 8.0}
    for name, (base, spread) in spreads.items():
        noise = np.random.default_rng([zlib.crc32(name.encode()), seed]).standard_normal(out[name].shape)
        drawn = base * np.exp(spread * noise) if base else spread * noise
        out[name] = jnp.asarray(drawn.astype(out[name].dtype))
    for name, factor in factors.items():
        out[name] = (out[name] * factor).astype(out[name].dtype)
    return out
```

```python
from contextlib import ExitStack
from typing import NamedTuple

import concourse.bass as bass
from concourse import mybir

F32 = mybir.dt.float32
F32R = mybir.dt.float32r
U32 = mybir.dt.uint32
ALU = mybir.AluOpType
ACT = mybir.ActivationFunctionType
AX = mybir.AxisListType

P = 128
D = 1024
KD = D // P
T_PROMPT, T_SAMPLE = 1024, 512
T_ALL = T_PROMPT + T_SAMPLE
TILES = T_ALL // P
PTILES = T_PROMPT // P
CHUNK = 512
CHUNKS = T_ALL // CHUNK
D_CONV = 512
CT = D_CONV // P
TAPS = 31
PAD = TAPS // 2
HEADS, KV, HD = 8, 2, 64
D_Q = HEADS * HD
QT = D_Q // P
KV_GROUP = HEADS // KV
SCALE = HD ** -0.5
EPS = 1e-6
E = 16
CAP_P, CAP_S = 2 * T_PROMPT // E, 2 * T_SAMPLE // E
CAP = CAP_P + CAP_S
F_EXP = 2048
FT = F_EXP // P
D_PLE = 256
SEG = (0, T_PROMPT + 2 * PAD)
GLU_COLS = T_ALL + 4 * PAD
CHUNK_TILES = CHUNK // P


def chunk_pos(c):
    return (0, c * CHUNK) if c * CHUNK < T_PROMPT else (1, c * CHUNK - T_PROMPT)


class Step(NamedTuple):
    u: int
    j: int
    h4: int
    q0: int
    tok0: int
    nt: int
    tile: int
    po: int
    banks: int


class Kept:
    pass


class Chain:

    def __init__(self, eng, sem):
        self.eng, self.sem, self.n = eng, sem, 0

    def did(self, ins):
        ins.then_inc(self.sem, 1)
        self.n += 1
        return self.n

    def wait(self, n):
        self.eng.wait_ge(self.sem, n)


def stage_project(nc, K, io, sb, sem):
    flat = K.conv[:, :, :].rearrange("p c t -> p (c t)")
    x_ring = flat[:, 0:3 * D].rearrange("p (r d) -> p r d", r=3)
    gate_sig = flat[:, 3 * D:3 * D + 2 * T_ALL].rearrange("p (r c n) -> p r c n", r=2, c=CHUNKS)
    aT = sb("aT", [P, KD, T_ALL])
    w_ring = sb("w_ring", [P, 4, KD, P])
    square = sb("square", [P, 2, CHUNK])
    root = sb("root", [P, 2, CHUNK])
    inv = sb("inv", [P, 2, CHUNK])
    qn = sb("qn", [P, 2, CHUNK])
    by_cos = sb("by_cos", [P, 2, CHUNK])
    by_sin = sb("by_sin", [P, 2, CHUNK])
    cos = sb("cos", [P, T_PROMPT])
    sin = sb("sin", [P, T_PROMPT])
    junk = sb("junk", [P, D])
    g1 = sb("g1", [P, KD])
    qkg = sb("qkg", [P, 2])
    ssq = sb("ssq", [P, TILES])
    ms = sb("ms", [P, TILES])
    rstd = sb("rstd", [P, TILES])

    consts_loaded = sem("consts_loaded")
    x_loaded = [sem(f"x_loaded{i}") for i in range(3)]
    w_loaded = [sem(f"w_loaded{i}") for i in range(4)]
    ssq_ready, ms_ready, rstd_ready = sem("ssq_ready"), sem("ms_ready"), sem("rstd_ready")
    xn_ready, tr_done, aT_ready = sem("xn_ready"), sem("tr_done"), sem("aT_ready")
    z_done, sig_ready, glu_done = sem("z_done"), sem("sig_ready"), sem("glu_done")
    sq_ready, ms_done, root_ready, qn_ready = sem("sq_ready"), sem("ms_done"), sem("root_ready"), sem("qn_ready")
    rot_done, sin_ready, qk_ready, v_ready = sem("rot_done"), sem("sin_ready"), sem("qk_ready"), sem("v_ready")
    dve_own, half_ready = sem("dve_own1"), sem("half_ready")

    PS = K.PS
    CONSTS = 10
    SL = [s for i in range(CT) for s in (("gate", i), ("val", i))]
    SL += [("k", j) for j in range(KV)] + [("q", i) for i in range(QT)] + [("v", 0)]
    NW = len(SL)
    NQK0 = 2 * CT * CHUNKS
    NQK = (KV + QT) * CHUNKS
    NV0 = NQK0 + NQK
    w_in = io["w_in"].rearrange("a (k p) n -> (a p) k n", p=P)
    col0 = {"val": 0, "gate": D_CONV, "q": 2 * D_CONV, "k": 2 * D_CONV + D_Q, "v": 2 * D_CONV + D_Q + KV * HD}

    def consumer(n):
        if n < NQK0:
            i, c = divmod(n, CHUNKS)
            return (sig_ready if i % 2 == 0 else glu_done), (i // 2) * CHUNKS + c + 1
        if n < NV0:
            return qn_ready, n - NQK0 + 1
        return v_ready, n - NV0 + 1

    with nc.Block() as block:

        @block.sync
        def _(sp):
            def load_x(t):
                if t >= 3:
                    sp.wait_ge(tr_done, t - 2)
                sp.dma_start(x_ring[:, t % 3, :], io["x_rows"](t)).then_inc(x_loaded[t % 3], 16)

            def load_w(i):
                if i >= 4:
                    sp.wait_ge(z_done, CHUNKS * (i - 3))
                kind, n = SL[i]
                if kind == "k":
                    for d in range(2):
                        sp.dma_start(w_ring[:, i % 4, :, d * HD:(d + 1) * HD],
                                     w_in[:, :, col0["k"] + n * HD:col0["k"] + (n + 1) * HD]).then_inc(w_loaded[i % 4], 16)
                else:
                    c = col0[kind] + n * P
                    sp.dma_start(w_ring[:, i % 4], w_in[:, :, c:c + P]).then_inc(w_loaded[i % 4], 16)

            load_x(0)
            for dst, src in ((K.ident, io["ident"]), (g1, io["norm1_g"])):
                sp.dma_start(dst[:, :], src).then_inc(consts_loaded, 16)
            load_x(1)
            load_x(2)
            for dst, src in ((K.eps, io["eps_col"]), (K.head_ones, io["head_ones"]), (K.rot, io["rot"]),
                             (qkg, io["qk_gain"]), (cos, io["cos"]), (sin, io["sin"]), (K.conv_w, io["conv_w"]), (K.chan_mean, io["chan_mean"])):
                sp.dma_start(dst[:, :], src).then_inc(consts_loaded, 16)
            for i in range(4):
                load_w(i)
            for t in range(3, TILES):
                load_x(t)
            for i in range(4, NW):
                load_w(i)

        @block.gpsimd
        def _(pool):
            nc.gpsimd.memset(K.glu[:, :, :], 0.0).then_inc(K.glu_cleared, 1)
            nc.gpsimd.memset(K.v_aug[:, :, :, :], 1.0).then_inc(K.v_cleared, 1)
            nc.gpsimd.memset(K.minus_half[:, :], -0.5).then_inc(half_ready, 1)
            pool.wait_ge(half_ready, 1)
            for t in range(TILES):
                pool.wait_ge(ssq_ready, t + 1)
                nc.gpsimd.tensor_scalar(ms[:, t:t + 1], ssq[:, t:t + 1], 1.0 / D, EPS, ALU.mult, ALU.add).then_inc(ms_ready, 1)
                pool.wait_ge(ms_ready, t + 1)
                nc.gpsimd.tensor_tensor(rstd[:, t:t + 1], ms[:, t:t + 1], K.minus_half[:, :], ALU.pow).then_inc(rstd_ready, 1)

        @block.scalar
        def _(act):
            for t in range(TILES):
                act.wait_ge(x_loaded[t % 3], 16 * (t // 3 + 1))
                if t:
                    act.wait_ge(ssq_ready, t)
                nc.scalar.activation(junk[:, :], x_ring[:, t % 3, :], ACT.Square, accum_out=ssq[:, t:t + 1]).then_inc(ssq_ready, 1)
            act.wait_ge(consts_loaded, 16 * CONSTS)
            for p in range(CT):
                for c in range(CHUNKS):
                    act.wait_ge(z_done, 2 * p * CHUNKS + c + 1)
                    if p >= 2:
                        act.wait_ge(glu_done, (p - 2) * CHUNKS + c + 1)
                    nc.scalar.activation(gate_sig[:, p % 2, c, :], PS[:, 4 + (2 * p * CHUNKS + c) % 4, :], ACT.Sigmoid).then_inc(sig_ready, 1)

            def root_of(m):
                act.wait_ge(ms_done, m + 1)
                if m >= 2:
                    act.wait_ge(qn_ready, m - 1)
                nc.scalar.activation(root[:, m % 2, :], PS[:, m % 2, :], ACT.Sqrt, bias=K.eps[:, :]).then_inc(root_ready, 1)

            for m in range(NQK):
                act.wait_ge(z_done, NQK0 + m + 1)
                if m >= 2:
                    act.wait_ge(ms_done, m - 1)
                nc.scalar.activation(square[:, m % 2, :], PS[:, 4 + (NQK0 + m) % 4, :], ACT.Square).then_inc(sq_ready, 1)
                if m >= 1:
                    root_of(m - 1)
            root_of(NQK - 1)
            act.wait_ge(K.v_cleared, 1)
            for t in range(TILES):
                act.wait_ge(z_done, NV0 + t + 1)
                nc.scalar.copy(K.v_aug[:, t, :, 0:HD],
                               PS[:, 4 + (NV0 + t) % 4, 0:P].rearrange("p (j d) -> p j d", j=KV)).then_inc(v_ready, 1)

        @block.vector
        def _(dve):
            own = Chain(dve, dve_own)

            def to_aT(t):
                dve.wait_ge(tr_done, t + 1)
                b = 2 * (t % 2)
                nc.vector.tensor_tensor(aT[:, :, t * P:(t + 1) * P],
                                        PS[:, b:b + 2, :].rearrange("p b (k n) -> p (b k) n", k=4),
                                        g1[:, :].unsqueeze(2).broadcast_to((P, KD, P)), ALU.mult).then_inc(aT_ready, 1)

            dve.wait_ge(consts_loaded, 16 * CONSTS)
            for t in range(TILES):
                dve.wait_ge(rstd_ready, t + 1)
                nc.vector.tensor_scalar(x_ring[:, t % 3, :], x_ring[:, t % 3, :], rstd[:, t:t + 1], None, ALU.mult).then_inc(xn_ready, 1)
                if t:
                    to_aT(t - 1)
            to_aT(TILES - 1)
            dve.wait_ge(K.glu_cleared, 1)
            for p in range(CT):
                for c in range(CHUNKS):
                    n = (2 * p + 1) * CHUNKS + c
                    dve.wait_ge(z_done, n + 1)
                    dve.wait_ge(sig_ready, p * CHUNKS + c + 1)
                    g, t0 = chunk_pos(c)
                    o = SEG[g] + PAD + t0
                    nc.vector.tensor_tensor(K.glu[:, p, o:o + CHUNK], PS[:, 4 + n % 4, :], gate_sig[:, p % 2, c, :], ALU.mult).then_inc(glu_done, 1)
            for m in range(NQK):
                s, c = divmod(m, CHUNKS)
                i = m % 2
                kind, idx = SL[2 * CT + s]
                t0 = chunk_pos(c)[1]
                dve.wait_ge(root_ready, m + 1)
                own.wait(own.did(nc.vector.reciprocal(inv[:, i, :], root[:, i, :])))
                if m >= 2:
                    dve.wait_ge(rot_done, m - 1)
                gain = qkg[:, 0:1] if kind == "q" else qkg[:, 1:2]
                nc.vector.scalar_tensor_tensor(qn[:, i, :], PS[:, 4 + (NQK0 + m) % 4, :], gain, inv[:, i, :], ALU.mult, ALU.mult).then_inc(qn_ready, 1)
                dve.wait_ge(qn_ready, m + 1)
                own.did(nc.vector.tensor_tensor(by_cos[:, i, :], qn[:, i, :], cos[:, t0:t0 + CHUNK], ALU.mult))
                dve.wait_ge(rot_done, m + 1)
                nc.vector.tensor_tensor(by_sin[:, i, :], PS[:, 2 + i, :], sin[:, t0:t0 + CHUNK], ALU.mult).then_inc(sin_ready, 1)
                own.wait(own.n)
                dve.wait_ge(sin_ready, m + 1)
                dst = (K.qT if kind == "q" else K.kT)[:, idx, c * CHUNK:(c + 1) * CHUNK]
                nc.vector.tensor_tensor(dst, by_cos[:, i, :], by_sin[:, i, :], ALU.add).then_inc(qk_ready, 1)

        @block.tensor
        def _(pe):
            pe.wait_ge(consts_loaded, 16 * CONSTS)
            for t in range(TILES):
                pe.wait_ge(xn_ready, t + 1)
                if t >= 2:
                    pe.wait_ge(aT_ready, t - 1)
                for k in range(KD):
                    b = 2 * (t % 2) + k // 4
                    mm = nc.tensor.transpose(PS[:, b, (k % 4) * P:(k % 4 + 1) * P], x_ring[:, t % 3, k * P:(k + 1) * P], K.ident[:, :])
                mm.then_inc(tr_done, 1)

            def bank_free(n):
                if n >= 4:
                    pe.wait_ge(*consumer(n - 4))

            def mean_square(m):
                pe.wait_ge(sq_ready, m + 1)
                if m >= 2:
                    pe.wait_ge(root_ready, m - 1)
                nc.tensor.matmul(PS[:, m % 2, :], K.head_ones[:, :], square[:, m % 2, :], start=True, stop=True).then_inc(ms_done, 1)

            def rotate(m):
                pe.wait_ge(qn_ready, m + 1)
                if m >= 2:
                    pe.wait_ge(sin_ready, m - 1)
                nc.tensor.matmul(PS[:, 2 + m % 2, :], K.rot[:, :], qn[:, m % 2, :], start=True, stop=True).then_inc(rot_done, 1)

            loads = [0] * 4
            for i, (kind, _idx) in enumerate(SL):
                loads[i % 4] += 32 if kind == "k" else 16
                pe.wait_ge(w_loaded[i % 4], loads[i % 4])
                if kind == "v":
                    break
                for c in range(CHUNKS):
                    n = i * CHUNKS + c
                    if i == 0:
                        pe.wait_ge(aT_ready, min(TILES, (c + 1) * CHUNK_TILES))
                        if c == 0:
                            pe.wait_ge(aT_ready, CHUNK_TILES)
                    bank_free(n)
                    for k in range(KD):
                        mm = nc.tensor.matmul(PS[:, 4 + n % 4, :], w_ring[:, i % 4, k, :], aT[:, k, c * CHUNK:(c + 1) * CHUNK],
                                              start=(k == 0), stop=(k == KD - 1))
                    mm.then_inc(z_done, 1)
                    m = n - NQK0
                    if m == 0:
                        pe.wait_ge(aT_ready, TILES)
                    if m >= 1:
                        mean_square(m - 1)
                    if m >= 2:
                        rotate(m - 2)
            mean_square(NQK - 1)
            rotate(NQK - 2)
            for t in range(TILES):
                bank_free(NV0 + t)
                for k in range(KD):
                    mm = nc.tensor.matmul(PS[:, 4 + (NV0 + t) % 4, 0:P], aT[:, k, t * P:(t + 1) * P], w_ring[:, (NW - 1) % 4, k, :],
                                          start=(k == 0), stop=(k == KD - 1))
                mm.then_inc(z_done, 1)
                if t == 0:
                    rotate(NQK - 1)


def stage_attend(nc, K, io, sb, sem):
    prob = sb("prob", [P, 2, T_PROMPT])
    probT = sb("probT", [P, 2, PTILES, KV_GROUP, P])
    units = [(g, i, j) for g, n in ((0, PTILES), (1, TILES - PTILES)) for i in range(n) for j in range(KV)]
    STEPS = len(units) * KV_GROUP
    smax = sb("smax", [P, STEPS])
    nmax = sb("nmax", [P, STEPS])
    inv_sum = sb("inv_sum", [HD, 2, KV_GROUP * P])
    qk_done, nmax_ready, exp_done, tr_done = sem("qk_done"), sem("nmax_ready"), sem("exp_done"), sem("pt_done")
    probT_ready, pv_done, o_ready = sem("probT_ready"), sem("pv_done"), sem("o_ready")
    own_sem, conv_own = sem("dve_own2"), sem("conv_own")
    PS = K.PS

    def step(n):
        g, i, j = units[n // KV_GROUP]
        h4 = n % KV_GROUP
        tok0, ntile = (0, PTILES) if g == 0 else (T_PROMPT, TILES - PTILES)
        return Step(u=n // KV_GROUP, j=j, h4=h4, q0=tok0 + i * P, tok0=tok0, nt=ntile,
                    tile=2 * j + h4 // 2, po=HD * (h4 % 2), banks=ntile // 4)

    def scores(n):
        s = step(n)
        return PS[:, 2 * (n % 2):2 * (n % 2) + s.banks, :]

    with nc.Block() as block:

        @block.tensor
        def _(pe):
            def score(n):
                s = step(n)
                for b in range(s.banks):
                    mm = nc.tensor.matmul(PS[:, 2 * (n % 2) + b, :], K.qT[s.po:s.po + HD, s.tile, s.q0:s.q0 + P],
                                          K.kT[s.po:s.po + HD, s.j, s.tok0 + b * CHUNK:s.tok0 + (b + 1) * CHUNK], start=True, stop=True)
                mm.then_inc(qk_done, 1)

            def values(u, quarter):
                s = step(u * KV_GROUP)
                per = s.nt // 4
                if quarter == 0:
                    pe.wait_ge(probT_ready, KV_GROUP * (u + 1))
                    if u >= 2:
                        pe.wait_ge(o_ready, 2 * (u - 1))
                for st in range(quarter * per, (quarter + 1) * per):
                    mm = nc.tensor.matmul(PS[:, 6 + u % 2, :], K.v_aug[:, s.tok0 // P + st, s.j, :],
                                          probT[:, u % 2, st, :, :], start=(st == 0), stop=(st == s.nt - 1))
                if quarter == 3:
                    mm.then_inc(pv_done, 1)

            score(0)
            score(1)
            for n in range(STEPS):
                s = step(n)
                pe.wait_ge(exp_done, n + 1)
                if n >= 1:
                    pe.wait_ge(probT_ready, n)
                for st in range(s.nt):
                    mm = nc.tensor.transpose(PS[:, 4 + st // 4, (st % 4) * P:(st % 4 + 1) * P], prob[:, n % 2, st * P:(st + 1) * P], K.ident[:, :])
                mm.then_inc(tr_done, 1)
                if n + 2 < STEPS:
                    score(n + 2)
                if s.u >= 1:
                    values(s.u - 1, s.h4)
            for q in range(4):
                values(len(units) - 1, q)

        @block.scalar
        def _(act):
            def copy_out(n):
                s = step(n)
                act.wait_ge(tr_done, n + 1)
                if s.u >= 2:
                    act.wait_ge(pv_done, s.u - 1)
                nc.scalar.copy(probT[:, s.u % 2, 0:s.nt, s.h4, :],
                               PS[:, 4:4 + s.banks, :].rearrange("p b (k n) -> p (b k) n", k=4)).then_inc(probT_ready, 1)

            for n in range(STEPS):
                s = step(n)
                act.wait_ge(nmax_ready, n + 1)
                if n >= 2:
                    act.wait_ge(tr_done, n - 1)
                nc.scalar.activation(prob[:, n % 2, 0:s.nt * P], scores(n).rearrange("p b n -> p (b n)"), ACT.Exp,
                                     bias=nmax[:, n:n + 1], scale=SCALE).then_inc(exp_done, 1)
                if n >= 1:
                    copy_out(n - 1)
            copy_out(STEPS - 1)

        @block.vector
        def _(dve):
            own = Chain(dve, own_sem)
            conv = Chain(dve, conv_own)
            OPS = CT * TAPS * 2

            def conv_tap(k):
                ct, r = divmod(k, 2 * TAPS)
                tap, g = divmod(r, 2)
                n = T_PROMPT if g == 0 else T_SAMPLE
                src = K.glu[:, ct, SEG[g] + tap:SEG[g] + tap + n]
                acc = K.conv[:, ct, g * T_PROMPT:g * T_PROMPT + n]
                w = K.conv_w[:, ct * (TAPS + 1) + tap:ct * (TAPS + 1) + tap + 1]
                if tap == 0:
                    b = K.conv_w[:, ct * (TAPS + 1) + TAPS:(ct + 1) * (TAPS + 1)]
                    conv.did(nc.vector.tensor_scalar(acc, src, w, b, ALU.mult, ALU.add))
                else:
                    conv.wait(k - 1)
                    conv.did(nc.vector.scalar_tensor_tensor(acc, src, w, acc, ALU.mult, ALU.add))

            def normalise(u):
                s = step(u * KV_GROUP)
                dve.wait_ge(pv_done, u + 1)
                own.wait(own.did(nc.vector.reciprocal(inv_sum[:, u % 2, :], PS[HD:P, 6 + u % 2, :])))
                for odd in range(2):
                    out = K.qT[odd * HD:(odd + 1) * HD, 2 * s.j:2 * s.j + 2, s.q0:s.q0 + P]
                    pick = lambda ap: ap.rearrange("p (a b n) -> p a b n", b=2, n=P)[:, :, odd, :]
                    nc.vector.tensor_tensor(out, pick(PS[0:HD, 6 + u % 2, :]), pick(inv_sum[:, u % 2, :]), ALU.mult).then_inc(o_ready, 1)

            done = 0
            for n in range(STEPS):
                dve.wait_ge(qk_done, n + 1)
                k = own.did(nc.vector.tensor_reduce(smax[:, n:n + 1], scores(n).rearrange("p b n -> p (b n)"), AX.X, ALU.max))
                own.wait(k)
                nc.vector.tensor_scalar(nmax[:, n:n + 1], smax[:, n:n + 1], -SCALE, None, ALU.mult).then_inc(nmax_ready, 1)
                if n % KV_GROUP == 0 and n >= 2 * KV_GROUP:
                    normalise(n // KV_GROUP - 2)
                upto = OPS * (n + 1) // STEPS
                for k in range(done, upto):
                    conv_tap(k)
                done = upto
            normalise(len(units) - 2)
            normalise(len(units) - 1)


def stage_mix_route(nc, K, io, sb, sem):
    w_out = sb("w_out", [P, KD, D])
    sq = sb("sq", [P, CT, CHUNK])
    root = sb("root3", [P, CHUNK])
    inv = sb("inv3", [P, CHUNK])
    g2 = sb("g2", [P, D])
    w_r = sb("w_r", [P, KD, E])
    cg = sb("cg", [P, 4 * CT])
    h = sb("h", [P, 3, D])
    xn = sb("xn", [P, 3, D])
    junk = sb("junk3", [P, D])
    xnT = sb("xnT", [P, KD, P])
    ssq, ms, rstd = sb("ssq3", [P, TILES]), sb("ms3", [P, TILES]), sb("rstd3", [P, TILES])
    rt = sb("rt", [P, 2, 4])
    ex = sb("ex", [P, 2, E])
    aff = sb("aff", [P, 2, E])
    affP, affS = sb("affP", [E, T_PROMPT]), sb("affS", [E, T_SAMPLE])
    valP, valS = sb("valP", [E, CAP_P]), sb("valS", [E, 2, CAP_S])
    idxP, idxS = sb("idxP", [E, CAP_P], U32), sb("idxS", [E, CAP_S], U32)
    idxPf, idxSf = sb("idxPf", [E, CAP_P]), sb("idxSf", [E, CAP_S])
    pT = sb("pT", [P, 2, 2, P])
    p_sb = sb("p_sb", [P, 2, D_PLE])
    w_pp = sb("w_pp", [P, 2, D])
    e_sb = sb("e_sb", [P, 2, D])

    loaded = sem("loaded3")
    wout_loaded = sem("wout_loaded")
    x_loaded = [sem(f"x3_loaded{i}") for i in range(3)]
    stat_ready, stat_done = sem("stat_ready"), sem("stat_done")
    centred, root_ready, mix_ready = sem("centred"), sem("root3_ready"), sem("mix_ready")
    silu_ready, inv_ready = sem("silu_ready"), sem("inv_ready")
    out_done, h_ready, ssq_ready, ms_ready, rstd_ready = (sem(f"{n}3") for n in ("out_done", "h_ready", "ssq", "ms", "rstd"))
    xn_ready, tr_done, xnT_ready, logit_done, exp_ready = (sem(f"{n}3") for n in ("xn_ready", "tr_done", "xnT_ready", "logit_done", "exp_ready"))
    aff_ready, affT_done, affT_ready = sem("aff_ready"), sem("affT_done"), sem("affT_ready")
    h_stored = [sem(f"h_stored{i}") for i in range(3)]
    xn_stored = [sem(f"xn_stored{i}") for i in range(3)]
    topk_ready, topkT_done = sem("topk_ready"), sem("topkT_done")
    p_loaded = [sem(f"p_loaded{i}") for i in range(2)]
    e_stored = [sem(f"e_stored{i}") for i in range(2)]
    pT_done, pT_ready, e_done, e_ready = sem("pT_done"), sem("pT_ready"), sem("e_done"), sem("e_ready")
    own_sem = sem("dve_own3")
    PS = K.PS
    NEG = -1.0

    def conv_of(c):
        return K.conv[:, :, c * CHUNK:(c + 1) * CHUNK]

    def attn_of(c):
        return K.qT[:, :, c * CHUNK:(c + 1) * CHUNK]

    MEAN, VAR, MSC, MSA = range(4)

    with nc.Block() as block:

        @block.sync
        def _(sp):
            for dst, src in ((cg[:, :], io["chan_gain"]), (w_r[:, :, :], io["w_router"].rearrange("a (k p) n -> (a p) k n", p=P)),
                             (g2[:, :], io["norm2_g"].partition_broadcast(P)),
                             (w_pp[:, :, :], io["ple_proj"].rearrange("a (k p) n -> (a p) k n", p=P))):
                sp.dma_start(dst, src).then_inc(loaded, 16)
            sp.dma_start(w_out[:, :, :], io["w_out"].rearrange("a (k p) n -> (a p) k n", p=P)).then_inc(wout_loaded, 16)
            for t in range(TILES + 1):
                if t < TILES:
                    if t >= 3:
                        sp.wait_ge(h_stored[t % 3], 16 * (t // 3))
                        sp.wait_ge(ssq_ready, t - 2)
                        sp.wait_ge(xn_ready, t - 2)
                    sp.dma_start(h[:, t % 3, :], io["x_rows"](t)).then_inc(x_loaded[t % 3], 16)
                if t >= 1:
                    s = t - 1
                    sp.wait_ge(h_ready, s + 1)
                    sp.dma_start(K.h_rows(s), h[:, s % 3, :]).then_inc(h_stored[s % 3], 16)
                    sp.wait_ge(xn_ready, s + 1)
                    sp.dma_start(K.xn_rows(s), xn[:, s % 3, :]).then_inc(xn_stored[s % 3], 16)
            for t in range(TILES + 1):
                if t < TILES:
                    if t >= 2:
                        sp.wait_ge(pT_done, t - 1)
                    sp.dma_start(p_sb[:, t % 2, :], io["p_rows"](t)).then_inc(p_loaded[t % 2], 16)
                if t >= 1:
                    sp.wait_ge(e_ready, 2 * t)
                    sp.dma_start(K.e_rows(t - 1), e_sb[:, (t - 1) % 2, :]).then_inc(e_stored[(t - 1) % 2], 16)
            for i in range(3):
                sp.wait_ge(h_stored[i], 16 * (TILES // 3))
                sp.wait_ge(xn_stored[i], 16 * (TILES // 3))
            for i in range(2):
                sp.wait_ge(e_stored[i], 16 * (TILES // 2))

        @block.gpsimd
        def _(pool):
            for t in range(TILES):
                pool.wait_ge(ssq_ready, t + 1)
                nc.gpsimd.tensor_scalar(ms[:, t:t + 1], ssq[:, t:t + 1], 1.0 / D, EPS, ALU.mult, ALU.add).then_inc(ms_ready, 1)
                pool.wait_ge(ms_ready, t + 1)
                nc.gpsimd.tensor_tensor(rstd[:, t:t + 1], ms[:, t:t + 1], K.minus_half[:, :], ALU.pow).then_inc(rstd_ready, 1)

        def stat_no(c, which):
            return 4 * c + which + 1

        @block.scalar
        def _(act):
            act.wait_ge(loaded, 64)

            def square_of(src, c, which):
                nc.scalar.activation(sq[:, :, :], src, ACT.Square).then_inc(stat_ready, 1)

            def take_root(c, which):
                act.wait_ge(stat_done, stat_no(c, which))
                if 3 * c + which > 1:
                    act.wait_ge(inv_ready, 3 * c + which - 1)
                nc.scalar.activation(root[:, :], PS[:, 4, :], ACT.Sqrt, bias=K.eps[:, :]).then_inc(root_ready, 1)

            def chunk_norms(c):
                act.wait_ge(centred, 2 * c + 1)
                if c:
                    act.wait_ge(stat_done, stat_no(c - 1, MSA))
                square_of(conv_of(c), c, VAR)
                take_root(c, VAR)
                act.wait_ge(centred, 2 * c + 2)
                for i in range(CT):
                    s = nc.scalar.activation(conv_of(c)[:, i, :], conv_of(c)[:, i, :], ACT.Silu, bias=cg[:, CT + i:CT + i + 1],
                                             scale=cg[:, i:i + 1])
                s.then_inc(silu_ready, 1)
                act.wait_ge(silu_ready, c + 1)
                square_of(conv_of(c), c, MSC)
                take_root(c, MSC)
                square_of(attn_of(c), c, MSA)
                take_root(c, MSA)

            def route(t):
                act.wait_ge(logit_done, t + 1)
                act.wait_ge(aff_ready, 3 * t + 1)
                nc.scalar.activation(ex[:, t % 2, :], PS[:, 5, 0:E], ACT.Exp, bias=rt[:, t % 2, 0:1],
                                     accum_out=rt[:, t % 2, 1:2]).then_inc(exp_ready, 1)

            chunk_norms(0)
            for t in range(TILES + 3):
                if t < TILES and t % CHUNK_TILES == 1 and t // CHUNK_TILES + 1 < CHUNKS:
                    chunk_norms(t // CHUNK_TILES + 1)
                if t < TILES:
                    act.wait_ge(h_ready, t + 1)
                    if t:
                        act.wait_ge(ssq_ready, t)
                    nc.scalar.activation(junk[:, :], h[:, t % 3, :], ACT.Square, accum_out=ssq[:, t:t + 1]).then_inc(ssq_ready, 1)
                if 1 <= t < TILES + 1:
                    act.wait_ge(tr_done, t)
                    if t >= 2:
                        act.wait_ge(logit_done, t - 1)
                    nc.scalar.copy(xnT[:, :, :], PS[:, 6:8, :].rearrange("p b (k n) -> p (b k) n", k=4)).then_inc(xnT_ready, 1)
                if 2 <= t < TILES + 2:
                    route(t - 2)
            for t in range(TILES):
                act.wait_ge(pT_done, t + 1)
                if t >= 2:
                    act.wait_ge(e_done, t - 1)
                nc.scalar.copy(pT[:, t % 2, :, :], PS[:, 6 + t % 2, 0:2 * P].rearrange("p (k n) -> p k n", k=2)).then_inc(pT_ready, 1)
                act.wait_ge(e_done, t + 1)
                if t >= 2:
                    act.wait_ge(e_stored[t % 2], 16 * (t // 2))
                for half in range(2):
                    nc.scalar.copy(e_sb[:, t % 2, half * CHUNK:(half + 1) * CHUNK], PS[:, 2 * (t % 2) + half, :]).then_inc(e_ready, 1)

        @block.vector
        def _(dve):
            own = Chain(dve, own_sem)
            roots = [0]

            def over_tiles(ap):
                return ap.unsqueeze(1).broadcast_to((P, CT, CHUNK))

            def invert(user, count):
                if roots[0]:
                    dve.wait_ge(user, count)
                roots[0] += 1
                dve.wait_ge(root_ready, roots[0])
                nc.vector.reciprocal(inv[:, :], root[:, :]).then_inc(inv_ready, 1)
                dve.wait_ge(inv_ready, roots[0])

            def chunk_norms(c):
                dve.wait_ge(stat_done, stat_no(c, MEAN))
                nc.vector.tensor_tensor(conv_of(c), conv_of(c), over_tiles(PS[:, 4, :]), ALU.subtract).then_inc(centred, 1)
                invert(mix_ready, (CT + QT) * c)
                dve.wait_ge(centred, 2 * c + 1)
                nc.vector.tensor_tensor(conv_of(c), conv_of(c), over_tiles(inv[:, :]), ALU.mult).then_inc(centred, 1)
                invert(centred, 2 * c + 2)
                for i in range(CT):
                    nc.vector.scalar_tensor_tensor(conv_of(c)[:, i, :], conv_of(c)[:, i, :], cg[:, 2 * CT + i:2 * CT + i + 1], inv[:, :],
                                                   ALU.mult, ALU.mult).then_inc(mix_ready, 1)
                invert(mix_ready, (CT + QT) * c + CT)
                for i in range(QT):
                    nc.vector.scalar_tensor_tensor(attn_of(c)[:, i, :], attn_of(c)[:, i, :], cg[:, 3 * CT + i:3 * CT + i + 1], inv[:, :],
                                                   ALU.mult, ALU.mult).then_inc(mix_ready, 1)

            def residual(t):
                dve.wait_ge(out_done, t + 1)
                dve.wait_ge(x_loaded[t % 3], 16 * (t // 3 + 1))
                b = 2 * (t % 2)
                nc.vector.tensor_tensor(h[:, t % 3, :].rearrange("p (b n) -> p b n", b=2), PS[:, b:b + 2, :],
                                        h[:, t % 3, :].rearrange("p (b n) -> p b n", b=2), ALU.add).then_inc(h_ready, 1)

            def norm(t):
                dve.wait_ge(rstd_ready, t + 1)
                dve.wait_ge(h_ready, t + 1)
                if t >= 3:
                    dve.wait_ge(xn_stored[t % 3], 16 * (t // 3))
                    dve.wait_ge(tr_done, t - 2)
                nc.vector.scalar_tensor_tensor(xn[:, t % 3, :], h[:, t % 3, :], rstd[:, t:t + 1], g2[:, :], ALU.mult, ALU.mult).then_inc(xn_ready, 1)

            def route(t):
                i = t % 2
                dve.wait_ge(logit_done, t + 1)
                if t >= 2:
                    dve.wait_ge(exp_ready, t - 1)
                nc.vector.tensor_reduce(rt[:, i, 0:1], PS[:, 5, 0:E], AX.X, ALU.max, negate=True).then_inc(aff_ready, 1)
                dve.wait_ge(exp_ready, t + 1)
                nc.vector.reciprocal(rt[:, i, 2:3], rt[:, i, 1:2]).then_inc(aff_ready, 1)
                dve.wait_ge(aff_ready, 3 * t + 2)
                if t >= 2:
                    dve.wait_ge(affT_done, t - 1)
                nc.vector.tensor_scalar(aff[:, i, :], ex[:, i, :], rt[:, i, 2:3], None, ALU.mult).then_inc(aff_ready, 1)

            def keep_affinity(t):
                dve.wait_ge(affT_done, t + 1)
                dst = affP[:, t * P:(t + 1) * P] if t < PTILES else affS[:, (t - PTILES) * P:(t - PTILES + 1) * P]
                nc.vector.tensor_copy(dst, PS[0:E, 5, CHUNK // 2:CHUNK // 2 + P]).then_inc(affT_ready, 1)

            def top(vals, idx, a, rounds):
                for r in range(rounds):
                    v8, i8 = vals[:, 8 * r:8 * r + 8], idx[:, 8 * r:8 * r + 8]
                    own.wait(own.did(nc.vector.max(v8, a)))
                    own.wait(own.did(nc.vector.max_index(i8, v8, a)))
                    own.wait(own.did(nc.vector.match_replace(a, v8, a, NEG)))

            dve.wait_ge(loaded, 64)
            chunk_norms(0)
            for t in range(TILES + 3):
                if t < TILES and t % CHUNK_TILES == 1 and t // CHUNK_TILES + 1 < CHUNKS:
                    chunk_norms(t // CHUNK_TILES + 1)
                if t < TILES:
                    residual(t)
                    norm(t)
                if 3 <= t:
                    keep_affinity(t - 3)
                if 2 <= t < TILES + 2:
                    route(t - 2)
            dve.wait_ge(affT_ready, TILES)
            top(valP[:, :], idxP[:, :], affP[:, :], CAP_P // 8)
            top(valS[:, 0, :], idxS[:, :], affS[:, :], CAP_S // 8)
            nc.vector.tensor_copy(idxPf[:, :], idxP[:, :]).then_inc(topk_ready, 1)
            nc.vector.tensor_copy(idxSf[:, :], idxS[:, :]).then_inc(topk_ready, 1)
            nc.vector.tensor_copy(valS[:, 1, :], valS[:, 0, :]).then_inc(topk_ready, 1)
            dve.wait_ge(topkT_done, 1)
            own.did(nc.vector.tensor_copy(K.idxT_p[:, 0:E], PS[:, 5, 0:E]))
            own.did(nc.vector.tensor_copy(K.idxT_s[:, 0:E], PS[0:CAP_S, 5, E:2 * E]))
            own.did(nc.vector.tensor_copy(K.gateT_p[:, :], PS[:, 5, 2 * E:3 * E]))
            own.did(nc.vector.tensor_copy(K.gateT_s[:, :], PS[:, 5, 3 * E:4 * E]))

        @block.tensor
        def _(pe):
            def mean_of(src, c, which):
                for i in range(CT):
                    mm = nc.tensor.matmul(PS[:, 4, :], K.chan_mean[:, :], src[:, i, :], start=(i == 0), stop=(i == CT - 1))
                mm.then_inc(stat_done, 1)

            def first_mean(c):
                if c:
                    pe.wait_ge(root_ready, 3 * c)
                mean_of(conv_of(c), c, MEAN)

            def other_means(c):
                for n, which in enumerate((VAR, MSC, MSA)):
                    pe.wait_ge(stat_ready, 3 * c + n + 1)
                    if n == 0:
                        pe.wait_ge(centred, 2 * c + 1)
                    else:
                        pe.wait_ge(root_ready, 3 * c + n)
                    mean_of(sq, c, which)

            def transposes(t):
                pe.wait_ge(xn_ready, t + 1)
                if t:
                    pe.wait_ge(xnT_ready, t)
                for k in range(KD):
                    mm = nc.tensor.transpose(PS[:, 6 + k // 4, (k % 4) * P:(k % 4 + 1) * P], xn[:, t % 3, k * P:(k + 1) * P], K.ident[:, :])
                mm.then_inc(tr_done, 1)

            def logits(t):
                pe.wait_ge(xnT_ready, t + 1)
                if t:
                    pe.wait_ge(affT_ready, t)
                for k in range(KD):
                    mm = nc.tensor.matmul(PS[:, 5, 0:E], xnT[:, k, :], w_r[:, k, :], start=(k == 0), stop=(k == KD - 1))
                mm.then_inc(logit_done, 1)

            def turn_affinity(t):
                pe.wait_ge(aff_ready, 3 * t + 3)
                nc.tensor.transpose(PS[0:E, 5, CHUNK // 2:CHUNK // 2 + P], aff[:, t % 2, :], K.ident[:, :]).then_inc(affT_done, 1)

            pe.wait_ge(loaded, 64)
            first_mean(0)
            other_means(0)
            pe.wait_ge(wout_loaded, 16)
            for t in range(TILES + 3):
                c = t // CHUNK_TILES
                if t < TILES and t % CHUNK_TILES == 1 and c + 1 < CHUNKS:
                    first_mean(c + 1)
                if t < TILES:
                    if t % CHUNK_TILES == 0:
                        pe.wait_ge(mix_ready, (CT + QT) * (c + 1))
                    if t >= 2:
                        pe.wait_ge(h_ready, t - 1)
                    for k in range(KD):
                        lhs = (K.conv if k < CT else K.qT)[:, k % CT, t * P:(t + 1) * P]
                        for half in range(2):
                            mm = nc.tensor.matmul(PS[:, 2 * (t % 2) + half, :], lhs, w_out[:, k, half * CHUNK:(half + 1) * CHUNK],
                                                  start=(k == 0), stop=(k == KD - 1))
                    mm.then_inc(out_done, 1)
                if t < TILES and t % CHUNK_TILES == 1 and c + 1 < CHUNKS:
                    other_means(c + 1)
                if 3 <= t:
                    turn_affinity(t - 3)
                if 1 <= t < TILES + 1:
                    transposes(t - 1)
                if 2 <= t < TILES + 2:
                    logits(t - 2)
            for t in range(TILES):
                pe.wait_ge(p_loaded[t % 2], 16 * (t // 2 + 1))
                if t < 2:
                    pe.wait_ge(xnT_ready, TILES)
                    pe.wait_ge(h_ready, TILES)
                else:
                    pe.wait_ge(pT_ready, t - 1)
                    pe.wait_ge(e_ready, 2 * (t - 1))
                for k in range(2):
                    mm = nc.tensor.transpose(PS[:, 6 + t % 2, k * P:(k + 1) * P], p_sb[:, t % 2, k * P:(k + 1) * P], K.ident[:, :])
                mm.then_inc(pT_done, 1)
                pe.wait_ge(pT_ready, t + 1)
                for k in range(2):
                    for half in range(2):
                        mm = nc.tensor.matmul(PS[:, 2 * (t % 2) + half, :], pT[:, t % 2, k, :], w_pp[:, k, half * CHUNK:(half + 1) * CHUNK],
                                              start=(k == 0), stop=(k == 1))
                mm.then_inc(e_done, 1)
            pe.wait_ge(topk_ready, 3)
            pe.wait_ge(affT_ready, TILES)
            small = K.ident[0:E, 0:E]
            nc.tensor.transpose(PS[:, 5, 0:E], idxPf[:, :], small)
            nc.tensor.transpose(PS[0:CAP_S, 5, E:2 * E], idxSf[:, :], small)
            nc.tensor.transpose(PS[:, 5, 2 * E:3 * E], valP[:, :], small)
            nc.tensor.transpose(PS[:, 5, 3 * E:4 * E], valS[:, :, :].rearrange("e a c -> e (a c)"), small).then_inc(topkT_done, 1)


def stage_experts(nc, K, io, sb, sem):
    RAW, HL = 6, 4
    NCH = 3 * FT // 2
    CC = 2048
    raw = sb("raw", [P, RAW, CC])
    wh, wl = sb("wh", [P, HL, CC], F32R), sb("wl", [P, HL, CC], F32R)
    xe_p, xe_s = sb("xe_p", [CAP_P, D]), sb("xe_s", [CAP_S, D])
    xhl = sb("xhl", [P, KD, 2, CAP], F32R)
    hhl = sb("hhl", [P, FT, 2 * CAP], F32R)
    HIGH, LOW_S, LOW_P, BOTH_S = slice(0, CAP), slice(CAP, CAP + CAP_S), slice(CAP + CAP_S, 2 * CAP), slice(CAP_P, CAP_P + 2 * CAP_S)
    gsum, usum, sg, hid = (sb(n, [P, 2, CAP]) for n in ("gsum", "usum", "sg", "hid"))
    y_p, y_s, y_low = sb("y_p", [CAP_P, D]), sb("y_s", [CAP_S, D]), sb("y_low", [CAP_S, D])
    ix_p, ix_s, sx_p, sx_s = sb("ix_p", [P, 1], U32), sb("ix_s", [CAP_S, 1], U32), sb("sx_p", [P, 1], U32), sb("sx_s", [CAP_S, 1], U32)
    gt_p, gt_s = sb("gt_p", [P, 1]), sb("gt_s", [P, 1])

    raw_loaded = [sem(f"raw_loaded{i}") for i in range(RAW)]
    high_ready = sem("high_ready")
    split_done = sem("split_done")
    down_used = sem("down_used")
    gathered_p, gathered_s = sem("gathered_p"), sem("gathered_s")
    index_ready, gates_ready, sindex_ready = sem("index_ready"), sem("gates_ready"), sem("sindex_ready")
    rows_asked = sem("rows_asked")
    xt_done, xh_ready, xl_ready = sem("xt_done"), sem("xh_ready"), sem("xl_ready")
    gate_done, up_done = sem("gate_done"), sem("up_done")
    gsum_ready, usum_ready = sem("gsum_ready"), sem("usum_ready")
    sg_ready, hid_ready, hh_ready, hl_ready = sem("sg_ready"), sem("hid_ready"), sem("hh_ready"), sem("hl_ready")
    yp_ready, ylow_ready, ys_ready = sem("yp_ready"), sem("ylow_ready"), sem("ys_ready")
    scat_p, scat_s = sem("scattered_p"), sem("scattered_s")
    PS = K.PS

    wg = io["w_gate"].rearrange("a e (k p) f -> (a e) p k f", p=P)
    wu = io["w_up"].rearrange("a e (k p) f -> (a e) p k f", p=P)
    wd = io["w_down"].rearrange("a e (k p) n -> (a e) p k n", p=P)

    def split_ready(eng, e, c):
        eng.wait_ge(split_done, e * NCH + (RAW + c + 1))

    with nc.Block() as block:

        @block.sync
        def _(sp):
            with sp.Fori(0, E) as e:
                for c in range(NCH):
                    sp.wait_ge(split_done, e * NCH + (c + 1))
                    dst = raw[:, c % RAW, :]
                    if c < FT:
                        src = (wg if c % 2 == 0 else wu)[bass.ds(e, 1), :, :, (c // 2) * 2 * P:(c // 2 + 1) * 2 * P].rearrange("e p k f -> (e p) k f")
                        dst = dst.rearrange("p (k f) -> p k f", k=KD)
                    else:
                        i = c - FT
                        src = wd[bass.ds(e, 1), :, 2 * i:2 * i + 2, :].rearrange("e p k n -> (e p) k n")
                        dst = dst.rearrange("p (k n) -> p k n", k=2)
                    sp.dma_start(dst, src).then_inc(raw_loaded[c % RAW], 16)
            sp.wait_ge(scat_p, 16 * E)
            sp.wait_ge(scat_s, 16 * E)

        def loaded_wait(eng, e, c):
            eng.wait_ge(raw_loaded[c % RAW], e * (16 * NCH // RAW) + 16 * (c // RAW + 1))

        @block.gpsimd
        def _(pool):
            def gather(e, nth):
                nc.gpsimd.tensor_copy(ix_p[:, :], K.idxT_p[:, bass.ds(e, 1)]).then_inc(index_ready, 1)
                nc.gpsimd.tensor_copy(ix_s[:, :], K.idxT_s[:, bass.ds(e, 1)]).then_inc(index_ready, 1)
                pool.wait_ge(index_ready, nth * 2 + 2)
                pool.sem_inc(rows_asked, 1)
                nc.gpsimd.indirect_dma_start(xe_p[:, :], None, K.xn_p, bass.IndirectOffsetOnAxis(ap=ix_p[:, :], axis=0)).then_inc(gathered_p, 16)
                nc.gpsimd.indirect_dma_start(xe_s[:, :], None, K.xn_s, bass.IndirectOffsetOnAxis(ap=ix_s[:, :], axis=0)).then_inc(gathered_s, 16)

            def combine(f, nth):
                i = f % 2
                pool.wait_ge(sg_ready, nth + (f + 1))
                pool.wait_ge(usum_ready, nth + (f + 3))
                nc.gpsimd.tensor_tensor(hid[:, i, :], sg[:, i, :], usum[:, i, :], ALU.mult).then_inc(hid_ready, 1)
                pool.wait_ge(hh_ready, nth + (f + 1))
                nc.gpsimd.tensor_tensor(hhl[:, f, LOW_P], hid[:, i, 0:CAP_P], hhl[:, f, 0:CAP_P].bitcast(F32), ALU.subtract).then_inc(hl_ready, 1)
                nc.gpsimd.tensor_tensor(hhl[:, f, LOW_S], hid[:, i, CAP_P:CAP], hhl[:, f, CAP_P:CAP].bitcast(F32), ALU.subtract).then_inc(hl_ready, 1)

            def body(e, first=False, last=False):
                for f in range(FT):
                    combine(f, e * FT)
                    if f == 1:
                        pool.wait_ge(yp_ready, e * 1 + 1)
                        pool.wait_ge(ys_ready, e * 1 + 1)
                        nc.gpsimd.tensor_copy(gt_p[:, :], K.gateT_p[:, bass.ds(e, 1)]).then_inc(gates_ready, 1)
                        nc.gpsimd.tensor_copy(gt_s[:, :], K.gateT_s[:, bass.ds(e, 1)]).then_inc(gates_ready, 1)
                    if f == 2 and not last:
                        pool.wait_ge(gathered_p, e * 16 + 16)
                        pool.wait_ge(gathered_s, e * 16 + 16)
                        pool.wait_ge(xt_done, e * 2 + 2)
                        gather(e + 1, e + 1)
                if not first:
                    pool.wait_ge(scat_p, e * 16)
                    pool.wait_ge(scat_s, e * 16)
                nc.gpsimd.tensor_copy(sx_p[:, :], K.idxT_p[:, bass.ds(e, 1)]).then_inc(sindex_ready, 1)
                nc.gpsimd.tensor_copy(sx_s[:, :], K.idxT_s[:, bass.ds(e, 1)]).then_inc(sindex_ready, 1)
                pool.wait_ge(sindex_ready, e * 2 + 2)
                pool.wait_ge(yp_ready, e * 1 + 2)
                pool.sem_inc(rows_asked, 1)
                nc.gpsimd.indirect_dma_start(K.h_p, bass.IndirectOffsetOnAxis(ap=sx_p[:, :], axis=0), y_p[:, :], None,
                                             compute_op=ALU.add).then_inc(scat_p, 16)
                pool.wait_ge(ys_ready, e * 1 + 2)
                pool.sem_inc(rows_asked, 1)
                nc.gpsimd.indirect_dma_start(K.h_s, bass.IndirectOffsetOnAxis(ap=sx_s[:, :], axis=0), y_s[:, :], None,
                                             compute_op=ALU.add).then_inc(scat_s, 16)

            gather(0, 0)
            body(0, first=True)
            with pool.Fori(1, E - 1) as e:
                body(e)
            body(E - 1, last=True)

        @block.scalar
        def _(act):
            act.sem_inc(yp_ready, 1)

            def high(e, c):
                loaded_wait(act, e, c)
                prev = c - HL
                if 0 <= prev < FT:
                    act.wait_ge(gate_done if prev % 2 == 0 else up_done, e * FT + (2 * (prev // 2) + 2))
                elif prev >= FT:
                    act.wait_ge(down_used, e * (FT // 2) + (prev - FT + 1))
                nc.scalar.copy(wh[:, c % HL, :], raw[:, c % RAW, :]).then_inc(high_ready, 1)

            def x_high(nth):
                for half in range(2):
                    act.wait_ge(xt_done, nth * 2 + (half + 1))
                    src = PS[:, 2 * half:2 * half + 2, 0:2 * CAP].rearrange("p b (k n) -> p b k n", k=2)
                    dst = xhl[:, 4 * half:4 * half + 4, 0, :].rearrange("p (b k) n -> p b k n", k=2)
                    nc.scalar.copy(dst, src).then_inc(xh_ready, 1)

            def hidden(e, f):
                i = f % 2
                act.wait_ge(gsum_ready, e * FT + (f + 3))
                if f >= 2:
                    act.wait_ge(hid_ready, e * FT + (f - 1))
                nc.scalar.activation(sg[:, i, :], gsum[:, i, :], ACT.Silu).then_inc(sg_ready, 1)
                act.wait_ge(hid_ready, e * FT + (f + 1))
                nc.scalar.copy(hhl[:, f, HIGH], hid[:, i, :]).then_inc(hh_ready, 1)

            def body(e, first=False, last=False):
                for fp in range(FT // 2):
                    for f in (2 * fp, 2 * fp + 1):
                        hidden(e, f)
                    high(e, 2 * fp + 4)
                    high(e, 2 * fp + 5)
                for c in range(FT + HL, NCH + (0 if last else HL)):
                    high(e, c)
                    if c == FT + HL + 1 and not last:
                        x_high(e + 1)
                act.wait_ge(down_used, e * (FT // 2) + FT // 2)
                act.wait_ge(gates_ready, e * 2 + 2)
                if not first:
                    act.wait_ge(scat_p, e * 16)
                nc.scalar.mul(y_p[:, :], PS[:, 4:6, :].rearrange("p b n -> p (b n)"), gt_p[:, 0:1]).then_inc(yp_ready, 1)
                act.wait_ge(ys_ready, e * 1 + 1)
                nc.scalar.mul(y_low[:, :], PS[CAP_S:P, 6:8, :].rearrange("p b n -> p (b n)"), gt_s[CAP_S:P, 0:1]).then_inc(ylow_ready, 1)

            x_high(0)
            for c in range(HL):
                high(0, c)
            body(0, first=True)
            with act.Fori(1, E - 1) as e:
                body(e)
            body(E - 1, last=True)

        @block.vector
        def _(dve):
            dve.sem_inc(split_done, RAW)
            dve.sem_inc(gsum_ready, 2)
            dve.sem_inc(usum_ready, 2)
            dve.sem_inc(ys_ready, 1)

            def low(e, c):
                dve.wait_ge(high_ready, e * NCH + (c + 1))
                nc.vector.tensor_tensor(wl[:, c % HL, :], raw[:, c % RAW, :], wh[:, c % HL, :].bitcast(F32), ALU.subtract).then_inc(split_done, 1)

            def x_low(nth):
                for half in range(2):
                    dve.wait_ge(xh_ready, nth * 2 + (half + 1))
                    src = PS[:, 2 * half:2 * half + 2, 0:2 * CAP].rearrange("p b (k n) -> p b k n", k=2)
                    at = lambda part: xhl[:, 4 * half:4 * half + 4, part, :].rearrange("p (b k) n -> p b k n", k=2)
                    nc.vector.tensor_tensor(at(1), src, at(0).bitcast(F32), ALU.subtract).then_inc(xl_ready, 1)

            def sums(e, f):
                i = f % 2
                for done, ready, dst, bank, read in ((gate_done, gsum_ready, gsum, i, sg_ready), (up_done, usum_ready, usum, 2 + i, hid_ready)):
                    dve.wait_ge(done, e * FT + (f + 1))
                    if f >= 2:
                        dve.wait_ge(read, e * FT + (f - 1))
                    nc.vector.tensor_reduce(dst[:, i, :], PS[:, bank, 0:2 * CAP].rearrange("p (a n) -> p n a", a=2), AX.X, ALU.add).then_inc(ready, 1)

            def body(e, first=False, last=False):
                for fp in range(FT // 2):
                    for f in (2 * fp, 2 * fp + 1):
                        sums(e, f)
                    low(e, 2 * fp + 4)
                    low(e, 2 * fp + 5)
                for c in range(FT + HL, NCH + (0 if last else HL)):
                    low(e, c)
                    if c == FT + HL + 1 and not last:
                        x_low(e + 1)
                dve.wait_ge(ylow_ready, e * 1 + 1)
                if not first:
                    dve.wait_ge(scat_s, e * 16)
                nc.vector.scalar_tensor_tensor(y_s[:, :], PS[0:CAP_S, 6:8, :].rearrange("p b n -> p (b n)"), gt_s[0:CAP_S, 0:1], y_low[:, :],
                                               ALU.mult, ALU.add).then_inc(ys_ready, 1)

            x_low(0)
            for c in range(HL):
                low(0, c)
            body(0, first=True)
            with dve.Fori(1, E - 1) as e:
                body(e)
            body(E - 1, last=True)

        @block.tensor
        def _(pe):
            def turn(nth):
                pe.wait_ge(gathered_p, nth * 16 + 16)
                pe.wait_ge(gathered_s, nth * 16 + 16)
                pe.wait_ge(gsum_ready, nth * FT + 2)
                pe.wait_ge(usum_ready, nth * FT + 2)
                for k in range(KD):
                    b, o = k // 2, (k % 2) * CAP
                    nc.tensor.transpose(PS[:, b, o:o + CAP_P], xe_p[:, k * P:(k + 1) * P], K.ident[:, :])
                    mm = nc.tensor.transpose(PS[:, b, o + CAP_P:o + CAP], xe_s[:, k * P:(k + 1) * P], K.ident[0:CAP_S, 0:CAP_S])
                    if k % 4 == 3:
                        mm.then_inc(xt_done, 1)

            def gate_up(e, f):
                i, sub = f % 2, f % 2
                for part, (bank, free, done) in enumerate(((i, gsum_ready, gate_done), (2 + i, usum_ready, up_done))):
                    c = (f // 2) * 2 + part
                    if sub == 0:
                        split_ready(pe, e, c)
                    pe.wait_ge(free, e * FT + (f + 1))
                    hi = wh[:, c % HL, :].rearrange("p (k f) -> p k f", k=KD)
                    lo = wl[:, c % HL, :].rearrange("p (k f) -> p k f", k=KD)
                    for k in range(KD):
                        nc.tensor.matmul(PS[:, bank, 0:2 * CAP], hi[:, k, sub * P:(sub + 1) * P], xhl[:, k, :, :].rearrange("p a n -> p (a n)"),
                                         start=(k == 0), stop=False)
                        mm = nc.tensor.matmul(PS[:, bank, 0:CAP], lo[:, k, sub * P:(sub + 1) * P], xhl[:, k, 0, :],
                                              start=False, stop=(k == KD - 1))
                    mm.then_inc(done, 1)

            def down(e, f):
                c = FT + f // 2
                if f % 2 == 0:
                    split_ready(pe, e, c)
                pe.wait_ge(hl_ready, e * (2 * FT) + 2 * (f + 1))
                if f == 0:
                    pe.wait_ge(yp_ready, e * 1 + 1)
                    pe.wait_ge(ys_ready, e * 1 + 1)
                at = (f % 2) * D
                hi = [wh[:, c % HL, at + n * CHUNK:at + (n + 1) * CHUNK] for n in range(2)]
                lo = [wl[:, c % HL, at + n * CHUNK:at + (n + 1) * CHUNK] for n in range(2)]
                ph, pl, both = hhl[:, f, 0:CAP_P], hhl[:, f, LOW_P], hhl[:, f, BOTH_S]
                first, final = f == 0, f == FT - 1
                for n in range(2):
                    nc.tensor.matmul(PS[:, 4 + n, :], ph, hi[n], start=first, stop=False)
                for n in range(2):
                    nc.tensor.matmul(PS[:, 4 + n, :], ph, lo[n], start=False, stop=False)
                for n in range(2):
                    nc.tensor.matmul(PS[:, 4 + n, :], pl, hi[n], start=False, stop=final)
                for n in range(2):
                    nc.tensor.matmul(PS[:, 6 + n, :], both, hi[n], start=first, stop=False)
                for n in range(2):
                    mm = nc.tensor.matmul(PS[:, 6 + n, :], both, lo[n], start=False, stop=final)
                return mm

            def body(e, first=False, last=False):
                pe.wait_ge(xl_ready, e * 2 + 2)
                for f in range(FT):
                    gate_up(e, f)
                for f in range(FT):
                    mm = down(e, f)
                    if f % 2 == 1:
                        mm.then_inc(down_used, 1)
                    if f == 3 and not last:
                        turn(e + 1)

            turn(0)
            body(0, first=True)
            with pe.Fori(1, E - 1) as e:
                body(e)
            body(E - 1, last=True)


def stage_embed(nc, K, io, sb, sem):
    w_pg = sb("w_pg", [P, KD, D])
    g3, bias = sb("g3", [P, D]), sb("bias", [P, D])
    h, e_in = sb("h5", [P, 3, D]), sb("e_in", [P, 2, D])
    hn = sb("hn", [P, 2, D])
    hnT = sb("hnT", [P, 2, KD, P])
    junk = sb("junk5", [P, D])
    pre, sig = sb("pre", [P, 2, D]), sb("sig", [P, 2, D])
    out = sb("out5", [P, 2, D])
    ssq, ms, rstd = sb("ssq5", [P, TILES]), sb("ms5", [P, TILES]), sb("rstd5", [P, TILES])
    loaded, w_loaded = sem("loaded5"), sem("w5_loaded")
    h_loaded = [sem(f"h5_loaded{i}") for i in range(3)]
    e_loaded = [sem(f"e5_loaded{i}") for i in range(2)]
    out_stored = [sem(f"out_stored{i}") for i in range(2)]
    ssq_ready, ms_ready, rstd_ready = sem("ssq5_ready"), sem("ms5_ready"), sem("rstd5_ready")
    hn_ready, tr_done, hnT_ready, gate_done = sem("hn_ready"), sem("tr5_done"), sem("hnT_ready"), sem("gate5_done")
    pre_ready, sig_ready, prod_ready, out_ready = sem("pre_ready"), sem("sig5_ready"), sem("prod_ready"), sem("out_ready")
    PS = K.PS

    with nc.Block() as block:

        @block.sync
        def _(sp):
            def load(t):
                if t >= 3:
                    sp.wait_ge(out_ready, t - 2)
                sp.dma_start(h[:, t % 3, :], K.h_rows(t)).then_inc(h_loaded[t % 3], 16)

            load(0)
            sp.dma_start(g3[:, :], io["ple_norm_g"].partition_broadcast(P)).then_inc(loaded, 16)
            sp.dma_start(w_pg[:, :, :], io["ple_gate_w"].rearrange("a (k p) n -> (a p) k n", p=P)).then_inc(w_loaded, 16)
            sp.dma_start(bias[:, :], io["ple_gate_b"].partition_broadcast(P)).then_inc(loaded, 16)
            load(1)
            load(2)
            for t in range(TILES):
                if t >= 2:
                    sp.wait_ge(prod_ready, t - 1)
                sp.dma_start(e_in[:, t % 2, :], K.e_rows(t)).then_inc(e_loaded[t % 2], 16)
                if t >= 3:
                    load(t)
                if t >= 1:
                    sp.wait_ge(out_ready, t)
                    sp.dma_start(io["out_rows"](t - 1), out[:, (t - 1) % 2, :]).then_inc(out_stored[(t - 1) % 2], 16)
            sp.wait_ge(out_ready, TILES)
            sp.dma_start(io["out_rows"](TILES - 1), out[:, (TILES - 1) % 2, :]).then_inc(out_stored[(TILES - 1) % 2], 16)
            for i in range(2):
                sp.wait_ge(out_stored[i], 16 * (TILES // 2))

        @block.gpsimd
        def _(pool):
            for t in range(TILES + 1):
                if t < TILES:
                    pool.wait_ge(ssq_ready, t + 1)
                    nc.gpsimd.tensor_scalar(ms[:, t:t + 1], ssq[:, t:t + 1], 1.0 / D, EPS, ALU.mult, ALU.add).then_inc(ms_ready, 1)
                    pool.wait_ge(ms_ready, t + 1)
                    nc.gpsimd.tensor_tensor(rstd[:, t:t + 1], ms[:, t:t + 1], K.minus_half[:, :], ALU.pow).then_inc(rstd_ready, 1)

        @block.scalar
        def _(act):
            def square(t):
                act.wait_ge(h_loaded[t % 3], 16 * (t // 3 + 1))
                if t:
                    act.wait_ge(ssq_ready, t)
                nc.scalar.activation(junk[:, :], h[:, t % 3, :], ACT.Square, accum_out=ssq[:, t:t + 1]).then_inc(ssq_ready, 1)

            def copy_T(t):
                act.wait_ge(tr_done, t + 1)
                if t >= 2:
                    act.wait_ge(gate_done, t - 1)
                nc.scalar.copy(hnT[:, t % 2, :, :], PS[:, 6:8, :].rearrange("p b (k n) -> p (b k) n", k=4)).then_inc(hnT_ready, 1)

            def sigmoid(t):
                act.wait_ge(pre_ready, t + 1)
                if t >= 2:
                    act.wait_ge(prod_ready, t - 1)
                nc.scalar.activation(sig[:, t % 2, :], pre[:, t % 2, :], ACT.Sigmoid).then_inc(sig_ready, 1)

            square(0)
            copy_T(0)
            for t in range(TILES):
                if t + 1 < TILES:
                    square(t + 1)
                    copy_T(t + 1)
                sigmoid(t)

        @block.vector
        def _(dve):
            def norm(t):
                dve.wait_ge(rstd_ready, t + 1)
                if t >= 2:
                    dve.wait_ge(tr_done, t - 1)
                nc.vector.scalar_tensor_tensor(hn[:, t % 2, :], h[:, t % 3, :], rstd[:, t:t + 1], g3[:, :], ALU.mult, ALU.mult).then_inc(hn_ready, 1)

            dve.wait_ge(loaded, 32)
            norm(0)
            for t in range(TILES):
                i = t % 2
                if t + 1 < TILES:
                    norm(t + 1)
                dve.wait_ge(gate_done, t + 1)
                if t >= 2:
                    dve.wait_ge(sig_ready, t - 1)
                b = 2 * (t % 2)
                nc.vector.tensor_tensor(pre[:, i, :].rearrange("p (b n) -> p b n", b=2), PS[:, b:b + 2, :],
                                        bias[:, :].rearrange("p (b n) -> p b n", b=2), ALU.add).then_inc(pre_ready, 1)
                dve.wait_ge(sig_ready, t + 1)
                dve.wait_ge(e_loaded[i], 16 * (t // 2 + 1))
                nc.vector.tensor_tensor(sig[:, i, :], sig[:, i, :], e_in[:, i, :], ALU.mult).then_inc(prod_ready, 1)
                dve.wait_ge(prod_ready, t + 1)
                if t >= 2:
                    dve.wait_ge(out_stored[i], 16 * (t // 2))
                nc.vector.tensor_tensor(out[:, i, :], sig[:, i, :], h[:, t % 3, :], ALU.add).then_inc(out_ready, 1)

        @block.tensor
        def _(pe):
            def turn(t):
                pe.wait_ge(hn_ready, t + 1)
                if t:
                    pe.wait_ge(hnT_ready, t)
                for k in range(KD):
                    mm = nc.tensor.transpose(PS[:, 6 + k // 4, (k % 4) * P:(k % 4 + 1) * P], hn[:, t % 2, k * P:(k + 1) * P], K.ident[:, :])
                mm.then_inc(tr_done, 1)

            turn(0)
            pe.wait_ge(w_loaded, 16)
            for t in range(TILES):
                if t + 1 < TILES:
                    turn(t + 1)
                pe.wait_ge(hnT_ready, t + 1)
                if t >= 2:
                    pe.wait_ge(pre_ready, t - 1)
                for k in range(KD):
                    for half in range(2):
                        mm = nc.tensor.matmul(PS[:, 2 * (t % 2) + half, :], hnT[:, t % 2, k, :], w_pg[:, k, half * CHUNK:(half + 1) * CHUNK],
                                              start=(k == 0), stop=(k == KD - 1))
                mm.then_inc(gate_done, 1)


def encoder_layer_kernel(nc, io, stages=5):
    K = Kept()

    def rows(prompt, sample):
        return lambda t: prompt[t * P:(t + 1) * P, :] if t < PTILES else sample[(t - PTILES) * P:(t - PTILES + 1) * P, :]

    io["x_rows"] = rows(io["x_prompt"][0], io["x_sample"][0])
    io["p_rows"] = rows(io["p_prompt"][0, 0], io["p_sample"][0, 0])
    io["out_rows"] = rows(io["y_prompt"][0], io["y_sample"][0])
    def scratch(name):
        return [nc.dram_tensor(f"{name}_rows_{g}", (t, D), F32, kind="Internal").ap() for g, t in (("p", T_PROMPT), ("s", T_SAMPLE))]

    K.h_p, K.h_s = scratch("h")
    K.xn_p, K.xn_s = scratch("xn")
    K.h_rows, K.xn_rows, K.e_rows = rows(K.h_p, K.h_s), rows(K.xn_p, K.xn_s), rows(*scratch("e"))

    with ExitStack() as whole:
        def alloc(stack):
            return lambda name, shape, dt=F32: stack.enter_context(nc.sbuf_tensor(name, shape, dt))

        def sem(name):
            return whole.enter_context(nc.semaphore(name))

        keep = alloc(whole)
        K.PS = whole.enter_context(nc.psum_tensor("PS", [P, 8, CHUNK], F32))
        K.ident, K.eps, K.minus_half = keep("ident", [P, P]), keep("eps", [P, 1]), keep("minus_half", [P, 1])
        K.idxT_p, K.idxT_s = keep("idxT_p", [P, E], U32), keep("idxT_s", [CAP_S, E], U32)
        K.gateT_p, K.gateT_s = keep("gateT_p", [P, E]), keep("gateT_s", [P, E])
        K.glu_cleared, K.v_cleared = sem("glu_cleared"), sem("v_cleared")
        with ExitStack() as mixers:
            part = alloc(mixers)
            K.qT, K.kT = part("qT", [P, QT, T_ALL]), part("kT", [P, KV, T_ALL])
            K.v_aug = part("v_aug", [P, TILES, KV, P])
            K.conv_w = part("conv_w", [P, CT * (TAPS + 1)])
            K.head_ones, K.rot, K.chan_mean = part("head_ones", [P, P]), part("rot", [P, P]), part("chan_mean", [P, P])
            K.conv = part("conv", [P, CT, T_ALL])
            with ExitStack() as convs:
                K.glu = alloc(convs)("glu", [P, CT, GLU_COLS])
                with ExitStack() as s:
                    stage_project(nc, K, io, alloc(s), sem)
                if stages >= 2:
                    with ExitStack() as s:
                        stage_attend(nc, K, io, alloc(s), sem)
            if stages >= 3:
                with ExitStack() as s:
                    stage_mix_route(nc, K, io, alloc(s), sem)
        if stages >= 4:
            with ExitStack() as s:
                stage_experts(nc, K, io, alloc(s), sem)
        if stages >= 5:
            with ExitStack() as s:
                stage_embed(nc, K, io, alloc(s), sem)


def shape_constants():
    import numpy as np
    f = np.float32
    half = HD // 4
    freqs = (f(1.0) / (f(10000.0) ** (np.arange(0, HD // 2, 2, dtype=f) / f(HD // 2)))).astype(f)
    t = np.arange(T_PROMPT)
    ang = np.zeros((HD, T_PROMPT), f)
    for d in range(HD):
        pos = (t // 64 if d < HD // 2 else t % 64).astype(f)
        ang[d] = pos * freqs[d % half]
    two = lambda a: np.ascontiguousarray(np.concatenate([a, a], 0).astype(f))
    rot = np.zeros((P, P), f)
    for base in range(0, P, HD // 2):
        for i in range(half):
            rot[base + half + i, base + i] = -1.0
            rot[base + i, base + half + i] = 1.0
    head_ones = np.kron(np.eye(P // HD), np.full((HD, HD), 1.0 / HD)).astype(f)
    return dict(cos=two(np.cos(ang)), sin=two(np.sin(ang)), rot=rot, head_ones=head_ones, ident=np.eye(P, dtype=f),
                chan_mean=np.full((P, P), 1.0 / D_CONV, f), eps_col=np.full((P, 1), EPS, f))


def layouts(inputs):
    import numpy as np
    a = {n: np.ascontiguousarray(v) for n, v in inputs.items()}
    col = lambda v, k: np.ascontiguousarray(v.reshape(k, P).T)
    a["norm1_g"] = col(a["norm1_g"], KD)
    a["qk_gain"] = np.ascontiguousarray(np.stack([np.tile(a.pop("q_norm_g")[0], 2), np.tile(a.pop("k_norm_g")[0], 2)], 1))
    taps = np.concatenate([a.pop("conv_dw_w")[0], a.pop("conv_dw_b")], 0)
    a["conv_w"] = np.ascontiguousarray(taps.reshape(TAPS + 1, CT, P).transpose(2, 1, 0).reshape(P, CT * (TAPS + 1)))
    a["chan_gain"] = np.ascontiguousarray(np.concatenate([col(a.pop(n), CT) for n in ("conv_ln_g", "conv_ln_b", "conv_out_g", "attn_out_g")], 1))
    for n in ("norm2_g", "ple_norm_g", "ple_gate_b"):
        a[n] = a[n].reshape(D)
    return a | shape_constants()


def kernel(**inputs):
    import concourse.bacc as _bacc
    from concourse.bass_utils import run_bass_kernel_spmd as _run

    arrays = layouts(inputs)
    nc = _bacc.Bacc("TRN2", target_bir_lowering=False, num_devices=1)
    io = {name: nc.dram_tensor(f"in_{name}", a.shape, mybir.dt.from_np(a.dtype), kind="ExternalInput").ap()
          for name, a in arrays.items()}
    for name, t in (("y_prompt", T_PROMPT), ("y_sample", T_SAMPLE)):
        io[name] = nc.dram_tensor(f"out_{name}", (1, t, D), F32, kind="ExternalOutput").ap()
    encoder_layer_kernel(nc, io)
    r = _run(nc, [{f"in_{n}": a for n, a in arrays.items()}], core_ids=[0])
    return r.results[0]["out_y_prompt"], r.results[0]["out_y_sample"]
```

```python
from contextlib import ExitStack
from typing import NamedTuple

import concourse.bass as bass
from concourse import mybir

F32 = mybir.dt.float32
F32R = mybir.dt.float32r
U32 = mybir.dt.uint32
ALU = mybir.AluOpType
ACT = mybir.ActivationFunctionType
AX = mybir.AxisListType

P = 128
D = 1024
KD = D // P
T_PROMPT, T_SAMPLE = 1024, 512
T_ALL = T_PROMPT + T_SAMPLE
TILES = T_ALL // P
PTILES = T_PROMPT // P
CHUNK = 512
CHUNKS = T_ALL // CHUNK
D_CONV = 512
CT = D_CONV // P
TAPS = 31
PAD = TAPS // 2
HEADS, KV, HD = 8, 2, 64
D_Q = HEADS * HD
QT = D_Q // P
KV_GROUP = HEADS // KV
SCALE = HD ** -0.5
EPS = 1e-6
E = 16
CAP_P, CAP_S = 2 * T_PROMPT // E, 2 * T_SAMPLE // E
CAP = CAP_P + CAP_S
F_EXP = 2048
FT = F_EXP // P
D_PLE = 256
SEG = (0, T_PROMPT + 2 * PAD)
GLU_COLS = T_ALL + 4 * PAD
CHUNK_TILES = CHUNK // P
CONV_STEPS = CT * TAPS * 2
LN_EXP = "natural_log_exp_and_others"


def chunk_pos(c):
    return (0, c * CHUNK) if c * CHUNK < T_PROMPT else (1, c * CHUNK - T_PROMPT)


class Step(NamedTuple):
    u: int
    j: int
    h4: int
    q0: int
    tok0: int
    nt: int
    banks: int


class Kept:
    pass


class Chain:

    def __init__(self, eng, sem):
        self.eng, self.sem, self.n = eng, sem, 0

    def did(self, ins):
        ins.then_inc(self.sem, 1)
        self.n += 1
        return self.n

    def wait(self, n):
        self.eng.wait_ge(self.sem, n)


def conv_tap(nc, K, dve, k):
    ct, r = divmod(k, 2 * TAPS)
    tap, g = divmod(r, 2)
    n = T_PROMPT if g == 0 else T_SAMPLE
    src = K.glu[:, ct, SEG[g] + tap:SEG[g] + tap + n]
    acc = K.conv[:, ct, g * T_PROMPT:g * T_PROMPT + n]
    w = K.conv_w[:, ct * (TAPS + 1) + tap:ct * (TAPS + 1) + tap + 1]
    if tap == 0:
        b = K.conv_w[:, ct * (TAPS + 1) + TAPS:(ct + 1) * (TAPS + 1)]
        nc.vector.tensor_scalar(acc, src, w, b, ALU.mult, ALU.add).then_inc(K.taps_ready, 1)
    else:
        dve.wait_ge(K.taps_ready, k - 1)
        nc.vector.scalar_tensor_tensor(acc, src, w, acc, ALU.mult, ALU.add).then_inc(K.taps_ready, 1)


def stage_project(nc, K, io, sb, sem):
    flat = K.conv[:, :, :].rearrange("p c t -> p (c t)")
    x_ring = flat[:, 0:3 * D].rearrange("p (r d) -> p r d", r=3)
    gate_sig = flat[:, 3 * D:3 * D + 2 * T_ALL].rearrange("p (r c n) -> p r c n", r=2, c=CHUNKS)
    W_SLOTS = 3
    aT = sb("aT", [P, KD, T_ALL])
    w_ring = sb("w_ring", [P, W_SLOTS, KD, P])
    square = sb("square", [P, 2, CHUNK])
    inv = sb("inv", [P, 2, CHUNK])
    qn = sb("qn", [P, 2, CHUNK])
    by_cos = sb("by_cos", [P, 2, CHUNK])
    by_sin = sb("by_sin", [P, 2, CHUNK])
    cos = sb("cos", [P, T_PROMPT])
    sin = sb("sin", [P, T_PROMPT])
    junk = square[:, :, :].rearrange("p r n -> p (r n)")
    g1 = sb("g1", [P, KD])
    qkg, one = sb("qkg", [P, 2]), sb("one", [P, 1])
    ssq = sb("ssq", [P, TILES])
    ms = sb("ms", [P, TILES])
    rstd = sb("rstd", [P, TILES])

    consts_loaded = sem("consts_loaded")
    x_loaded = [sem(f"x_loaded{i}") for i in range(3)]
    w_loaded = [sem(f"w_loaded{i}") for i in range(W_SLOTS)]
    ssq_ready, ms_ready, rstd_ready = sem("ssq_ready"), sem("ms_ready"), sem("rstd_ready")
    xn_ready, tr_done, aT_ready = sem("xn_ready"), sem("tr_done"), sem("aT_ready")
    z_done, sig_ready, glu_done = sem("z_done"), sem("sig_ready"), sem("glu_done")
    sq_ready, ms_done, ln_ready, inv_ready, qn_ready = (sem(n) for n in ("sq_ready", "ms_done", "ln1_ready", "inv1_ready", "qn_ready"))
    rot_done, sin_ready = sem("rot_done"), sem("sin_ready")
    vh_ready, v_ready, one_ready = sem("vh_ready"), sem("v_ready"), sem("one_ready")
    sum_ready, kh_ready = sem("sum_ready"), sem("kh_ready")
    dve_own, half_ready = sem("dve_own1"), sem("half_ready")

    PS = K.PS
    CONSTS = 10
    SL = [s for i in range(CT) for s in (("gate", i), ("val", i))]
    SL += [("k", j) for j in range(KV)] + [("q", i) for i in range(QT)] + [("v", 0)]
    NW = len(SL)
    NQK0 = 2 * CT * CHUNKS
    NK = KV * CHUNKS
    NQK = (KV + QT) * CHUNKS
    NV0 = NQK0 + NQK
    w_in = io["w_in"].rearrange("a (k p) n -> (a p) k n", p=P)
    col0 = {"val": 0, "gate": D_CONV, "q": 2 * D_CONV, "k": 2 * D_CONV + D_Q, "v": 2 * D_CONV + D_Q + KV * HD}

    def consumer(n):
        if n < NQK0:
            i, c = divmod(n, CHUNKS)
            return (sig_ready if i % 2 == 0 else glu_done), (i // 2) * CHUNKS + c + 1
        if n < NV0:
            return qn_ready, n - NQK0 + 1
        return v_ready, n - NV0 + 1

    def keys(ap, m):
        j, c = divmod(m, CHUNKS)
        return ap[:, j, c * CHUNK:(c + 1) * CHUNK]

    def v_product(t):
        return PS[:, 4 + (NV0 + t) % 4, 0:P].rearrange("p (j d) -> p j d", j=KV)

    with nc.Block() as block:

        @block.sync
        def _(sp):
            def load_x(t):
                if t >= 3:
                    sp.wait_ge(tr_done, t - 2)
                sp.dma_start(x_ring[:, t % 3, :], io["x_rows"](t)).then_inc(x_loaded[t % 3], 16)

            def load_w(i):
                if i >= W_SLOTS:
                    sp.wait_ge(z_done, CHUNKS * (i - W_SLOTS + 1))
                kind, n = SL[i]
                if kind == "k":
                    for d in range(2):
                        sp.dma_start(w_ring[:, i % W_SLOTS, :, d * HD:(d + 1) * HD],
                                     w_in[:, :, col0["k"] + n * HD:col0["k"] + (n + 1) * HD]).then_inc(w_loaded[i % W_SLOTS], 16)
                else:
                    c = col0[kind] + n * P
                    sp.dma_start(w_ring[:, i % W_SLOTS], w_in[:, :, c:c + P]).then_inc(w_loaded[i % W_SLOTS], 16)

            load_x(0)
            for dst, src in ((K.ident, io["ident"]), (g1, io["norm1_g"])):
                sp.dma_start(dst[:, :], src).then_inc(consts_loaded, 16)
            load_x(1)
            load_x(2)
            for dst, src in ((K.eps, io["eps_col"]), (K.head_ones, io["head_ones"]), (K.rot, io["rot"]),
                             (qkg, io["qk_gain"]), (cos, io["cos"]), (sin, io["sin"]), (K.conv_w, io["conv_w"]), (K.chan_mean, io["chan_mean"])):
                sp.dma_start(dst[:, :], src).then_inc(consts_loaded, 16)
            for i in range(W_SLOTS):
                load_w(i)
            for t in range(3, TILES):
                load_x(t)
            for i in range(W_SLOTS, NW):
                load_w(i)

        @block.gpsimd
        def _(pool):
            nc.gpsimd.memset(K.glu[:, :, :], 0.0).then_inc(K.glu_cleared, 1)
            nc.gpsimd.memset(one[:, :], 1.0).then_inc(one_ready, 1)
            nc.gpsimd.memset(K.minus_half[:, :], -0.5).then_inc(half_ready, 1)
            pool.wait_ge(half_ready, 1)
            for t in range(TILES):
                pool.wait_ge(ssq_ready, t + 1)
                nc.gpsimd.tensor_scalar(ms[:, t:t + 1], ssq[:, t:t + 1], 1.0 / D, EPS, ALU.mult, ALU.add).then_inc(ms_ready, 1)
                pool.wait_ge(ms_ready, t + 1)
                nc.gpsimd.tensor_tensor(rstd[:, t:t + 1], ms[:, t:t + 1], K.minus_half[:, :], ALU.pow).then_inc(rstd_ready, 1)

        @block.scalar
        def _(act):
            for t in range(TILES):
                act.wait_ge(x_loaded[t % 3], 16 * (t // 3 + 1))
                if t:
                    act.wait_ge(ssq_ready, t)
                nc.scalar.activation(junk, x_ring[:, t % 3, :], ACT.Square, accum_out=ssq[:, t:t + 1]).then_inc(ssq_ready, 1)
            act.wait_ge(consts_loaded, 16 * CONSTS)
            for p in range(CT):
                for c in range(CHUNKS):
                    act.wait_ge(z_done, 2 * p * CHUNKS + c + 1)
                    if p >= 2:
                        act.wait_ge(glu_done, (p - 2) * CHUNKS + c + 1)
                    nc.scalar.activation(gate_sig[:, p % 2, c, :], PS[:, 4 + (2 * p * CHUNKS + c) % 4, :], ACT.Sigmoid).then_inc(sig_ready, 1)

            nc.scalar.preload_act_table_set(LN_EXP)

            def inverse_root(m):
                act.wait_ge(ms_done, m + 1)
                if m >= 2:
                    act.wait_ge(qn_ready, m - 1)
                nc.scalar.activation(inv[:, m % 2, :], PS[:, m % 2, :], ACT.Ln, bias=K.eps[:, :]).then_inc(ln_ready, 1)
                act.wait_ge(ln_ready, m + 1)
                nc.scalar.activation(inv[:, m % 2, :], inv[:, m % 2, :], ACT.Exp, scale=-0.5).then_inc(inv_ready, 1)

            for m in range(NQK):
                act.wait_ge(z_done, NQK0 + m + 1)
                if m >= 2:
                    act.wait_ge(ms_done, m - 1)
                nc.scalar.activation(square[:, m % 2, :], PS[:, 4 + (NQK0 + m) % 4, :], ACT.Square).then_inc(sq_ready, 1)
                if m >= 1:
                    inverse_root(m - 1)
                if 0 <= m - 2 < NK:
                    act.wait_ge(sum_ready, m - 1)
                    nc.scalar.copy(keys(K.k_high, m - 2), by_cos[:, m % 2, :]).then_inc(kh_ready, 1)
            inverse_root(NQK - 1)
            for t in range(TILES):
                act.wait_ge(z_done, NV0 + t + 1)
                nc.scalar.copy(K.v_high[:, t, :, 0:HD], v_product(t)).then_inc(vh_ready, 1)

        @block.vector
        def _(dve):
            own = Chain(dve, dve_own)
            taps = [0]

            def conv_taps(n):
                for k in range(taps[0], taps[0] + n):
                    if k % (2 * TAPS) == 0:
                        ct = k // (2 * TAPS)
                        dve.wait_ge(glu_done, CHUNKS * (CT if ct >= 2 else ct + 1))
                    conv_tap(nc, K, dve, k)
                taps[0] += n

            def to_aT(t):
                dve.wait_ge(tr_done, t + 1)
                b = 2 * (t % 2)
                nc.vector.tensor_tensor(aT[:, :, t * P:(t + 1) * P],
                                        PS[:, b:b + 2, :].rearrange("p b (k n) -> p (b k) n", k=4),
                                        g1[:, :].unsqueeze(2).broadcast_to((P, KD, P)), ALU.mult).then_inc(aT_ready, 1)

            dve.wait_ge(consts_loaded, 16 * CONSTS)
            for t in range(TILES):
                dve.wait_ge(rstd_ready, t + 1)
                nc.vector.tensor_scalar(x_ring[:, t % 3, :], x_ring[:, t % 3, :], rstd[:, t:t + 1], None, ALU.mult).then_inc(xn_ready, 1)
                if t:
                    to_aT(t - 1)
            to_aT(TILES - 1)
            dve.wait_ge(one_ready, 1)
            nc.vector.tensor_copy(K.v_high[:, :, :, HD:P].rearrange("p t j n -> p (t j) n"),
                                  one[:, :].unsqueeze(2).broadcast_to((P, TILES * KV, HD)))
            dve.wait_ge(K.glu_cleared, 1)
            for p in range(CT):
                for c in range(CHUNKS):
                    n = (2 * p + 1) * CHUNKS + c
                    dve.wait_ge(z_done, n + 1)
                    dve.wait_ge(sig_ready, p * CHUNKS + c + 1)
                    g, t0 = chunk_pos(c)
                    o = SEG[g] + PAD + t0
                    nc.vector.tensor_tensor(K.glu[:, p, o:o + CHUNK], PS[:, 4 + n % 4, :], gate_sig[:, p % 2, c, :], ALU.mult).then_inc(glu_done, 1)
                    if p or c == CHUNKS - 1:
                        conv_taps(18 if c == CHUNKS - 1 else 5)
            for m in range(NQK):
                s, c = divmod(m, CHUNKS)
                i = m % 2
                kind, idx = SL[2 * CT + s]
                t0 = chunk_pos(c)[1]
                dve.wait_ge(inv_ready, m + 1)
                if m >= 2:
                    dve.wait_ge(rot_done, m - 1)
                gain = qkg[:, 0:1] if kind == "q" else qkg[:, 1:2]
                nc.vector.scalar_tensor_tensor(qn[:, i, :], PS[:, 4 + (NQK0 + m) % 4, :], gain, inv[:, i, :], ALU.mult, ALU.mult).then_inc(qn_ready, 1)
                dve.wait_ge(qn_ready, m + 1)
                own.did(nc.vector.tensor_tensor(by_cos[:, i, :], qn[:, i, :], cos[:, t0:t0 + CHUNK], ALU.mult))
                dve.wait_ge(rot_done, m + 1)
                nc.vector.tensor_tensor(by_sin[:, i, :], PS[:, 2 + i, :], sin[:, t0:t0 + CHUNK], ALU.mult).then_inc(sin_ready, 1)
                own.wait(own.n)
                dve.wait_ge(sin_ready, m + 1)
                if kind == "q":
                    nc.vector.tensor_tensor(K.qT[:, idx, c * CHUNK:(c + 1) * CHUNK], by_cos[:, i, :], by_sin[:, i, :], ALU.add)
                else:
                    nc.vector.tensor_tensor(by_cos[:, i, :], by_cos[:, i, :], by_sin[:, i, :], ALU.add).then_inc(sum_ready, 1)
                if 1 <= m <= NK:
                    dve.wait_ge(kh_ready, m)
                    nc.vector.tensor_tensor(keys(K.k_low, m - 1), by_cos[:, 1 - i, :], keys(K.k_high, m - 1).bitcast(F32), ALU.subtract)
                conv_taps(4)
            for t in range(TILES):
                dve.wait_ge(vh_ready, t + 1)
                nc.vector.tensor_tensor(K.v_low[:, t, :, :], v_product(t), K.v_high[:, t, :, 0:HD].bitcast(F32), ALU.subtract).then_inc(v_ready, 1)
                conv_taps(1)
            K.taps_done = taps[0]

        @block.tensor
        def _(pe):
            pe.wait_ge(consts_loaded, 16 * CONSTS)
            for t in range(TILES):
                pe.wait_ge(xn_ready, t + 1)
                if t >= 2:
                    pe.wait_ge(aT_ready, t - 1)
                for k in range(KD):
                    b = 2 * (t % 2) + k // 4
                    mm = nc.tensor.transpose(PS[:, b, (k % 4) * P:(k % 4 + 1) * P], x_ring[:, t % 3, k * P:(k + 1) * P], K.ident[:, :])
                mm.then_inc(tr_done, 1)

            def bank_free(n):
                if n >= 4:
                    pe.wait_ge(*consumer(n - 4))

            def mean_square(m):
                pe.wait_ge(sq_ready, m + 1)
                if m >= 2:
                    pe.wait_ge(ln_ready, m - 1)
                nc.tensor.matmul(PS[:, m % 2, :], K.head_ones[:, :], square[:, m % 2, :], start=True, stop=True).then_inc(ms_done, 1)

            def rotate(m):
                pe.wait_ge(qn_ready, m + 1)
                if m >= 2:
                    pe.wait_ge(sin_ready, m - 1)
                nc.tensor.matmul(PS[:, 2 + m % 2, :], K.rot[:, :], qn[:, m % 2, :], start=True, stop=True).then_inc(rot_done, 1)

            loads = [0] * W_SLOTS
            for i, (kind, _idx) in enumerate(SL):
                loads[i % W_SLOTS] += 32 if kind == "k" else 16
                pe.wait_ge(w_loaded[i % W_SLOTS], loads[i % W_SLOTS])
                if kind == "v":
                    break
                for c in range(CHUNKS):
                    n = i * CHUNKS + c
                    if i == 0:
                        pe.wait_ge(aT_ready, min(TILES, (c + 1) * CHUNK_TILES))
                        if c == 0:
                            pe.wait_ge(aT_ready, CHUNK_TILES)
                    bank_free(n)
                    for k in range(KD):
                        mm = nc.tensor.matmul(PS[:, 4 + n % 4, :], w_ring[:, i % W_SLOTS, k, :], aT[:, k, c * CHUNK:(c + 1) * CHUNK],
                                              start=(k == 0), stop=(k == KD - 1))
                    mm.then_inc(z_done, 1)
                    m = n - NQK0
                    if m == 0:
                        pe.wait_ge(aT_ready, TILES)
                    if m >= 1:
                        mean_square(m - 1)
                    if m >= 2:
                        rotate(m - 2)
            mean_square(NQK - 1)
            rotate(NQK - 2)
            for t in range(TILES):
                bank_free(NV0 + t)
                for k in range(KD):
                    mm = nc.tensor.matmul(PS[:, 4 + (NV0 + t) % 4, 0:P], aT[:, k, t * P:(t + 1) * P], w_ring[:, (NW - 1) % W_SLOTS, k, :],
                                          start=(k == 0), stop=(k == KD - 1))
                mm.then_inc(z_done, 1)
                if t == 0:
                    rotate(NQK - 1)


def stage_attend(nc, K, io, sb, sem):
    units = [(g, i, j) for g, n in ((0, PTILES), (1, TILES - PTILES)) for i in range(n) for j in range(KV)]
    STEPS = len(units) * KV_GROUP
    q_parts = sb("q_parts", [P, 2, KV_GROUP, P], F32R)
    prob = sb("prob", [P, 2, T_PROMPT])
    ph, pl = (sb(n, [P, 2, PTILES, KV_GROUP, P], F32R) for n in ("probT_high", "probT_low"))
    nmax = sb("nmax", [P, STEPS])
    inv_sum = sb("inv_sum", [HD, 2, KV_GROUP * P])
    qh_ready, ql_ready = sem("qh_ready"), sem("ql_ready")
    qk_done, nmax_ready, exp_done, tr_done = sem("qk_done"), sem("nmax_ready"), sem("exp_done"), sem("pt_done")
    ph_ready, pl_ready, pv_done = sem("ph_ready"), sem("pl_ready"), sem("pv_done")
    ln_ready, inv_ready, o_ready = sem("ln_sum_ready"), sem("inv_sum_ready"), sem("o_ready")
    PS = K.PS

    def step(n):
        g, i, j = units[n // KV_GROUP]
        tok0, ntile = (0, PTILES) if g == 0 else (T_PROMPT, TILES - PTILES)
        return Step(u=n // KV_GROUP, j=j, h4=n % KV_GROUP, q0=tok0 + i * P, tok0=tok0, nt=ntile, banks=ntile // 4)

    def scores(n):
        return PS[:, 2 * (n % 2):2 * (n % 2) + step(n).banks, :].rearrange("p b n -> p (b n)")

    def blocks(n):
        return sum(step(m).banks for m in range(n))

    def q_of(u, odd):
        s = step(u * KV_GROUP)
        return K.qT[odd * HD:(odd + 1) * HD, 2 * s.j:2 * s.j + 2, s.q0:s.q0 + P]

    def parts_of(u, odd, on):
        return q_parts[on * HD:(on + 1) * HD, u % 2, :, :].rearrange("p (a b) n -> p a b n", b=2)[:, :, odd, :]

    with nc.Block() as block:

        @block.tensor
        def _(pe):
            def score(n):
                s = step(n)
                if s.h4 == 0:
                    pe.wait_ge(ql_ready, 2 * (s.u + 1))
                for b in range(s.banks):
                    at = slice(s.tok0 + b * CHUNK, s.tok0 + (b + 1) * CHUNK)
                    nc.tensor.matmul(PS[:, 2 * (n % 2) + b, :], q_parts[:, s.u % 2, s.h4, :], K.k_high[:, s.j, at], start=True, stop=False)
                    mm = nc.tensor.matmul(PS[:, 2 * (n % 2) + b, :], q_parts[:, s.u % 2, s.h4, :], K.k_low[:, s.j, at],
                                          start=False, stop=True)
                mm.then_inc(qk_done, 1)

            def values(u, quarter):
                s = step(u * KV_GROUP)
                per = s.nt // 4
                if quarter == 0:
                    pe.wait_ge(pl_ready, blocks(KV_GROUP * (u + 1)))
                    if u >= 2:
                        pe.wait_ge(o_ready, 2 * (u - 1))
                for st in range(quarter * per, (quarter + 1) * per):
                    t = s.tok0 // P + st
                    nc.tensor.matmul(PS[:, 6 + u % 2, :], K.v_high[:, t, s.j, :], ph[:, u % 2, st, :, :], start=(st == 0), stop=False)
                    nc.tensor.matmul(PS[0:HD, 6 + u % 2, :], K.v_low[:, t, s.j, :], ph[:, u % 2, st, :, :], start=False, stop=False)
                    mm = nc.tensor.matmul(PS[:, 6 + u % 2, :], K.v_high[:, t, s.j, :], pl[:, u % 2, st, :, :],
                                          start=False, stop=(st == s.nt - 1))
                if quarter == 3:
                    mm.then_inc(pv_done, 1)

            score(0)
            score(1)
            for n in range(STEPS):
                s = step(n)
                pe.wait_ge(exp_done, n + 1)
                for b in range(s.banks):
                    x = blocks(n) + b
                    if x >= 2:
                        pe.wait_ge(pl_ready, x - 1)
                    for st in range(4):
                        mm = nc.tensor.transpose(PS[:, 4 + x % 2, st * P:(st + 1) * P], prob[:, n % 2, (4 * b + st) * P:(4 * b + st + 1) * P], K.ident[:, :])
                    mm.then_inc(tr_done, 1)
                if n + 2 < STEPS:
                    score(n + 2)
                if s.u >= 1:
                    values(s.u - 1, s.h4)
            for q in range(4):
                values(len(units) - 1, q)

        @block.scalar
        def _(act):
            def high_queries(u):
                if u >= 2:
                    act.wait_ge(qk_done, KV_GROUP * (u - 1))
                for odd in range(2):
                    nc.scalar.mul(parts_of(u, odd, odd), q_of(u, odd), SCALE).then_inc(qh_ready, 1)

            def copy_out(n):
                s = step(n)
                for b in range(s.banks):
                    x = blocks(n) + b
                    act.wait_ge(tr_done, x + 1)
                    if s.u >= 2:
                        act.wait_ge(pv_done, s.u - 1)
                    nc.scalar.copy(ph[:, s.u % 2, 4 * b:4 * (b + 1), s.h4, :],
                                   PS[:, 4 + x % 2, :].rearrange("p (k n) -> p k n", k=4)).then_inc(ph_ready, 1)

            def invert_sums(u):
                act.wait_ge(pv_done, u + 1)
                if u >= 2:
                    act.wait_ge(o_ready, 2 * (u - 1))
                nc.scalar.activation(inv_sum[:, u % 2, :], PS[HD:P, 6 + u % 2, :], ACT.Ln).then_inc(ln_ready, 1)
                act.wait_ge(ln_ready, u + 1)
                nc.scalar.activation(inv_sum[:, u % 2, :], inv_sum[:, u % 2, :], ACT.Exp, scale=-1.0).then_inc(inv_ready, 1)

            high_queries(0)
            for n in range(STEPS):
                s = step(n)
                act.wait_ge(nmax_ready, n + 1)
                if n >= 2:
                    act.wait_ge(tr_done, blocks(n - 1))
                nc.scalar.activation(prob[:, n % 2, 0:s.nt * P], scores(n), ACT.Exp, bias=nmax[:, n:n + 1]).then_inc(exp_done, 1)
                if n >= 1:
                    copy_out(n - 1)
                if s.h4 == 0 and s.u + 1 < len(units):
                    high_queries(s.u + 1)
                if s.h4 == 1 and s.u >= 2:
                    invert_sums(s.u - 2)
            copy_out(STEPS - 1)
            invert_sums(len(units) - 2)
            invert_sums(len(units) - 1)

        @block.vector
        def _(dve):
            def low_queries(u):
                for odd in range(2):
                    dve.wait_ge(qh_ready, 2 * u + odd + 1)
                    nc.vector.scalar_tensor_tensor(parts_of(u, odd, 1 - odd), q_of(u, odd), SCALE, parts_of(u, odd, odd).bitcast(F32),
                                                   ALU.mult, ALU.subtract).then_inc(ql_ready, 1)

            def negated_max(n):
                dve.wait_ge(qk_done, n + 1)
                nc.vector.tensor_reduce(nmax[:, n:n + 1], scores(n), AX.X, ALU.max, negate=True).then_inc(nmax_ready, 1)

            def low_probs(n):
                s = step(n)
                for b in range(s.banks):
                    x = blocks(n) + b
                    dve.wait_ge(ph_ready, x + 1)
                    at = lambda buf: buf[:, s.u % 2, 4 * b:4 * (b + 1), s.h4, :]
                    nc.vector.tensor_tensor(at(pl), PS[:, 4 + x % 2, :].rearrange("p (k n) -> p k n", k=4), at(ph).bitcast(F32), ALU.subtract).then_inc(pl_ready, 1)

            def normalise(u):
                dve.wait_ge(inv_ready, u + 1)
                for odd in range(2):
                    pick = lambda ap: ap.rearrange("p (a b n) -> p a b n", b=2, n=P)[:, :, odd, :]
                    nc.vector.tensor_tensor(q_of(u, odd), pick(PS[0:HD, 6 + u % 2, :]), pick(inv_sum[:, u % 2, :]), ALU.mult).then_inc(o_ready, 1)

            low_queries(0)
            negated_max(0)
            done = K.taps_done
            for n in range(STEPS):
                s = step(n)
                if n >= 1:
                    low_probs(n - 1)
                if n + 1 < STEPS:
                    negated_max(n + 1)
                if s.h4 == 0 and s.u + 1 < len(units):
                    low_queries(s.u + 1)
                if s.h4 == 2 and s.u >= 2:
                    normalise(s.u - 2)
                upto = K.taps_done + (CONV_STEPS - K.taps_done) * (n + 1) // STEPS
                for k in range(done, upto):
                    conv_tap(nc, K, dve, k)
                done = upto
            low_probs(STEPS - 1)
            normalise(len(units) - 2)
            normalise(len(units) - 1)


def stage_mix_route(nc, K, io, sb, sem):
    w_out = sb("w_out", [P, KD, D])
    sq = sb("sq", [P, CT, CHUNK])
    root = sb("root3", [P, CHUNK])
    inv = sb("inv3", [P, CHUNK])
    g2 = sb("g2", [P, D])
    w_r = sb("w_r", [P, KD, E])
    cg = sb("cg", [P, 4 * CT])
    h = sb("h", [P, 3, D])
    xn = sb("xn", [P, 3, D])
    junk = sb("junk3", [P, D])
    xnT = sb("xnT", [P, KD, P])
    ssq, ms, rstd = sb("ssq3", [P, TILES]), sb("ms3", [P, TILES]), sb("rstd3", [P, TILES])
    rt = sb("rt", [P, 2, 4])
    ex = sb("ex", [P, 2, E])
    aff = sb("aff", [P, 2, E])
    affP, affS = sb("affP", [E, T_PROMPT]), sb("affS", [E, T_SAMPLE])
    valP, valS = sb("valP", [E, CAP_P]), sb("valS", [E, 2, CAP_S])
    idxP, idxS = sb("idxP", [E, CAP_P], U32), sb("idxS", [E, CAP_S], U32)
    idxPf, idxSf = sb("idxPf", [E, CAP_P]), sb("idxSf", [E, CAP_S])
    pT = sb("pT", [P, 2, 2, P])
    p_sb = sb("p_sb", [P, 2, D_PLE])
    w_pp = sb("w_pp", [P, 2, D])
    e_sb = sb("e_sb", [P, 2, D])

    loaded = sem("loaded3")
    wout_loaded = sem("wout_loaded")
    x_loaded = [sem(f"x3_loaded{i}") for i in range(3)]
    stat_ready, stat_done = sem("stat_ready"), sem("stat_done")
    centred, root_ready, mix_ready = sem("centred"), sem("root3_ready"), sem("mix_ready")
    silu_ready, inv_ready = sem("silu_ready"), sem("inv_ready")
    out_done, h_ready, ssq_ready, ms_ready, rstd_ready = (sem(f"{n}3") for n in ("out_done", "h_ready", "ssq", "ms", "rstd"))
    xn_ready, tr_done, xnT_ready, logit_done, exp_ready = (sem(f"{n}3") for n in ("xn_ready", "tr_done", "xnT_ready", "logit_done", "exp_ready"))
    aff_ready, affT_done, affT_ready = sem("aff_ready"), sem("affT_done"), sem("affT_ready")
    h_stored = [sem(f"h_stored{i}") for i in range(3)]
    xn_stored = [sem(f"xn_stored{i}") for i in range(3)]
    topk_ready, topkT_done = sem("topk_ready"), sem("topkT_done")
    p_loaded = [sem(f"p_loaded{i}") for i in range(2)]
    e_stored = [sem(f"e_stored{i}") for i in range(2)]
    pT_done, pT_ready, e_done, e_ready = sem("pT_done"), sem("pT_ready"), sem("e_done"), sem("e_ready")
    own_sem = sem("dve_own3")
    PS = K.PS
    NEG = -1.0

    def conv_of(c):
        return K.conv[:, :, c * CHUNK:(c + 1) * CHUNK]

    def attn_of(c):
        return K.qT[:, :, c * CHUNK:(c + 1) * CHUNK]

    MEAN, VAR, MSC, MSA = range(4)

    with nc.Block() as block:

        @block.sync
        def _(sp):
            for dst, src in ((cg[:, :], io["chan_gain"]), (w_r[:, :, :], io["w_router"].rearrange("a (k p) n -> (a p) k n", p=P)),
                             (g2[:, :], io["norm2_g"].partition_broadcast(P)),
                             (w_pp[:, :, :], io["ple_proj"].rearrange("a (k p) n -> (a p) k n", p=P))):
                sp.dma_start(dst, src).then_inc(loaded, 16)
            sp.dma_start(w_out[:, :, :], io["w_out"].rearrange("a (k p) n -> (a p) k n", p=P)).then_inc(wout_loaded, 16)
            for t in range(TILES + 1):
                if t < TILES:
                    if t >= 3:
                        sp.wait_ge(h_stored[t % 3], 16 * (t // 3))
                        sp.wait_ge(ssq_ready, t - 2)
                        sp.wait_ge(xn_ready, t - 2)
                    sp.dma_start(h[:, t % 3, :], io["x_rows"](t)).then_inc(x_loaded[t % 3], 16)
                if t >= 1:
                    s = t - 1
                    sp.wait_ge(h_ready, s + 1)
                    sp.dma_start(K.h_rows(s), h[:, s % 3, :]).then_inc(h_stored[s % 3], 16)
                    sp.wait_ge(xn_ready, s + 1)
                    sp.dma_start(K.xn_rows(s), xn[:, s % 3, :]).then_inc(xn_stored[s % 3], 16)
            for t in range(TILES + 1):
                if t < TILES:
                    if t >= 2:
                        sp.wait_ge(pT_done, t - 1)
                    sp.dma_start(p_sb[:, t % 2, :], io["p_rows"](t)).then_inc(p_loaded[t % 2], 16)
                if t >= 1:
                    sp.wait_ge(e_ready, 2 * t)
                    sp.dma_start(K.e_rows(t - 1), e_sb[:, (t - 1) % 2, :]).then_inc(e_stored[(t - 1) % 2], 16)
            for i in range(3):
                sp.wait_ge(h_stored[i], 16 * (TILES // 3))
                sp.wait_ge(xn_stored[i], 16 * (TILES // 3))
            for i in range(2):
                sp.wait_ge(e_stored[i], 16 * (TILES // 2))

        @block.gpsimd
        def _(pool):
            for t in range(TILES):
                pool.wait_ge(ssq_ready, t + 1)
                nc.gpsimd.tensor_scalar(ms[:, t:t + 1], ssq[:, t:t + 1], 1.0 / D, EPS, ALU.mult, ALU.add).then_inc(ms_ready, 1)
                pool.wait_ge(ms_ready, t + 1)
                nc.gpsimd.tensor_tensor(rstd[:, t:t + 1], ms[:, t:t + 1], K.minus_half[:, :], ALU.pow).then_inc(rstd_ready, 1)

        def stat_no(c, which):
            return 4 * c + which + 1

        @block.scalar
        def _(act):
            act.wait_ge(loaded, 64)

            def square_of(src, c, which):
                nc.scalar.activation(sq[:, :, :], src, ACT.Square).then_inc(stat_ready, 1)

            def take_root(c, which):
                act.wait_ge(stat_done, stat_no(c, which))
                if 3 * c + which > 1:
                    act.wait_ge(inv_ready, 3 * c + which - 1)
                nc.scalar.activation(root[:, :], PS[:, 4, :], ACT.Sqrt, bias=K.eps[:, :]).then_inc(root_ready, 1)

            def chunk_norms(c):
                act.wait_ge(centred, 2 * c + 1)
                if c:
                    act.wait_ge(stat_done, stat_no(c - 1, MSA))
                square_of(conv_of(c), c, VAR)
                take_root(c, VAR)
                act.wait_ge(centred, 2 * c + 2)
                for i in range(CT):
                    s = nc.scalar.activation(conv_of(c)[:, i, :], conv_of(c)[:, i, :], ACT.Silu, bias=cg[:, CT + i:CT + i + 1],
                                             scale=cg[:, i:i + 1])
                s.then_inc(silu_ready, 1)
                act.wait_ge(silu_ready, c + 1)
                square_of(conv_of(c), c, MSC)
                take_root(c, MSC)
                square_of(attn_of(c), c, MSA)
                take_root(c, MSA)

            def route(t):
                act.wait_ge(logit_done, t + 1)
                act.wait_ge(aff_ready, 3 * t + 1)
                nc.scalar.activation(ex[:, t % 2, :], PS[:, 5, 0:E], ACT.Exp, bias=rt[:, t % 2, 0:1],
                                     accum_out=rt[:, t % 2, 1:2]).then_inc(exp_ready, 1)

            chunk_norms(0)
            for t in range(TILES + 3):
                if t < TILES and t % CHUNK_TILES == 1 and t // CHUNK_TILES + 1 < CHUNKS:
                    chunk_norms(t // CHUNK_TILES + 1)
                if t < TILES:
                    act.wait_ge(h_ready, t + 1)
                    if t:
                        act.wait_ge(ssq_ready, t)
                    nc.scalar.activation(junk[:, :], h[:, t % 3, :], ACT.Square, accum_out=ssq[:, t:t + 1]).then_inc(ssq_ready, 1)
                if 1 <= t < TILES + 1:
                    act.wait_ge(tr_done, t)
                    if t >= 2:
                        act.wait_ge(logit_done, t - 1)
                    nc.scalar.copy(xnT[:, :, :], PS[:, 6:8, :].rearrange("p b (k n) -> p (b k) n", k=4)).then_inc(xnT_ready, 1)
                if 2 <= t < TILES + 2:
                    route(t - 2)
            for t in range(TILES):
                act.wait_ge(pT_done, t + 1)
                if t >= 2:
                    act.wait_ge(e_done, t - 1)
                nc.scalar.copy(pT[:, t % 2, :, :], PS[:, 6 + t % 2, 0:2 * P].rearrange("p (k n) -> p k n", k=2)).then_inc(pT_ready, 1)
                act.wait_ge(e_done, t + 1)
                if t >= 2:
                    act.wait_ge(e_stored[t % 2], 16 * (t // 2))
                for half in range(2):
                    nc.scalar.copy(e_sb[:, t % 2, half * CHUNK:(half + 1) * CHUNK], PS[:, 2 * (t % 2) + half, :]).then_inc(e_ready, 1)

        @block.vector
        def _(dve):
            own = Chain(dve, own_sem)
            roots = [0]

            def over_tiles(ap):
                return ap.unsqueeze(1).broadcast_to((P, CT, CHUNK))

            def invert(user, count):
                if roots[0]:
                    dve.wait_ge(user, count)
                roots[0] += 1
                dve.wait_ge(root_ready, roots[0])
                nc.vector.reciprocal(inv[:, :], root[:, :]).then_inc(inv_ready, 1)
                dve.wait_ge(inv_ready, roots[0])

            def chunk_norms(c):
                dve.wait_ge(stat_done, stat_no(c, MEAN))
                nc.vector.tensor_tensor(conv_of(c), conv_of(c), over_tiles(PS[:, 4, :]), ALU.subtract).then_inc(centred, 1)
                invert(mix_ready, (CT + QT) * c)
                dve.wait_ge(centred, 2 * c + 1)
                nc.vector.tensor_tensor(conv_of(c), conv_of(c), over_tiles(inv[:, :]), ALU.mult).then_inc(centred, 1)
                invert(centred, 2 * c + 2)
                for i in range(CT):
                    nc.vector.scalar_tensor_tensor(conv_of(c)[:, i, :], conv_of(c)[:, i, :], cg[:, 2 * CT + i:2 * CT + i + 1], inv[:, :],
                                                   ALU.mult, ALU.mult).then_inc(mix_ready, 1)
                invert(mix_ready, (CT + QT) * c + CT)
                for i in range(QT):
                    nc.vector.scalar_tensor_tensor(attn_of(c)[:, i, :], attn_of(c)[:, i, :], cg[:, 3 * CT + i:3 * CT + i + 1], inv[:, :],
                                                   ALU.mult, ALU.mult).then_inc(mix_ready, 1)

            def residual(t):
                dve.wait_ge(out_done, t + 1)
                dve.wait_ge(x_loaded[t % 3], 16 * (t // 3 + 1))
                b = 2 * (t % 2)
                nc.vector.tensor_tensor(h[:, t % 3, :].rearrange("p (b n) -> p b n", b=2), PS[:, b:b + 2, :],
                                        h[:, t % 3, :].rearrange("p (b n) -> p b n", b=2), ALU.add).then_inc(h_ready, 1)

            def norm(t):
                dve.wait_ge(rstd_ready, t + 1)
                dve.wait_ge(h_ready, t + 1)
                if t >= 3:
                    dve.wait_ge(xn_stored[t % 3], 16 * (t // 3))
                    dve.wait_ge(tr_done, t - 2)
                nc.vector.scalar_tensor_tensor(xn[:, t % 3, :], h[:, t % 3, :], rstd[:, t:t + 1], g2[:, :], ALU.mult, ALU.mult).then_inc(xn_ready, 1)

            def route(t):
                i = t % 2
                dve.wait_ge(logit_done, t + 1)
                if t >= 2:
                    dve.wait_ge(exp_ready, t - 1)
                nc.vector.tensor_reduce(rt[:, i, 0:1], PS[:, 5, 0:E], AX.X, ALU.max, negate=True).then_inc(aff_ready, 1)
                dve.wait_ge(exp_ready, t + 1)
                nc.vector.reciprocal(rt[:, i, 2:3], rt[:, i, 1:2]).then_inc(aff_ready, 1)
                dve.wait_ge(aff_ready, 3 * t + 2)
                if t >= 2:
                    dve.wait_ge(affT_done, t - 1)
                nc.vector.tensor_scalar(aff[:, i, :], ex[:, i, :], rt[:, i, 2:3], None, ALU.mult).then_inc(aff_ready, 1)

            def keep_affinity(t):
                dve.wait_ge(affT_done, t + 1)
                dst = affP[:, t * P:(t + 1) * P] if t < PTILES else affS[:, (t - PTILES) * P:(t - PTILES + 1) * P]
                nc.vector.tensor_copy(dst, PS[0:E, 5, CHUNK // 2:CHUNK // 2 + P]).then_inc(affT_ready, 1)

            def top(vals, idx, a, rounds):
                for r in range(rounds):
                    v8, i8 = vals[:, 8 * r:8 * r + 8], idx[:, 8 * r:8 * r + 8]
                    own.wait(own.did(nc.vector.max(v8, a)))
                    own.wait(own.did(nc.vector.max_index(i8, v8, a)))
                    own.wait(own.did(nc.vector.match_replace(a, v8, a, NEG)))

            dve.wait_ge(loaded, 64)
            chunk_norms(0)
            for t in range(TILES + 3):
                if t < TILES and t % CHUNK_TILES == 1 and t // CHUNK_TILES + 1 < CHUNKS:
                    chunk_norms(t // CHUNK_TILES + 1)
                if t < TILES:
                    residual(t)
                    norm(t)
                if 3 <= t:
                    keep_affinity(t - 3)
                if 2 <= t < TILES + 2:
                    route(t - 2)
            dve.wait_ge(affT_ready, TILES)
            top(valP[:, :], idxP[:, :], affP[:, :], CAP_P // 8)
            top(valS[:, 0, :], idxS[:, :], affS[:, :], CAP_S // 8)
            nc.vector.tensor_copy(idxPf[:, :], idxP[:, :]).then_inc(topk_ready, 1)
            nc.vector.tensor_copy(idxSf[:, :], idxS[:, :]).then_inc(topk_ready, 1)
            nc.vector.tensor_copy(valS[:, 1, :], valS[:, 0, :]).then_inc(topk_ready, 1)
            dve.wait_ge(topkT_done, 1)
            own.did(nc.vector.tensor_copy(K.idxT_p[:, 0:E], PS[:, 5, 0:E]))
            own.did(nc.vector.tensor_copy(K.idxT_s[:, 0:E], PS[0:CAP_S, 5, E:2 * E]))
            own.did(nc.vector.tensor_copy(K.gateT_p[:, :], PS[:, 5, 2 * E:3 * E]))
            own.did(nc.vector.tensor_copy(K.gateT_s[:, :], PS[:, 5, 3 * E:4 * E]))

        @block.tensor
        def _(pe):
            def mean_of(src, c, which):
                for i in range(CT):
                    mm = nc.tensor.matmul(PS[:, 4, :], K.chan_mean[:, :], src[:, i, :], start=(i == 0), stop=(i == CT - 1))
                mm.then_inc(stat_done, 1)

            def first_mean(c):
                if c:
                    pe.wait_ge(root_ready, 3 * c)
                mean_of(conv_of(c), c, MEAN)

            def other_means(c):
                for n, which in enumerate((VAR, MSC, MSA)):
                    pe.wait_ge(stat_ready, 3 * c + n + 1)
                    if n == 0:
                        pe.wait_ge(centred, 2 * c + 1)
                    else:
                        pe.wait_ge(root_ready, 3 * c + n)
                    mean_of(sq, c, which)

            def transposes(t):
                pe.wait_ge(xn_ready, t + 1)
                if t:
                    pe.wait_ge(xnT_ready, t)
                for k in range(KD):
                    mm = nc.tensor.transpose(PS[:, 6 + k // 4, (k % 4) * P:(k % 4 + 1) * P], xn[:, t % 3, k * P:(k + 1) * P], K.ident[:, :])
                mm.then_inc(tr_done, 1)

            def logits(t):
                pe.wait_ge(xnT_ready, t + 1)
                if t:
                    pe.wait_ge(affT_ready, t)
                for k in range(KD):
                    mm = nc.tensor.matmul(PS[:, 5, 0:E], xnT[:, k, :], w_r[:, k, :], start=(k == 0), stop=(k == KD - 1))
                mm.then_inc(logit_done, 1)

            def turn_affinity(t):
                pe.wait_ge(aff_ready, 3 * t + 3)
                nc.tensor.transpose(PS[0:E, 5, CHUNK // 2:CHUNK // 2 + P], aff[:, t % 2, :], K.ident[:, :]).then_inc(affT_done, 1)

            pe.wait_ge(loaded, 64)
            first_mean(0)
            other_means(0)
            pe.wait_ge(wout_loaded, 16)
            for t in range(TILES + 3):
                c = t // CHUNK_TILES
                if t < TILES and t % CHUNK_TILES == 1 and c + 1 < CHUNKS:
                    first_mean(c + 1)
                if t < TILES:
                    if t % CHUNK_TILES == 0:
                        pe.wait_ge(mix_ready, (CT + QT) * (c + 1))
                    if t >= 2:
                        pe.wait_ge(h_ready, t - 1)
                    for k in range(KD):
                        lhs = (K.conv if k < CT else K.qT)[:, k % CT, t * P:(t + 1) * P]
                        for half in range(2):
                            mm = nc.tensor.matmul(PS[:, 2 * (t % 2) + half, :], lhs, w_out[:, k, half * CHUNK:(half + 1) * CHUNK],
                                                  start=(k == 0), stop=(k == KD - 1))
                    mm.then_inc(out_done, 1)
                if t < TILES and t % CHUNK_TILES == 1 and c + 1 < CHUNKS:
                    other_means(c + 1)
                if 3 <= t:
                    turn_affinity(t - 3)
                if 1 <= t < TILES + 1:
                    transposes(t - 1)
                if 2 <= t < TILES + 2:
                    logits(t - 2)
            for t in range(TILES):
                pe.wait_ge(p_loaded[t % 2], 16 * (t // 2 + 1))
                if t < 2:
                    pe.wait_ge(xnT_ready, TILES)
                    pe.wait_ge(h_ready, TILES)
                else:
                    pe.wait_ge(pT_ready, t - 1)
                    pe.wait_ge(e_ready, 2 * (t - 1))
                for k in range(2):
                    mm = nc.tensor.transpose(PS[:, 6 + t % 2, k * P:(k + 1) * P], p_sb[:, t % 2, k * P:(k + 1) * P], K.ident[:, :])
                mm.then_inc(pT_done, 1)
                pe.wait_ge(pT_ready, t + 1)
                for k in range(2):
                    for half in range(2):
                        mm = nc.tensor.matmul(PS[:, 2 * (t % 2) + half, :], pT[:, t % 2, k, :], w_pp[:, k, half * CHUNK:(half + 1) * CHUNK],
                                              start=(k == 0), stop=(k == 1))
                mm.then_inc(e_done, 1)
            pe.wait_ge(topk_ready, 3)
            pe.wait_ge(affT_ready, TILES)
            small = K.ident[0:E, 0:E]
            nc.tensor.transpose(PS[:, 5, 0:E], idxPf[:, :], small)
            nc.tensor.transpose(PS[0:CAP_S, 5, E:2 * E], idxSf[:, :], small)
            nc.tensor.transpose(PS[:, 5, 2 * E:3 * E], valP[:, :], small)
            nc.tensor.transpose(PS[:, 5, 3 * E:4 * E], valS[:, :, :].rearrange("e a c -> e (a c)"), small).then_inc(topkT_done, 1)


def stage_experts(nc, K, io, sb, sem):
    RAW, HL = 6, 4
    NCH = 3 * FT // 2
    CC = 2048
    raw = sb("raw", [P, RAW, CC])
    wh, wl = sb("wh", [P, HL, CC], F32R), sb("wl", [P, HL, CC], F32R)
    xe_p, xe_s = sb("xe_p", [CAP_P, D]), sb("xe_s", [CAP_S, D])
    xhl = sb("xhl", [P, KD, 2, CAP], F32R)
    hhl = sb("hhl", [P, FT, 2 * CAP], F32R)
    HIGH, LOW_S, LOW_P, BOTH_S = slice(0, CAP), slice(CAP, CAP + CAP_S), slice(CAP + CAP_S, 2 * CAP), slice(CAP_P, CAP_P + 2 * CAP_S)
    gsum, usum, sg, hid = (sb(n, [P, 2, CAP]) for n in ("gsum", "usum", "sg", "hid"))
    y_p, y_s, y_low = sb("y_p", [CAP_P, D]), sb("y_s", [CAP_S, D]), sb("y_low", [CAP_S, D])
    ix_p, ix_s, sx_p, sx_s = sb("ix_p", [P, 1], U32), sb("ix_s", [CAP_S, 1], U32), sb("sx_p", [P, 1], U32), sb("sx_s", [CAP_S, 1], U32)
    gt_p, gt_s = sb("gt_p", [P, 1]), sb("gt_s", [P, 1])

    raw_loaded = [sem(f"raw_loaded{i}") for i in range(RAW)]
    high_ready = sem("high_ready")
    split_done = sem("split_done")
    down_used = sem("down_used")
    gathered_p, gathered_s = sem("gathered_p"), sem("gathered_s")
    index_ready, gates_ready, sindex_ready = sem("index_ready"), sem("gates_ready"), sem("sindex_ready")
    rows_asked = sem("rows_asked")
    xt_done, xh_ready, xl_ready = sem("xt_done"), sem("xh_ready"), sem("xl_ready")
    gate_done, up_done = sem("gate_done"), sem("up_done")
    gsum_ready, usum_ready = sem("gsum_ready"), sem("usum_ready")
    sg_ready, hid_ready, hh_ready, hl_ready = sem("sg_ready"), sem("hid_ready"), sem("hh_ready"), sem("hl_ready")
    yp_ready, ylow_ready, ys_ready = sem("yp_ready"), sem("ylow_ready"), sem("ys_ready")
    scat_p, scat_s = sem("scattered_p"), sem("scattered_s")
    PS = K.PS

    wg = io["w_gate"].rearrange("a e (k p) f -> (a e) p k f", p=P)
    wu = io["w_up"].rearrange("a e (k p) f -> (a e) p k f", p=P)
    wd = io["w_down"].rearrange("a e (k p) n -> (a e) p k n", p=P)

    def split_ready(eng, e, c):
        eng.wait_ge(split_done, e * NCH + (RAW + c + 1))

    with nc.Block() as block:

        @block.sync
        def _(sp):
            with sp.Fori(0, E) as e:
                for c in range(NCH):
                    sp.wait_ge(split_done, e * NCH + (c + 1))
                    dst = raw[:, c % RAW, :]
                    if c < FT:
                        src = (wg if c % 2 == 0 else wu)[bass.ds(e, 1), :, :, (c // 2) * 2 * P:(c // 2 + 1) * 2 * P].rearrange("e p k f -> (e p) k f")
                        dst = dst.rearrange("p (k f) -> p k f", k=KD)
                    else:
                        i = c - FT
                        src = wd[bass.ds(e, 1), :, 2 * i:2 * i + 2, :].rearrange("e p k n -> (e p) k n")
                        dst = dst.rearrange("p (k n) -> p k n", k=2)
                    sp.dma_start(dst, src).then_inc(raw_loaded[c % RAW], 16)
            sp.dma_start(K.w_pg[:, :, :], io["ple_gate_w"].rearrange("a (k p) n -> (a p) k n", p=P)).then_inc(K.wpg_loaded, 16)
            sp.wait_ge(scat_p, 16 * E)
            sp.wait_ge(scat_s, 16 * E)

        def loaded_wait(eng, e, c):
            eng.wait_ge(raw_loaded[c % RAW], e * (16 * NCH // RAW) + 16 * (c // RAW + 1))

        @block.gpsimd
        def _(pool):
            def gather(e, nth):
                nc.gpsimd.tensor_copy(ix_p[:, :], K.idxT_p[:, bass.ds(e, 1)]).then_inc(index_ready, 1)
                nc.gpsimd.tensor_copy(ix_s[:, :], K.idxT_s[:, bass.ds(e, 1)]).then_inc(index_ready, 1)
                pool.wait_ge(index_ready, nth * 2 + 2)
                pool.sem_inc(rows_asked, 1)
                nc.gpsimd.indirect_dma_start(xe_p[:, :], None, K.xn_p, bass.IndirectOffsetOnAxis(ap=ix_p[:, :], axis=0)).then_inc(gathered_p, 16)
                nc.gpsimd.indirect_dma_start(xe_s[:, :], None, K.xn_s, bass.IndirectOffsetOnAxis(ap=ix_s[:, :], axis=0)).then_inc(gathered_s, 16)

            def combine(f, nth):
                i = f % 2
                pool.wait_ge(sg_ready, nth + (f + 1))
                pool.wait_ge(usum_ready, nth + (f + 3))
                if f >= 2:
                    pool.wait_ge(hl_ready, 2 * nth + 2 * (f - 1))
                nc.gpsimd.tensor_tensor(hid[:, i, :], sg[:, i, :], usum[:, i, :], ALU.mult).then_inc(hid_ready, 1)

            def low_hid(f, nth):
                i = f % 2
                pool.wait_ge(hh_ready, nth + (f + 1))
                nc.gpsimd.tensor_tensor(hhl[:, f, LOW_P], hid[:, i, 0:CAP_P], hhl[:, f, 0:CAP_P].bitcast(F32), ALU.subtract).then_inc(hl_ready, 1)
                nc.gpsimd.tensor_tensor(hhl[:, f, LOW_S], hid[:, i, CAP_P:CAP], hhl[:, f, CAP_P:CAP].bitcast(F32), ALU.subtract).then_inc(hl_ready, 1)

            def body(e, first=False, last=False):
                for f in range(FT):
                    combine(f, e * FT)
                    if f:
                        low_hid(f - 1, e * FT)
                    if f == 1 and not first:
                        scatter(e - 1)
                    if f == 3 and not first:
                        pool.wait_ge(scat_p, e * 16)
                        pool.wait_ge(scat_s, e * 16)
                    if f == 3:
                        pool.wait_ge(yp_ready, e * 1 + 1)
                        pool.wait_ge(ys_ready, e * 1 + 1)
                        nc.gpsimd.tensor_copy(gt_p[:, :], K.gateT_p[:, bass.ds(e, 1)]).then_inc(gates_ready, 1)
                        nc.gpsimd.tensor_copy(gt_s[:, :], K.gateT_s[:, bass.ds(e, 1)]).then_inc(gates_ready, 1)
                    if f == 5 and not last:
                        pool.wait_ge(gathered_p, e * 16 + 16)
                        pool.wait_ge(gathered_s, e * 16 + 16)
                        pool.wait_ge(xt_done, e * 2 + 2)
                        gather(e + 1, e + 1)
                low_hid(FT - 1, e * FT)

            def scatter(e):
                nc.gpsimd.tensor_copy(sx_p[:, :], K.idxT_p[:, bass.ds(e, 1)]).then_inc(sindex_ready, 1)
                nc.gpsimd.tensor_copy(sx_s[:, :], K.idxT_s[:, bass.ds(e, 1)]).then_inc(sindex_ready, 1)
                pool.wait_ge(sindex_ready, e * 2 + 2)
                pool.wait_ge(yp_ready, e * 1 + 2)
                pool.sem_inc(rows_asked, 1)
                nc.gpsimd.indirect_dma_start(K.h_p, bass.IndirectOffsetOnAxis(ap=sx_p[:, :], axis=0), y_p[:, :], None,
                                             compute_op=ALU.add).then_inc(scat_p, 16)
                pool.wait_ge(ys_ready, e * 1 + 2)
                pool.sem_inc(rows_asked, 1)
                nc.gpsimd.indirect_dma_start(K.h_s, bass.IndirectOffsetOnAxis(ap=sx_s[:, :], axis=0), y_s[:, :], None,
                                             compute_op=ALU.add).then_inc(scat_s, 16)

            gather(0, 0)
            body(0, first=True)
            with pool.Fori(1, E - 1) as e:
                body(e)
            body(E - 1, last=True)
            pool.wait_ge(scat_p, 16 * (E - 1))
            pool.wait_ge(scat_s, 16 * (E - 1))
            scatter(E - 1)

        @block.scalar
        def _(act):
            act.sem_inc(yp_ready, 1)

            def high(e, c):
                loaded_wait(act, e, c)
                prev = c - HL
                if 0 <= prev < FT:
                    act.wait_ge(gate_done if prev % 2 == 0 else up_done, e * FT + (2 * (prev // 2) + 2))
                elif prev >= FT:
                    act.wait_ge(down_used, e * (FT // 2) + (prev - FT + 1))
                nc.scalar.copy(wh[:, c % HL, :], raw[:, c % RAW, :]).then_inc(high_ready, 1)

            def x_high(nth):
                for half in range(2):
                    act.wait_ge(xt_done, nth * 2 + (half + 1))
                    src = PS[:, 2 * half:2 * half + 2, 0:2 * CAP].rearrange("p b (k n) -> p b k n", k=2)
                    dst = xhl[:, 4 * half:4 * half + 4, 0, :].rearrange("p (b k) n -> p b k n", k=2)
                    nc.scalar.copy(dst, src).then_inc(xh_ready, 1)

            def gate_silu(e, f):
                i = f % 2
                act.wait_ge(gsum_ready, e * FT + (f + 3))
                if f >= 2:
                    act.wait_ge(hid_ready, e * FT + (f - 1))
                nc.scalar.activation(sg[:, i, :], gsum[:, i, :], ACT.Silu).then_inc(sg_ready, 1)

            def high_hid(e, f):
                i = f % 2
                act.wait_ge(hid_ready, e * FT + (f + 1))
                nc.scalar.copy(hhl[:, f, HIGH], hid[:, i, :]).then_inc(hh_ready, 1)

            def body(e, first=False, last=False):
                for fp in range(FT // 2):
                    for f in (2 * fp, 2 * fp + 1):
                        gate_silu(e, f)
                        if f:
                            high_hid(e, f - 1)
                    high(e, 2 * fp + 4)
                    high(e, 2 * fp + 5)
                high_hid(e, FT - 1)
                for c in range(FT + HL, NCH + (0 if last else HL)):
                    high(e, c)
                    if c == FT + HL + 1 and not last:
                        x_high(e + 1)
                act.wait_ge(down_used, e * (FT // 2) + FT // 2)
                act.wait_ge(gates_ready, e * 2 + 2)
                if not first:
                    act.wait_ge(scat_p, e * 16)
                nc.scalar.mul(y_p[:, :], PS[:, 4:6, :].rearrange("p b n -> p (b n)"), gt_p[:, 0:1]).then_inc(yp_ready, 1)
                act.wait_ge(ys_ready, e * 1 + 1)
                nc.scalar.mul(y_low[:, :], PS[CAP_S:P, 6:8, :].rearrange("p b n -> p (b n)"), gt_s[CAP_S:P, 0:1]).then_inc(ylow_ready, 1)

            x_high(0)
            for c in range(HL):
                high(0, c)
            body(0, first=True)
            with act.Fori(1, E - 1) as e:
                body(e)
            body(E - 1, last=True)

        @block.vector
        def _(dve):
            dve.sem_inc(split_done, RAW)
            dve.sem_inc(gsum_ready, 2)
            dve.sem_inc(usum_ready, 2)
            dve.sem_inc(ys_ready, 1)

            def low(e, c):
                dve.wait_ge(high_ready, e * NCH + (c + 1))
                nc.vector.tensor_tensor(wl[:, c % HL, :], raw[:, c % RAW, :], wh[:, c % HL, :].bitcast(F32), ALU.subtract).then_inc(split_done, 1)

            def x_low(nth):
                for half in range(2):
                    dve.wait_ge(xh_ready, nth * 2 + (half + 1))
                    src = PS[:, 2 * half:2 * half + 2, 0:2 * CAP].rearrange("p b (k n) -> p b k n", k=2)
                    at = lambda part: xhl[:, 4 * half:4 * half + 4, part, :].rearrange("p (b k) n -> p b k n", k=2)
                    nc.vector.tensor_tensor(at(1), src, at(0).bitcast(F32), ALU.subtract).then_inc(xl_ready, 1)

            def sums(e, f):
                i = f % 2
                for done, ready, dst, bank, read in ((gate_done, gsum_ready, gsum, i, sg_ready), (up_done, usum_ready, usum, 2 + i, hid_ready)):
                    dve.wait_ge(done, e * FT + (f + 1))
                    if f >= 2:
                        dve.wait_ge(read, e * FT + (f - 1))
                    nc.vector.tensor_reduce(dst[:, i, :], PS[:, bank, 0:2 * CAP].rearrange("p (a n) -> p n a", a=2), AX.X, ALU.add).then_inc(ready, 1)

            def body(e, first=False, last=False):
                for fp in range(FT // 2):
                    for f in (2 * fp, 2 * fp + 1):
                        sums(e, f)
                    low(e, 2 * fp + 4)
                    low(e, 2 * fp + 5)
                for c in range(FT + HL, NCH + (0 if last else HL)):
                    low(e, c)
                    if c == FT + HL + 1 and not last:
                        x_low(e + 1)
                dve.wait_ge(ylow_ready, e * 1 + 1)
                if not first:
                    dve.wait_ge(scat_s, e * 16)
                nc.vector.scalar_tensor_tensor(y_s[:, :], PS[0:CAP_S, 6:8, :].rearrange("p b n -> p (b n)"), gt_s[0:CAP_S, 0:1], y_low[:, :],
                                               ALU.mult, ALU.add).then_inc(ys_ready, 1)

            x_low(0)
            for c in range(HL):
                low(0, c)
            body(0, first=True)
            with dve.Fori(1, E - 1) as e:
                body(e)
            body(E - 1, last=True)

        @block.tensor
        def _(pe):
            def turn(nth):
                pe.wait_ge(gathered_p, nth * 16 + 16)
                pe.wait_ge(gathered_s, nth * 16 + 16)
                pe.wait_ge(gsum_ready, nth * FT + 2)
                pe.wait_ge(usum_ready, nth * FT + 2)
                for k in range(KD):
                    b, o = k // 2, (k % 2) * CAP
                    nc.tensor.transpose(PS[:, b, o:o + CAP_P], xe_p[:, k * P:(k + 1) * P], K.ident[:, :])
                    mm = nc.tensor.transpose(PS[:, b, o + CAP_P:o + CAP], xe_s[:, k * P:(k + 1) * P], K.ident[0:CAP_S, 0:CAP_S])
                    if k % 4 == 3:
                        mm.then_inc(xt_done, 1)

            def gate_up(e, f):
                i, sub = f % 2, f % 2
                for part, (bank, free, done) in enumerate(((i, gsum_ready, gate_done), (2 + i, usum_ready, up_done))):
                    c = (f // 2) * 2 + part
                    if sub == 0:
                        split_ready(pe, e, c)
                    pe.wait_ge(free, e * FT + (f + 1))
                    hi = wh[:, c % HL, :].rearrange("p (k f) -> p k f", k=KD)
                    lo = wl[:, c % HL, :].rearrange("p (k f) -> p k f", k=KD)
                    for k in range(KD):
                        nc.tensor.matmul(PS[:, bank, 0:2 * CAP], hi[:, k, sub * P:(sub + 1) * P], xhl[:, k, :, :].rearrange("p a n -> p (a n)"),
                                         start=(k == 0), stop=False)
                        mm = nc.tensor.matmul(PS[:, bank, 0:CAP], lo[:, k, sub * P:(sub + 1) * P], xhl[:, k, 0, :],
                                              start=False, stop=(k == KD - 1))
                    mm.then_inc(done, 1)

            def down(e, f):
                c = FT + f // 2
                if f % 2 == 0:
                    split_ready(pe, e, c)
                pe.wait_ge(hl_ready, e * (2 * FT) + 2 * (f + 1))
                if f == 0:
                    pe.wait_ge(yp_ready, e * 1 + 1)
                    pe.wait_ge(ys_ready, e * 1 + 1)
                at = (f % 2) * D
                hi = [wh[:, c % HL, at + n * CHUNK:at + (n + 1) * CHUNK] for n in range(2)]
                lo = [wl[:, c % HL, at + n * CHUNK:at + (n + 1) * CHUNK] for n in range(2)]
                ph, pl, both = hhl[:, f, 0:CAP_P], hhl[:, f, LOW_P], hhl[:, f, BOTH_S]
                first, final = f == 0, f == FT - 1
                for n in range(2):
                    nc.tensor.matmul(PS[:, 4 + n, :], ph, hi[n], start=first, stop=False)
                for n in range(2):
                    nc.tensor.matmul(PS[:, 4 + n, :], ph, lo[n], start=False, stop=False)
                for n in range(2):
                    nc.tensor.matmul(PS[:, 4 + n, :], pl, hi[n], start=False, stop=final)
                for n in range(2):
                    nc.tensor.matmul(PS[:, 6 + n, :], both, hi[n], start=first, stop=False)
                for n in range(2):
                    mm = nc.tensor.matmul(PS[:, 6 + n, :], both, lo[n], start=False, stop=final)
                return mm

            def body(e, first=False, last=False):
                pe.wait_ge(xl_ready, e * 2 + 2)
                for f in range(FT):
                    gate_up(e, f)
                for f in range(FT):
                    mm = down(e, f)
                    if f % 2 == 1:
                        mm.then_inc(down_used, 1)
                    if f == 3 and not last:
                        turn(e + 1)

            turn(0)
            body(0, first=True)
            with pe.Fori(1, E - 1) as e:
                body(e)
            body(E - 1, last=True)


def stage_embed(nc, K, io, sb, sem):
    wh, wl = sb("pgh", [P, KD, D], F32R), sb("pgl", [P, KD, D], F32R)
    g3, bias = sb("g3", [P, D]), sb("bias", [P, D])
    H = 6
    h, e_in = sb("h5", [P, H, D]), sb("e_in", [P, 2, D])
    hn = sb("hn", [P, 2, D])
    nh, nl = sb("hnT_high", [P, 3, KD, P], F32R), sb("hnT_low", [P, 3, KD, P], F32R)
    pre, out = sb("pre", [P, 2, D]), sb("out5", [P, 2, D])
    sig = sb("sig", [P, D])
    ssq, ms, rstd = sb("ssq5", [P, TILES]), sb("ms5", [P, TILES]), sb("rstd5", [P, TILES])
    loaded = sem("loaded5")
    h_loaded = [sem(f"h5_loaded{i}") for i in range(H)]
    e_loaded = [sem(f"e5_loaded{i}") for i in range(2)]
    out_stored = [sem(f"out_stored{i}") for i in range(2)]
    ssq_ready, ms_ready, rstd_ready = sem("ssq5_ready"), sem("ms5_ready"), sem("rstd5_ready")
    wh_ready, wl_ready = sem("pgh_ready"), sem("pgl_ready")
    hn_ready, tr_done, high_ready, low_ready, gate_done = sem("hn_ready"), sem("tr5_done"), sem("nh_ready"), sem("nl_ready"), sem("gate5_done")
    pre_ready, sig_ready, prod_ready, out_ready = sem("pre_ready"), sem("sig5_ready"), sem("prod_ready"), sem("out_ready")
    PS = K.PS

    def turned():
        return PS[:, 6:8, :].rearrange("p b (k n) -> p (b k) n", k=4)

    with nc.Block() as block:

        @block.sync
        def _(sp):
            def load(t):
                if t >= H:
                    sp.wait_ge(out_ready, t - H + 1)
                sp.dma_start(h[:, t % H, :], K.h_rows(t)).then_inc(h_loaded[t % H], 16)

            load(0)
            sp.dma_start(g3[:, :], io["ple_norm_g"].partition_broadcast(P)).then_inc(loaded, 16)
            for t in range(1, H):
                load(t)
            sp.dma_start(bias[:, :], io["ple_gate_b"].partition_broadcast(P)).then_inc(loaded, 16)
            for t in range(TILES):
                if t >= 2:
                    sp.wait_ge(prod_ready, t - 1)
                sp.dma_start(e_in[:, t % 2, :], K.e_rows(t)).then_inc(e_loaded[t % 2], 16)
                if t >= 1:
                    sp.wait_ge(out_ready, t)
                    sp.dma_start(io["out_rows"](t - 1), out[:, (t - 1) % 2, :]).then_inc(out_stored[(t - 1) % 2], 16)
                    if t - 1 + H < TILES:
                        load(t - 1 + H)
            sp.wait_ge(out_ready, TILES)
            sp.dma_start(io["out_rows"](TILES - 1), out[:, (TILES - 1) % 2, :]).then_inc(out_stored[(TILES - 1) % 2], 16)
            for i in range(2):
                sp.wait_ge(out_stored[i], 16 * (TILES // 2))

        @block.gpsimd
        def _(pool):
            for t in range(TILES):
                pool.wait_ge(ssq_ready, t + 1)
                nc.gpsimd.tensor_scalar(ms[:, t:t + 1], ssq[:, t:t + 1], 1.0 / D, EPS, ALU.mult, ALU.add).then_inc(ms_ready, 1)
                pool.wait_ge(ms_ready, t + 1)
                nc.gpsimd.tensor_tensor(rstd[:, t:t + 1], ms[:, t:t + 1], K.minus_half[:, :], ALU.pow).then_inc(rstd_ready, 1)

        @block.scalar
        def _(act):
            def square(t):
                act.wait_ge(h_loaded[t % H], 16 * (t // H + 1))
                if t >= 2:
                    act.wait_ge(sig_ready, t - 1)
                nc.scalar.activation(pre[:, t % 2, :], h[:, t % H, :], ACT.Square, accum_out=ssq[:, t:t + 1]).then_inc(ssq_ready, 1)

            def high(t):
                act.wait_ge(tr_done, t + 1)
                if t >= 3:
                    act.wait_ge(gate_done, t - 2)
                nc.scalar.copy(nh[:, t % 3, :, :], turned()).then_inc(high_ready, 1)

            def sigmoid(t):
                act.wait_ge(pre_ready, t + 1)
                if t:
                    act.wait_ge(prod_ready, t)
                nc.scalar.activation(sig[:, :], pre[:, t % 2, :], ACT.Sigmoid).then_inc(sig_ready, 1)

            square(0)
            square(1)
            act.wait_ge(K.wpg_loaded, 16)
            for k in range(KD):
                nc.scalar.copy(wh[:, k, :], K.w_pg[:, k, :]).then_inc(wh_ready, 1)
                if k == 1:
                    high(0)
            high(1)
            for t in range(TILES):
                sigmoid(t)
                if t + 2 < TILES:
                    square(t + 2)
                    high(t + 2)

        @block.vector
        def _(dve):
            def norm(t):
                dve.wait_ge(rstd_ready, t + 1)
                if t >= 2:
                    dve.wait_ge(tr_done, t - 1)
                nc.vector.scalar_tensor_tensor(hn[:, t % 2, :], h[:, t % H, :], rstd[:, t:t + 1], g3[:, :], ALU.mult, ALU.mult).then_inc(hn_ready, 1)

            def low(t):
                dve.wait_ge(high_ready, t + 1)
                nc.vector.tensor_tensor(nl[:, t % 3, :, :], turned(), nh[:, t % 3, :, :].bitcast(F32), ALU.subtract).then_inc(low_ready, 1)

            def low_weights(k):
                dve.wait_ge(wh_ready, k + 1)
                nc.vector.tensor_tensor(wl[:, k, :], K.w_pg[:, k, :], wh[:, k, :].bitcast(F32), ALU.subtract).then_inc(wl_ready, 1)

            halves = lambda ap: ap.rearrange("p (b n) -> p b n", b=2)
            dve.wait_ge(loaded, 32)
            norm(0)
            norm(1)
            for k in range(KD):
                low_weights(k)
                if k == 1:
                    low(0)
            low(1)
            for t in range(TILES):
                i = t % 2
                dve.wait_ge(gate_done, t + 1)
                dve.wait_ge(ssq_ready, t + 1)
                nc.vector.tensor_tensor(halves(pre[:, i, :]), PS[:, 2 * i:2 * i + 2, :], halves(bias[:, :]), ALU.add).then_inc(pre_ready, 1)
                if t + 2 < TILES:
                    norm(t + 2)
                dve.wait_ge(sig_ready, t + 1)
                dve.wait_ge(e_loaded[i], 16 * (t // 2 + 1))
                if t >= 2:
                    dve.wait_ge(out_stored[i], 16 * (t // 2))
                nc.vector.tensor_tensor(out[:, i, :], sig[:, :], e_in[:, i, :], ALU.mult).then_inc(prod_ready, 1)
                dve.wait_ge(prod_ready, t + 1)
                nc.vector.tensor_tensor(out[:, i, :], out[:, i, :], h[:, t % H, :], ALU.add).then_inc(out_ready, 1)
                if t + 2 < TILES:
                    low(t + 2)

        @block.tensor
        def _(pe):
            def turn(t):
                pe.wait_ge(hn_ready, t + 1)
                if t:
                    pe.wait_ge(low_ready, t)
                for k in range(KD):
                    mm = nc.tensor.transpose(PS[:, 6 + k // 4, (k % 4) * P:(k % 4 + 1) * P], hn[:, t % 2, k * P:(k + 1) * P], K.ident[:, :])
                mm.then_inc(tr_done, 1)

            turn(0)
            turn(1)
            for t in range(TILES):
                pe.wait_ge(low_ready, t + 1)
                if t >= 2:
                    pe.wait_ge(pre_ready, t - 1)
                b = 2 * (t % 2)
                for k in range(KD):
                    if t == 0:
                        pe.wait_ge(wl_ready, k + 1)
                    for x, w in ((nh, wh), (nh, wl), (nl, wh)):
                        for half in range(2):
                            mm = nc.tensor.matmul(PS[:, b + half, :], x[:, t % 3, k, :], w[:, k, half * CHUNK:(half + 1) * CHUNK],
                                                  start=(k == 0 and x is nh and w is wh), stop=(k == KD - 1 and x is nl))
                    if k == KD // 2 and 0 < t and t + 1 < TILES:
                        turn(t + 1)
                mm.then_inc(gate_done, 1)


def encoder_layer_kernel(nc, io, stages=5):
    K = Kept()

    def rows(prompt, sample):
        return lambda t: prompt[t * P:(t + 1) * P, :] if t < PTILES else sample[(t - PTILES) * P:(t - PTILES + 1) * P, :]

    io["x_rows"] = rows(io["x_prompt"][0], io["x_sample"][0])
    io["p_rows"] = rows(io["p_prompt"][0, 0], io["p_sample"][0, 0])
    io["out_rows"] = rows(io["y_prompt"][0], io["y_sample"][0])
    def scratch(name):
        return [nc.dram_tensor(f"{name}_rows_{g}", (t, D), F32, kind="Internal").ap() for g, t in (("p", T_PROMPT), ("s", T_SAMPLE))]

    K.h_p, K.h_s = scratch("h")
    K.xn_p, K.xn_s = scratch("xn")
    K.h_rows, K.xn_rows, K.e_rows = rows(K.h_p, K.h_s), rows(K.xn_p, K.xn_s), rows(*scratch("e"))

    with ExitStack() as whole:
        def alloc(stack):
            return lambda name, shape, dt=F32: stack.enter_context(nc.sbuf_tensor(name, shape, dt))

        def sem(name):
            return whole.enter_context(nc.semaphore(name))

        keep = alloc(whole)
        K.PS = whole.enter_context(nc.psum_tensor("PS", [P, 8, CHUNK], F32))
        K.ident, K.eps, K.minus_half = keep("ident", [P, P]), keep("eps", [P, 1]), keep("minus_half", [P, 1])
        K.idxT_p, K.idxT_s = keep("idxT_p", [P, E], U32), keep("idxT_s", [CAP_S, E], U32)
        K.gateT_p, K.gateT_s = keep("gateT_p", [P, E]), keep("gateT_s", [P, E])
        K.glu_cleared = sem("glu_cleared")
        with ExitStack() as mixers:
            part = alloc(mixers)
            K.qT, K.conv = part("qT", [P, QT, T_ALL]), part("conv", [P, CT, T_ALL])
            K.chan_mean = part("chan_mean", [P, P])
            K.taps_ready = sem("taps_ready")
            with ExitStack() as attention:
                part = alloc(attention)
                K.k_high, K.k_low = part("k_high", [P, KV, T_ALL], F32R), part("k_low", [P, KV, T_ALL], F32R)
                K.v_high, K.v_low = part("v_high", [P, TILES, KV, P], F32R), part("v_low", [P, TILES, KV, HD], F32R)
                K.conv_w = part("conv_w", [P, CT * (TAPS + 1)])
                K.head_ones, K.rot = part("head_ones", [P, P]), part("rot", [P, P])
                K.glu = part("glu", [P, CT, GLU_COLS])
                with ExitStack() as s:
                    stage_project(nc, K, io, alloc(s), sem)
                if stages >= 2:
                    with ExitStack() as s:
                        stage_attend(nc, K, io, alloc(s), sem)
            if stages >= 3:
                with ExitStack() as s:
                    stage_mix_route(nc, K, io, alloc(s), sem)
        K.w_pg, K.wpg_loaded = keep("w_pg", [P, KD, D]), sem("wpg_loaded")
        if stages >= 4:
            with ExitStack() as s:
                stage_experts(nc, K, io, alloc(s), sem)
        if stages >= 5:
            with ExitStack() as s:
                stage_embed(nc, K, io, alloc(s), sem)


def shape_constants():
    import numpy as np
    f = np.float32
    half = HD // 4
    freqs = (f(1.0) / (f(10000.0) ** (np.arange(0, HD // 2, 2, dtype=f) / f(HD // 2)))).astype(f)
    t = np.arange(T_PROMPT)
    ang = np.zeros((HD, T_PROMPT), f)
    for d in range(HD):
        pos = (t // 64 if d < HD // 2 else t % 64).astype(f)
        ang[d] = pos * freqs[d % half]
    two = lambda a: np.ascontiguousarray(np.concatenate([a, a], 0).astype(f))
    rot = np.zeros((P, P), f)
    for base in range(0, P, HD // 2):
        for i in range(half):
            rot[base + half + i, base + i] = -1.0
            rot[base + i, base + half + i] = 1.0
    head_ones = np.kron(np.eye(P // HD), np.full((HD, HD), 1.0 / HD)).astype(f)
    return dict(cos=two(np.cos(ang)), sin=two(np.sin(ang)), rot=rot, head_ones=head_ones, ident=np.eye(P, dtype=f),
                chan_mean=np.full((P, P), 1.0 / D_CONV, f), eps_col=np.full((P, 1), EPS, f))


def layouts(inputs):
    import numpy as np
    a = {n: np.ascontiguousarray(v) for n, v in inputs.items()}
    col = lambda v, k: np.ascontiguousarray(v.reshape(k, P).T)
    a["norm1_g"] = col(a["norm1_g"], KD)
    a["qk_gain"] = np.ascontiguousarray(np.stack([np.tile(a.pop("q_norm_g")[0], 2), np.tile(a.pop("k_norm_g")[0], 2)], 1))
    taps = np.concatenate([a.pop("conv_dw_w")[0], a.pop("conv_dw_b")], 0)
    a["conv_w"] = np.ascontiguousarray(taps.reshape(TAPS + 1, CT, P).transpose(2, 1, 0).reshape(P, CT * (TAPS + 1)))
    a["chan_gain"] = np.ascontiguousarray(np.concatenate([col(a.pop(n), CT) for n in ("conv_ln_g", "conv_ln_b", "conv_out_g", "attn_out_g")], 1))
    for n in ("norm2_g", "ple_norm_g", "ple_gate_b"):
        a[n] = a[n].reshape(D)
    return a | shape_constants()


def kernel(**inputs):
    import concourse.bacc as _bacc
    from concourse.bass_utils import run_bass_kernel_spmd as _run

    arrays = layouts(inputs)
    nc = _bacc.Bacc("TRN2", target_bir_lowering=False, num_devices=1)
    io = {name: nc.dram_tensor(f"in_{name}", a.shape, mybir.dt.from_np(a.dtype), kind="ExternalInput").ap()
          for name, a in arrays.items()}
    for name, t in (("y_prompt", T_PROMPT), ("y_sample", T_SAMPLE)):
        io[name] = nc.dram_tensor(f"out_{name}", (1, t, D), F32, kind="ExternalOutput").ap()
    encoder_layer_kernel(nc, io)
    r = _run(nc, [{f"in_{n}": a for n, a in arrays.items()}], core_ids=[0])
    return r.results[0]["out_y_prompt"], r.results[0]["out_y_sample"]
```

```python
from contextlib import ExitStack
from typing import NamedTuple

import concourse.bass as bass
from concourse import mybir

F32 = mybir.dt.float32
F32R = mybir.dt.float32r
U32 = mybir.dt.uint32
ALU = mybir.AluOpType
ACT = mybir.ActivationFunctionType
AX = mybir.AxisListType

P = 128
D = 1024
KD = D // P
T_PROMPT, T_SAMPLE = 1024, 512
T_ALL = T_PROMPT + T_SAMPLE
TILES = T_ALL // P
PTILES = T_PROMPT // P
CHUNK = 512
CHUNKS = T_ALL // CHUNK
D_CONV = 512
CT = D_CONV // P
TAPS = 31
PAD = TAPS // 2
HEADS, KV, HD = 8, 2, 64
D_Q = HEADS * HD
QT = D_Q // P
KV_GROUP = HEADS // KV
SCALE = HD ** -0.5
EPS = 1e-6
E = 16
CAP_P, CAP_S = 2 * T_PROMPT // E, 2 * T_SAMPLE // E
CAP = CAP_P + CAP_S
F_EXP = 2048
FT = F_EXP // P
D_PLE = 256
SEG = (0, T_PROMPT + 2 * PAD)
GLU_COLS = T_ALL + 4 * PAD
CHUNK_TILES = CHUNK // P
LN_EXP = "natural_log_exp_and_others"


def chunk_pos(c):
    return (0, c * CHUNK) if c * CHUNK < T_PROMPT else (1, c * CHUNK - T_PROMPT)


class Step(NamedTuple):
    u: int
    j: int
    h4: int
    q0: int
    tok0: int
    nt: int
    banks: int


class Kept:
    pass


class Chain:

    def __init__(self, eng, sem):
        self.eng, self.sem, self.n = eng, sem, 0

    def did(self, ins):
        ins.then_inc(self.sem, 1)
        self.n += 1
        return self.n

    def wait(self, n):
        self.eng.wait_ge(self.sem, n)


def conv_tap(K, engine, taps_ready, n, ct, r):
    tap, g = divmod(r, 2)
    cols = T_PROMPT if g == 0 else T_SAMPLE
    src = K.glu[:, ct, SEG[g] + tap:SEG[g] + tap + cols]
    acc = K.conv[:, ct, g * T_PROMPT:g * T_PROMPT + cols]
    w = K.conv_w[:, ct * (TAPS + 1) + tap:ct * (TAPS + 1) + tap + 1]
    if tap == 0:
        b = K.conv_w[:, ct * (TAPS + 1) + TAPS:(ct + 1) * (TAPS + 1)]
        engine.tensor_scalar(acc, src, w, b, ALU.mult, ALU.add).then_inc(taps_ready, 1)
    else:
        engine.wait_ge(taps_ready, n - 1)
        engine.scalar_tensor_tensor(acc, src, w, acc, ALU.mult, ALU.add).then_inc(taps_ready, 1)


POOL_CT = CT - 1
POOL_STEPS_1 = 4 * 18
POOL_STEPS = 4 * TAPS


def conv_on_pool(K, pool, product, first, last):
    for k in range(first, last):
        tap, r = divmod(k, 4)
        g = r % 2
        cols = T_PROMPT if g == 0 else T_SAMPLE
        at = slice(g * T_PROMPT, g * T_PROMPT + cols)
        col = POOL_CT * (TAPS + 1) + tap
        over = lambda c: K.conv_w[:, c:c + 1].broadcast_to((P, cols))
        acc = K.conv[:, POOL_CT, at]
        if k >= 2:
            pool.wait_ge(K.pool_taps, k - 1)
        if r < 2:
            src = K.glu[:, POOL_CT, SEG[g] + tap:SEG[g] + tap + cols]
            pool.tensor_tensor(acc if tap == 0 else product[:, at], src, over(col), ALU.mult).then_inc(K.pool_taps, 1)
        else:
            term = over(POOL_CT * (TAPS + 1) + TAPS) if tap == 0 else product[:, at]
            pool.tensor_tensor(acc, acc, term, ALU.add).then_inc(K.pool_taps, 1)


def stage_project(nc, K, io, sb, sem):
    flat = K.conv[:, :, :].rearrange("p c t -> p (c t)")
    x_ring = flat[:, 0:3 * D].rearrange("p (r d) -> p r d", r=3)
    gate_sig = flat[:, 3 * D:3 * D + 2 * T_ALL].rearrange("p (r c n) -> p r c n", r=2, c=CHUNKS)
    W_SLOTS = 3
    aT = sb("aT", [P, KD, T_ALL])
    w_ring = sb("w_ring", [P, W_SLOTS, KD, P])
    square = sb("square", [P, 2, CHUNK])
    inv = sb("inv", [P, 2, CHUNK])
    qn = sb("qn", [P, 2, CHUNK])
    by_cos = sb("by_cos", [P, 2, CHUNK])
    by_sin = sb("by_sin", [P, 2, CHUNK])
    cos = sb("cos", [P, T_PROMPT])
    sin = sb("sin", [P, T_PROMPT])
    junk = square[:, :, :].rearrange("p r n -> p (r n)")
    g1 = sb("g1", [P, KD])
    qkg, one = sb("qkg", [P, 2]), sb("one", [P, 1])
    ssq = sb("ssq", [P, TILES])
    ms = sb("ms", [P, TILES])
    rstd = sb("rstd", [P, TILES])

    consts_loaded = sem("consts_loaded")
    x_loaded = [sem(f"x_loaded{i}") for i in range(3)]
    w_loaded = [sem(f"w_loaded{i}") for i in range(W_SLOTS)]
    ssq_ready, ms_ready, rstd_ready = sem("ssq_ready"), sem("ms_ready"), sem("rstd_ready")
    xn_ready, tr_done, aT_ready = sem("xn_ready"), sem("tr_done"), sem("aT_ready")
    z_done, sig_ready, glu_done = sem("z_done"), sem("sig_ready"), sem("glu_done")
    sq_ready, ms_done, ln_ready, inv_ready, qn_ready = (sem(n) for n in ("sq_ready", "ms_done", "ln1_ready", "inv1_ready", "qn_ready"))
    rot_done, sin_ready = sem("rot_done"), sem("sin_ready")
    vh_ready, v_ready, one_ready = sem("vh_ready"), sem("v_ready"), sem("one_ready")
    dve_taps = sem("dve_taps")
    sum_ready, kh_ready = sem("sum_ready"), sem("kh_ready")
    dve_own, half_ready = sem("dve_own1"), sem("half_ready")

    PS = K.PS
    CONSTS = 10
    SL = [s for i in range(CT) for s in (("gate", i), ("val", i))]
    SL += [("k", j) for j in range(KV)] + [("q", i) for i in range(QT)] + [("v", 0)]
    NW = len(SL)
    NQK0 = 2 * CT * CHUNKS
    NK = KV * CHUNKS
    NQK = (KV + QT) * CHUNKS
    NV0 = NQK0 + NQK
    w_in = io["w_in"].rearrange("a (k p) n -> (a p) k n", p=P)
    col0 = {"val": 0, "gate": D_CONV, "q": 2 * D_CONV, "k": 2 * D_CONV + D_Q, "v": 2 * D_CONV + D_Q + KV * HD}

    def consumer(n):
        if n < NQK0:
            i, c = divmod(n, CHUNKS)
            return (sig_ready if i % 2 == 0 else glu_done), (i // 2) * CHUNKS + c + 1
        if n < NV0:
            return qn_ready, n - NQK0 + 1
        return v_ready, n - NV0 + 1

    def keys(ap, m):
        j, c = divmod(m, CHUNKS)
        return ap[:, j, c * CHUNK:(c + 1) * CHUNK]

    def v_product(t):
        return PS[:, 4 + (NV0 + t) % 4, 0:P].rearrange("p (j d) -> p j d", j=KV)

    with nc.Block() as block:

        @block.sync
        def _(sp):
            def load_x(t):
                if t >= 3:
                    sp.wait_ge(tr_done, t - 2)
                sp.dma_start(x_ring[:, t % 3, :], io["x_rows"](t)).then_inc(x_loaded[t % 3], 16)

            def load_w(i):
                if i >= W_SLOTS:
                    sp.wait_ge(z_done, CHUNKS * (i - W_SLOTS + 1))
                kind, n = SL[i]
                if kind == "k":
                    for d in range(2):
                        sp.dma_start(w_ring[:, i % W_SLOTS, :, d * HD:(d + 1) * HD],
                                     w_in[:, :, col0["k"] + n * HD:col0["k"] + (n + 1) * HD]).then_inc(w_loaded[i % W_SLOTS], 16)
                else:
                    c = col0[kind] + n * P
                    sp.dma_start(w_ring[:, i % W_SLOTS], w_in[:, :, c:c + P]).then_inc(w_loaded[i % W_SLOTS], 16)

            load_x(0)
            for dst, src in ((K.ident, io["ident"]), (g1, io["norm1_g"])):
                sp.dma_start(dst[:, :], src).then_inc(consts_loaded, 16)
            load_x(1)
            load_x(2)
            for dst, src in ((K.eps, io["eps_col"]), (K.head_ones, io["head_ones"]), (K.rot, io["rot"]),
                             (qkg, io["qk_gain"]), (cos, io["cos"]), (sin, io["sin"]), (K.conv_w, io["conv_w"]), (K.chan_mean, io["chan_mean"])):
                sp.dma_start(dst[:, :], src).then_inc(consts_loaded, 16)
            for i in range(W_SLOTS):
                load_w(i)
            for t in range(3, TILES):
                load_x(t)
            for i in range(W_SLOTS, NW):
                load_w(i)

        @block.gpsimd
        def _(pool):
            nc.gpsimd.memset(K.glu[:, :, :], 0.0).then_inc(K.glu_cleared, 1)
            nc.gpsimd.memset(one[:, :], 1.0).then_inc(one_ready, 1)
            nc.gpsimd.memset(K.minus_half[:, :], -0.5).then_inc(half_ready, 1)
            pool.wait_ge(half_ready, 1)
            for t in range(TILES):
                pool.wait_ge(ssq_ready, t + 1)
                nc.gpsimd.tensor_scalar(ms[:, t:t + 1], ssq[:, t:t + 1], 1.0 / D, EPS, ALU.mult, ALU.add).then_inc(ms_ready, 1)
                pool.wait_ge(ms_ready, t + 1)
                nc.gpsimd.tensor_tensor(rstd[:, t:t + 1], ms[:, t:t + 1], K.minus_half[:, :], ALU.pow).then_inc(rstd_ready, 1)
            pool.wait_ge(glu_done, CHUNKS * CT)
            conv_on_pool(K, nc.gpsimd, K.qT[:, QT - 1, :], 0, POOL_STEPS_1)

        @block.scalar
        def _(act):
            for t in range(TILES):
                act.wait_ge(x_loaded[t % 3], 16 * (t // 3 + 1))
                if t:
                    act.wait_ge(ssq_ready, t)
                nc.scalar.activation(junk, x_ring[:, t % 3, :], ACT.Square, accum_out=ssq[:, t:t + 1]).then_inc(ssq_ready, 1)
            act.wait_ge(consts_loaded, 16 * CONSTS)
            for p in range(CT):
                for c in range(CHUNKS):
                    act.wait_ge(z_done, 2 * p * CHUNKS + c + 1)
                    if p >= 2:
                        act.wait_ge(glu_done, (p - 2) * CHUNKS + c + 1)
                    nc.scalar.activation(gate_sig[:, p % 2, c, :], PS[:, 4 + (2 * p * CHUNKS + c) % 4, :], ACT.Sigmoid).then_inc(sig_ready, 1)

            nc.scalar.preload_act_table_set(LN_EXP)

            def inverse_root(m):
                act.wait_ge(ms_done, m + 1)
                if m >= 2:
                    act.wait_ge(qn_ready, m - 1)
                nc.scalar.activation(inv[:, m % 2, :], PS[:, m % 2, :], ACT.Ln, bias=K.eps[:, :]).then_inc(ln_ready, 1)
                act.wait_ge(ln_ready, m + 1)
                nc.scalar.activation(inv[:, m % 2, :], inv[:, m % 2, :], ACT.Exp, scale=-0.5).then_inc(inv_ready, 1)

            for m in range(NQK):
                act.wait_ge(z_done, NQK0 + m + 1)
                if m >= 2:
                    act.wait_ge(ms_done, m - 1)
                nc.scalar.activation(square[:, m % 2, :], PS[:, 4 + (NQK0 + m) % 4, :], ACT.Square).then_inc(sq_ready, 1)
                if m >= 1:
                    inverse_root(m - 1)
                if 0 <= m - 2 < NK:
                    act.wait_ge(sum_ready, m - 1)
                    nc.scalar.copy(keys(K.k_high, m - 2), by_cos[:, m % 2, :]).then_inc(kh_ready, 1)
            inverse_root(NQK - 1)
            for t in range(TILES):
                act.wait_ge(z_done, NV0 + t + 1)
                nc.scalar.copy(K.v_high[:, t, :, 0:HD], v_product(t)).then_inc(vh_ready, 1)

        @block.vector
        def _(dve):
            own = Chain(dve, dve_own)
            taps = [0]

            def conv_taps(n):
                for k in range(taps[0], min(taps[0] + n, POOL_CT * 2 * TAPS)):
                    ct, r = divmod(k, 2 * TAPS)
                    if r == 0:
                        dve.wait_ge(glu_done, CHUNKS * (ct + 1 if ct < 2 else CT))
                    conv_tap(K, nc.vector, dve_taps, k, ct, r)
                    taps[0] += 1

            def to_aT(t):
                dve.wait_ge(tr_done, t + 1)
                b = 2 * (t % 2)
                nc.vector.tensor_tensor(aT[:, :, t * P:(t + 1) * P],
                                        PS[:, b:b + 2, :].rearrange("p b (k n) -> p (b k) n", k=4),
                                        g1[:, :].unsqueeze(2).broadcast_to((P, KD, P)), ALU.mult).then_inc(aT_ready, 1)

            dve.wait_ge(consts_loaded, 16 * CONSTS)
            for t in range(TILES):
                dve.wait_ge(rstd_ready, t + 1)
                nc.vector.tensor_scalar(x_ring[:, t % 3, :], x_ring[:, t % 3, :], rstd[:, t:t + 1], None, ALU.mult).then_inc(xn_ready, 1)
                if t:
                    to_aT(t - 1)
            to_aT(TILES - 1)
            dve.wait_ge(one_ready, 1)
            nc.vector.tensor_copy(K.v_high[:, :, :, HD:P].rearrange("p t j n -> p (t j) n"),
                                  one[:, :].unsqueeze(2).broadcast_to((P, TILES * KV, HD)))
            dve.wait_ge(K.glu_cleared, 1)
            for p in range(CT):
                for c in range(CHUNKS):
                    n = (2 * p + 1) * CHUNKS + c
                    dve.wait_ge(z_done, n + 1)
                    dve.wait_ge(sig_ready, p * CHUNKS + c + 1)
                    g, t0 = chunk_pos(c)
                    o = SEG[g] + PAD + t0
                    nc.vector.tensor_tensor(K.glu[:, p, o:o + CHUNK], PS[:, 4 + n % 4, :], gate_sig[:, p % 2, c, :], ALU.mult).then_inc(glu_done, 1)
                    if p or c == CHUNKS - 1:
                        conv_taps(22 if c == CHUNKS - 1 else 6)
            for m in range(NQK):
                s, c = divmod(m, CHUNKS)
                i = m % 2
                kind, idx = SL[2 * CT + s]
                t0 = chunk_pos(c)[1]
                dve.wait_ge(inv_ready, m + 1)
                if m >= 2:
                    dve.wait_ge(rot_done, m - 1)
                gain = qkg[:, 0:1] if kind == "q" else qkg[:, 1:2]
                nc.vector.scalar_tensor_tensor(qn[:, i, :], PS[:, 4 + (NQK0 + m) % 4, :], gain, inv[:, i, :], ALU.mult, ALU.mult).then_inc(qn_ready, 1)
                dve.wait_ge(qn_ready, m + 1)
                own.did(nc.vector.tensor_tensor(by_cos[:, i, :], qn[:, i, :], cos[:, t0:t0 + CHUNK], ALU.mult))
                dve.wait_ge(rot_done, m + 1)
                nc.vector.tensor_tensor(by_sin[:, i, :], PS[:, 2 + i, :], sin[:, t0:t0 + CHUNK], ALU.mult).then_inc(sin_ready, 1)
                own.wait(own.n)
                dve.wait_ge(sin_ready, m + 1)
                if kind == "q":
                    if idx == QT - 1 and c == 0:
                        dve.wait_ge(K.pool_taps, POOL_STEPS_1)
                    nc.vector.tensor_tensor(K.qT[:, idx, c * CHUNK:(c + 1) * CHUNK], by_cos[:, i, :], by_sin[:, i, :], ALU.add)
                else:
                    nc.vector.tensor_tensor(by_cos[:, i, :], by_cos[:, i, :], by_sin[:, i, :], ALU.add).then_inc(sum_ready, 1)
                if 1 <= m <= NK:
                    dve.wait_ge(kh_ready, m)
                    nc.vector.tensor_tensor(keys(K.k_low, m - 1), by_cos[:, 1 - i, :], keys(K.k_high, m - 1).bitcast(F32), ALU.subtract)
                conv_taps(4)
            for t in range(TILES):
                dve.wait_ge(vh_ready, t + 1)
                nc.vector.tensor_tensor(K.v_low[:, t, :, :], v_product(t), K.v_high[:, t, :, 0:HD].bitcast(F32), ALU.subtract).then_inc(v_ready, 1)
                conv_taps(1)
            conv_taps(CT * 2 * TAPS)

        @block.tensor
        def _(pe):
            pe.wait_ge(consts_loaded, 16 * CONSTS)

            def turn(t):
                pe.wait_ge(xn_ready, t + 1)
                if t >= 2:
                    pe.wait_ge(aT_ready, t - 1)
                for k in range(KD):
                    b = 2 * (t % 2) + k // 4
                    mm = nc.tensor.transpose(PS[:, b, (k % 4) * P:(k % 4 + 1) * P], x_ring[:, t % 3, k * P:(k + 1) * P], K.ident[:, :])
                mm.then_inc(tr_done, 1)

            def bank_free(n):
                if n >= 4:
                    pe.wait_ge(*consumer(n - 4))

            def mean_square(m):
                pe.wait_ge(sq_ready, m + 1)
                if m >= 2:
                    pe.wait_ge(ln_ready, m - 1)
                nc.tensor.matmul(PS[:, m % 2, :], K.head_ones[:, :], square[:, m % 2, :], start=True, stop=True).then_inc(ms_done, 1)

            def rotate(m):
                pe.wait_ge(qn_ready, m + 1)
                if m >= 2:
                    pe.wait_ge(sin_ready, m - 1)
                nc.tensor.matmul(PS[:, 2 + m % 2, :], K.rot[:, :], qn[:, m % 2, :], start=True, stop=True).then_inc(rot_done, 1)

            loads = [0] * W_SLOTS
            for i, (kind, _idx) in enumerate(SL):
                loads[i % W_SLOTS] += 32 if kind == "k" else 16
                pe.wait_ge(w_loaded[i % W_SLOTS], loads[i % W_SLOTS])
                if kind == "v":
                    break
                for c in range(CHUNKS):
                    n = i * CHUNKS + c
                    if i == 0:
                        for t in range(c and (c + 1) * CHUNK_TILES, min(TILES, (c + 2) * CHUNK_TILES)):
                            turn(t)
                        pe.wait_ge(aT_ready, (c + 1) * CHUNK_TILES)
                    bank_free(n)
                    for k in range(KD):
                        mm = nc.tensor.matmul(PS[:, 4 + n % 4, :], w_ring[:, i % W_SLOTS, k, :], aT[:, k, c * CHUNK:(c + 1) * CHUNK],
                                              start=(k == 0), stop=(k == KD - 1))
                    mm.then_inc(z_done, 1)
                    m = n - NQK0
                    if m == 0:
                        pe.wait_ge(aT_ready, TILES)
                    if m >= 1:
                        mean_square(m - 1)
                    if m >= 2:
                        rotate(m - 2)
            mean_square(NQK - 1)
            rotate(NQK - 2)
            for t in range(TILES):
                bank_free(NV0 + t)
                for k in range(KD):
                    mm = nc.tensor.matmul(PS[:, 4 + (NV0 + t) % 4, 0:P], aT[:, k, t * P:(t + 1) * P], w_ring[:, (NW - 1) % W_SLOTS, k, :],
                                          start=(k == 0), stop=(k == KD - 1))
                mm.then_inc(z_done, 1)
                if t == 0:
                    rotate(NQK - 1)


def stage_attend(nc, K, io, sb, sem):
    units = [(g, i, j) for g, n in ((0, PTILES), (1, TILES - PTILES)) for i in range(n) for j in range(KV)]
    STEPS = len(units) * KV_GROUP
    q_parts = sb("q_parts", [P, 2, KV_GROUP, P], F32R)
    prob = sb("prob", [P, 2, T_PROMPT])
    ph, pl = (sb(n, [P, 2, PTILES, KV_GROUP, P], F32R) for n in ("probT_high", "probT_low"))
    nmax = sb("nmax", [P, STEPS])
    product = sb("conv_product", [P, T_ALL])
    inv_sum = sb("inv_sum", [HD, 2, KV_GROUP * P])
    qh_ready, ql_ready = sem("qh_ready"), sem("ql_ready")
    qk_done, nmax_ready, exp_done, tr_done = sem("qk_done"), sem("nmax_ready"), sem("exp_done"), sem("pt_done")
    ph_ready, pl_ready, pv_done = sem("ph_ready"), sem("pl_ready"), sem("pv_done")
    ln_ready, inv_ready, o_ready = sem("ln_sum_ready"), sem("inv_sum_ready"), sem("o_ready")
    PS = K.PS

    def step(n):
        g, i, j = units[n // KV_GROUP]
        tok0, ntile = (0, PTILES) if g == 0 else (T_PROMPT, TILES - PTILES)
        return Step(u=n // KV_GROUP, j=j, h4=n % KV_GROUP, q0=tok0 + i * P, tok0=tok0, nt=ntile, banks=ntile // 4)

    def scores(n):
        return PS[:, 2 * (n % 2):2 * (n % 2) + step(n).banks, :].rearrange("p b n -> p (b n)")

    def blocks(n):
        return sum(step(m).banks for m in range(n))

    def q_of(u, odd):
        s = step(u * KV_GROUP)
        return K.qT[odd * HD:(odd + 1) * HD, 2 * s.j:2 * s.j + 2, s.q0:s.q0 + P]

    def parts_of(u, odd, on):
        return q_parts[on * HD:(on + 1) * HD, u % 2, :, :].rearrange("p (a b) n -> p a b n", b=2)[:, :, odd, :]

    with nc.Block() as block:

        @block.tensor
        def _(pe):
            def score(n):
                s = step(n)
                if s.h4 == 0:
                    pe.wait_ge(ql_ready, 2 * (s.u + 1))
                for b in range(s.banks):
                    at = slice(s.tok0 + b * CHUNK, s.tok0 + (b + 1) * CHUNK)
                    nc.tensor.matmul(PS[:, 2 * (n % 2) + b, :], q_parts[:, s.u % 2, s.h4, :], K.k_high[:, s.j, at], start=True, stop=False)
                    mm = nc.tensor.matmul(PS[:, 2 * (n % 2) + b, :], q_parts[:, s.u % 2, s.h4, :], K.k_low[:, s.j, at],
                                          start=False, stop=True)
                mm.then_inc(qk_done, 1)

            def values(u, quarter):
                s = step(u * KV_GROUP)
                per = s.nt // 4
                if quarter == 0:
                    pe.wait_ge(pl_ready, blocks(KV_GROUP * (u + 1)))
                    if u >= 2:
                        pe.wait_ge(o_ready, 2 * (u - 1))
                for st in range(quarter * per, (quarter + 1) * per):
                    t = s.tok0 // P + st
                    nc.tensor.matmul(PS[:, 6 + u % 2, :], K.v_high[:, t, s.j, :], ph[:, u % 2, st, :, :], start=(st == 0), stop=False)
                    nc.tensor.matmul(PS[0:HD, 6 + u % 2, :], K.v_low[:, t, s.j, :], ph[:, u % 2, st, :, :], start=False, stop=False)
                    mm = nc.tensor.matmul(PS[:, 6 + u % 2, :], K.v_high[:, t, s.j, :], pl[:, u % 2, st, :, :],
                                          start=False, stop=(st == s.nt - 1))
                if quarter == 3:
                    mm.then_inc(pv_done, 1)

            score(0)
            score(1)
            for n in range(STEPS):
                s = step(n)
                pe.wait_ge(exp_done, n + 1)
                for b in range(s.banks):
                    x = blocks(n) + b
                    if x >= 2:
                        pe.wait_ge(pl_ready, x - 1)
                    for st in range(4):
                        mm = nc.tensor.transpose(PS[:, 4 + x % 2, st * P:(st + 1) * P], prob[:, n % 2, (4 * b + st) * P:(4 * b + st + 1) * P], K.ident[:, :])
                    mm.then_inc(tr_done, 1)
                if n + 2 < STEPS:
                    score(n + 2)
                if s.u >= 1:
                    values(s.u - 1, s.h4)
            for q in range(4):
                values(len(units) - 1, q)

        @block.gpsimd
        def _(pool):
            conv_on_pool(K, nc.gpsimd, product, POOL_STEPS_1, POOL_STEPS)

        @block.scalar
        def _(act):
            def high_queries(u):
                if u >= 2:
                    act.wait_ge(qk_done, KV_GROUP * (u - 1))
                for odd in range(2):
                    nc.scalar.mul(parts_of(u, odd, odd), q_of(u, odd), SCALE).then_inc(qh_ready, 1)

            def copy_out(n):
                s = step(n)
                for b in range(s.banks):
                    x = blocks(n) + b
                    act.wait_ge(tr_done, x + 1)
                    if s.u >= 2:
                        act.wait_ge(pv_done, s.u - 1)
                    nc.scalar.copy(ph[:, s.u % 2, 4 * b:4 * (b + 1), s.h4, :],
                                   PS[:, 4 + x % 2, :].rearrange("p (k n) -> p k n", k=4)).then_inc(ph_ready, 1)

            def invert_sums(u):
                act.wait_ge(pv_done, u + 1)
                if u >= 2:
                    act.wait_ge(o_ready, 2 * (u - 1))
                nc.scalar.activation(inv_sum[:, u % 2, :], PS[HD:P, 6 + u % 2, :], ACT.Ln).then_inc(ln_ready, 1)
                act.wait_ge(ln_ready, u + 1)
                nc.scalar.activation(inv_sum[:, u % 2, :], inv_sum[:, u % 2, :], ACT.Exp, scale=-1.0).then_inc(inv_ready, 1)

            high_queries(0)
            for n in range(STEPS):
                s = step(n)
                if n >= 1:
                    copy_out(n - 1)
                act.wait_ge(nmax_ready, n + 1)
                if n >= 2:
                    act.wait_ge(tr_done, blocks(n - 1))
                nc.scalar.activation(prob[:, n % 2, 0:s.nt * P], scores(n), ACT.Exp, bias=nmax[:, n:n + 1]).then_inc(exp_done, 1)
                if s.h4 == 0 and s.u + 1 < len(units):
                    high_queries(s.u + 1)
                if s.h4 == 1 and s.u >= 2:
                    invert_sums(s.u - 2)
            copy_out(STEPS - 1)
            invert_sums(len(units) - 2)
            invert_sums(len(units) - 1)

        @block.vector
        def _(dve):
            def low_queries(u):
                for odd in range(2):
                    dve.wait_ge(qh_ready, 2 * u + odd + 1)
                    nc.vector.scalar_tensor_tensor(parts_of(u, odd, 1 - odd), q_of(u, odd), SCALE, parts_of(u, odd, odd).bitcast(F32),
                                                   ALU.mult, ALU.subtract).then_inc(ql_ready, 1)

            def negated_max(n):
                dve.wait_ge(qk_done, n + 1)
                nc.vector.tensor_reduce(nmax[:, n:n + 1], scores(n), AX.X, ALU.max, negate=True).then_inc(nmax_ready, 1)

            def low_probs(n):
                s = step(n)
                for b in range(s.banks):
                    x = blocks(n) + b
                    dve.wait_ge(ph_ready, x + 1)
                    at = lambda buf: buf[:, s.u % 2, 4 * b:4 * (b + 1), s.h4, :]
                    nc.vector.tensor_tensor(at(pl), PS[:, 4 + x % 2, :].rearrange("p (k n) -> p k n", k=4), at(ph).bitcast(F32), ALU.subtract).then_inc(pl_ready, 1)

            def normalise(u):
                dve.wait_ge(inv_ready, u + 1)
                for odd in range(2):
                    pick = lambda ap: ap.rearrange("p (a b n) -> p a b n", b=2, n=P)[:, :, odd, :]
                    nc.vector.tensor_tensor(q_of(u, odd), pick(PS[0:HD, 6 + u % 2, :]), pick(inv_sum[:, u % 2, :]), ALU.mult).then_inc(o_ready, 1)

            low_queries(0)
            negated_max(0)
            for n in range(STEPS):
                s = step(n)
                if n >= 1:
                    low_probs(n - 1)
                if n + 1 < STEPS:
                    negated_max(n + 1)
                if s.h4 == 0 and s.u + 1 < len(units):
                    low_queries(s.u + 1)
                if s.h4 == 2 and s.u >= 2:
                    normalise(s.u - 2)
            low_probs(STEPS - 1)
            normalise(len(units) - 2)
            normalise(len(units) - 1)


def stage_mix_route(nc, K, io, sb, sem):
    wh, wl = sb("w_out_high", [P, KD, D], F32R), sb("w_out_low", [P, KD, D], F32R)
    mh, ml = sb("mix_high", [P, 2, KD, P], F32R), sb("mix_low", [P, 2, KD, P], F32R)
    sq = sb("sq", [P, CT, CHUNK])
    tile_sum = sb("tile_sum", [P, CHUNK])
    inv = sb("inv3", [P, 3, CHUNK])
    g2 = sb("g2", [P, D])
    w_r = sb("w_r", [P, KD, E])
    cg = sb("cg", [P, 4 * CT])
    h = sb("h", [P, 3, D])
    xn = sb("xn", [P, 3, D])
    xnT = sb("xnT", [P, KD, P])
    ssq, ms, rstd = sb("ssq3", [P, TILES]), sb("ms3", [P, TILES]), sb("rstd3", [P, TILES])
    rt = sb("rt", [P, 2, 4])
    ex = sb("ex", [P, 2, E])
    aff = sb("aff", [P, 2, E])
    affP, affS = sb("affP", [E, T_PROMPT]), sb("affS", [E, T_SAMPLE])
    valP, valS = sb("valP", [E, CAP_P]), sb("valS", [E, 2, CAP_S])
    idxP, idxS = sb("idxP", [E, CAP_P], U32), sb("idxS", [E, CAP_S], U32)
    idxPf, idxSf = sb("idxPf", [E, CAP_P]), sb("idxSf", [E, CAP_S])
    pT = sb("pT", [P, 2, 2, P])
    p_sb = sb("p_sb", [P, 2, D_PLE])
    w_pp = sb("w_pp", [P, 2, D])
    e_sb = sb("e_sb", [P, 2, D])
    junk = e_sb[:, 0, :]

    loaded = sem("loaded3")
    wout_loaded, wpp_loaded = [sem(f"wout_loaded{i}") for i in range(3)], sem("wpp_loaded")
    wh_ready, wl_ready, mh_ready, ml_ready = (sem(n) for n in ("wouth_ready", "woutl_ready", "mh_ready", "ml_ready"))
    x_loaded = [sem(f"x3_loaded{i}") for i in range(3)]
    stat_ready, sum_ready, stat_done = sem("stat_ready"), sem("tile_sum_ready"), sem("stat_done")
    centred, ln_ready, mix_ready = sem("centred"), sem("ln3_ready"), sem("mix_ready")
    silu_ready, inv_ready = sem("silu_ready"), sem("inv3_ready")
    out_done, h_ready, ssq_ready, ms_ready, rstd_ready = (sem(f"{n}3") for n in ("out_done", "h_ready", "ssq", "ms", "rstd"))
    xn_ready, tr_done, xnT_ready, logit_done, exp_ready = (sem(f"{n}3") for n in ("xn_ready", "tr_done", "xnT_ready", "logit_done", "exp_ready"))
    aff_ready, affT_done, affT_ready = sem("aff_ready"), sem("affT_done"), sem("affT_ready")
    h_stored = [sem(f"h_stored{i}") for i in range(3)]
    xn_stored = [sem(f"xn_stored{i}") for i in range(3)]
    topk_ready, topkT_done = sem("topk_ready"), sem("topkT_done")
    p_loaded = [sem(f"p_loaded{i}") for i in range(2)]
    e_stored = [sem(f"e_stored{i}") for i in range(2)]
    pT_done, pT_ready, e_done, e_ready = sem("pT_done"), sem("pT_ready"), sem("e_done"), sem("e_ready")
    own_sem = sem("dve_own3")
    PS = K.PS
    NEG = -1.0

    def conv_of(c):
        return K.conv[:, :, c * CHUNK:(c + 1) * CHUNK]

    def attn_of(c):
        return K.qT[:, :, c * CHUNK:(c + 1) * CHUNK]

    MEAN, VAR, MSC, MSA = range(4)
    EARLY = TILES * 2 // 3
    W_SPLIT = ((0, 2), (2, 5), (5, KD))
    LOADS = 16 * 3

    def mix_tile(t):
        at = slice(t * P, (t + 1) * P)
        return K.conv[:, :, at], K.qT[:, :, at]

    def split_early(t):
        return t + 1 < TILES and (t + 1) % CHUNK_TILES != 0

    def norm_ahead(t):
        part, c = t % CHUNK_TILES - 1, t // CHUNK_TILES + 1
        return (c, part) if t < TILES and part >= 0 and c < CHUNKS else None

    with nc.Block() as block:

        @block.sync
        def _(sp):
            for dst, src in ((cg[:, :], io["chan_gain"]), (w_r[:, :, :], io["w_router"].rearrange("a (k p) n -> (a p) k n", p=P)),
                             (g2[:, :], io["norm2_g"].partition_broadcast(P))):
                sp.dma_start(dst, src).then_inc(loaded, 16)
            for k in range(KD):
                if k >= 3:
                    sp.wait_ge(wl_ready, k - 2)
                sp.dma_start(xn[:, k % 3, :], io["w_out"][0, k * P:(k + 1) * P, :]).then_inc(wout_loaded[k % 3], 16)
            sp.dma_start(w_pp[:, :, :], io["ple_proj"].rearrange("a (k p) n -> (a p) k n", p=P)).then_inc(wpp_loaded, 16)
            for t in range(2):
                sp.dma_start(p_sb[:, t, :], io["p_rows"](t)).then_inc(p_loaded[t], 16)
            for t in range(TILES + 1):
                if t < TILES:
                    if t >= 3:
                        sp.wait_ge(h_stored[t % 3], 16 * (t // 3))
                        sp.wait_ge(ssq_ready, t - 2)
                        sp.wait_ge(xn_ready, t - 2)
                    sp.dma_start(h[:, t % 3, :], io["x_rows"](t)).then_inc(x_loaded[t % 3], 16)
                if t >= 1:
                    s = t - 1
                    sp.wait_ge(h_ready, s + 1)
                    sp.dma_start(K.h_rows(s), h[:, s % 3, :]).then_inc(h_stored[s % 3], 16)
                    sp.wait_ge(xn_ready, s + 1)
                    sp.dma_start(K.xn_rows(s), xn[:, s % 3, :]).then_inc(xn_stored[s % 3], 16)
            for t in range(TILES):
                if t + 2 < TILES:
                    sp.wait_ge(pT_done, t + 1)
                    sp.dma_start(p_sb[:, t % 2, :], io["p_rows"](t + 2)).then_inc(p_loaded[t % 2], 16)
                sp.wait_ge(e_ready, 2 * (t + 1))
                sp.dma_start(K.e_rows(t), e_sb[:, t % 2, :]).then_inc(e_stored[t % 2], 16)
            for i in range(3):
                sp.wait_ge(h_stored[i], 16 * (TILES // 3))
                sp.wait_ge(xn_stored[i], 16 * (TILES // 3))
            for i in range(2):
                sp.wait_ge(e_stored[i], 16 * (TILES // 2))

        @block.gpsimd
        def _(pool):
            for t in range(TILES):
                pool.wait_ge(ssq_ready, t + 1)
                nc.gpsimd.tensor_scalar(ms[:, t:t + 1], ssq[:, t:t + 1], 1.0 / D, EPS, ALU.mult, ALU.add).then_inc(ms_ready, 1)
                pool.wait_ge(ms_ready, t + 1)
                nc.gpsimd.tensor_tensor(rstd[:, t:t + 1], ms[:, t:t + 1], K.minus_half[:, :], ALU.pow).then_inc(rstd_ready, 1)

        def stat_no(c, which):
            return 4 * c + which + 1

        @block.scalar
        def _(act):
            def square_of(src):
                nc.scalar.activation(sq[:, :, :], src, ACT.Square).then_inc(stat_ready, 1)

            def inverse_root(c, n, which, user, count):
                act.wait_ge(stat_done, stat_no(c, which))
                if c:
                    act.wait_ge(user, count)
                nc.scalar.activation(inv[:, n, :], PS[:, 4, :], ACT.Ln, bias=K.eps[:, :]).then_inc(ln_ready, 1)
                act.wait_ge(ln_ready, 3 * c + n + 1)
                nc.scalar.activation(inv[:, n, :], inv[:, n, :], ACT.Exp, scale=-0.5).then_inc(inv_ready, 1)

            def chunk_norm(c, part):
                if part == 0:
                    act.wait_ge(centred, 2 * c + 1)
                    if c:
                        act.wait_ge(sum_ready, stat_no(c - 1, MSA))
                    square_of(conv_of(c))
                    inverse_root(c, 0, VAR, centred, 2 * c)
                elif part == 1:
                    act.wait_ge(centred, 2 * c + 2)
                    act.wait_ge(loaded, LOADS)
                    for i in range(CT):
                        s = nc.scalar.activation(conv_of(c)[:, i, :], conv_of(c)[:, i, :], ACT.Silu, bias=cg[:, CT + i:CT + i + 1],
                                                 scale=cg[:, i:i + 1])
                    s.then_inc(silu_ready, 1)
                    nc.scalar.preload_act_table_set(LN_EXP)
                    act.wait_ge(silu_ready, c + 1)
                    square_of(conv_of(c))
                    inverse_root(c, 1, MSC, mix_ready, (CT + QT) * (c - 1) + CT)
                else:
                    square_of(attn_of(c))
                    inverse_root(c, 2, MSA, mix_ready, (CT + QT) * c)

            def high_weights(first, last):
                for k in range(first, last):
                    act.wait_ge(wout_loaded[k % 3], 16 * (k // 3 + 1))
                    nc.scalar.copy(wh[:, k, :], xn[:, k % 3, :]).then_inc(wh_ready, 1)

            def high_mix(t):
                act.wait_ge(mix_ready, (CT + QT) * (t // CHUNK_TILES + 1))
                if t >= 2:
                    act.wait_ge(out_done, t - 1)
                for half, src in enumerate(mix_tile(t)):
                    nc.scalar.copy(mh[:, t % 2, half * CT:(half + 1) * CT, :], src).then_inc(mh_ready, 1)

            def route(t):
                act.wait_ge(logit_done, t + 1)
                act.wait_ge(aff_ready, 3 * t + 1)
                nc.scalar.activation(ex[:, t % 2, :], PS[:, 5, 0:E], ACT.Exp, bias=rt[:, t % 2, 0:1],
                                     accum_out=rt[:, t % 2, 1:2]).then_inc(exp_ready, 1)

            def copy_p(t):
                act.wait_ge(pT_done, t + 1)
                if t >= 2:
                    act.wait_ge(e_done, t - 1)
                nc.scalar.copy(pT[:, t % 2, :, :], PS[:, 6 + t % 2, 0:2 * P].rearrange("p (k n) -> p k n", k=2)).then_inc(pT_ready, 1)

            def embeddings(first, last):
                copy_p(first)
                for t in range(first, last):
                    if t + 1 < last:
                        copy_p(t + 1)
                    act.wait_ge(e_done, t + 1)
                    if t >= 2:
                        act.wait_ge(e_stored[t % 2], 16 * (t // 2))
                    for half in range(2):
                        nc.scalar.copy(e_sb[:, t % 2, half * CHUNK:(half + 1) * CHUNK], PS[:, 2 * (t % 2) + half, :]).then_inc(e_ready, 1)

            for part in range(3):
                chunk_norm(0, part)
                high_weights(*W_SPLIT[part])
            high_mix(0)
            for t in range(TILES + 3):
                if split_early(t):
                    high_mix(t + 1)
                if norm_ahead(t):
                    chunk_norm(*norm_ahead(t))
                if t == TILES:
                    embeddings(0, EARLY)
                if t < TILES:
                    act.wait_ge(h_ready, t + 1)
                    if t:
                        act.wait_ge(ssq_ready, t)
                    nc.scalar.activation(junk, h[:, t % 3, :], ACT.Square, accum_out=ssq[:, t:t + 1]).then_inc(ssq_ready, 1)
                if t + 1 < TILES and not split_early(t):
                    high_mix(t + 1)
                if 1 <= t < TILES + 1:
                    act.wait_ge(tr_done, t)
                    if t >= 2:
                        act.wait_ge(logit_done, t - 1)
                    nc.scalar.copy(xnT[:, :, :], PS[:, 6:8, :].rearrange("p b (k n) -> p (b k) n", k=4)).then_inc(xnT_ready, 1)
                if 2 <= t < TILES + 2:
                    route(t - 2)
            embeddings(EARLY, TILES)

        @block.vector
        def _(dve):
            own = Chain(dve, own_sem)

            def over_tiles(ap):
                return ap.unsqueeze(1).broadcast_to((P, CT, CHUNK))

            def sum_tiles(src, c, which):
                if stat_no(c, which) > 1:
                    dve.wait_ge(stat_done, stat_no(c, which) - 1)
                nc.vector.tensor_reduce(tile_sum[:, :], src.rearrange("p c n -> p n c"), AX.X, ALU.add).then_inc(sum_ready, 1)

            def sum_squares(c, part):
                dve.wait_ge(stat_ready, 3 * c + part + 1)
                sum_tiles(sq[:, :, :], c, (VAR, MSC, MSA)[part])

            def chunk_norm(c, part):
                if part == 0:
                    dve.wait_ge(stat_done, stat_no(c, MEAN))
                    nc.vector.tensor_tensor(conv_of(c), conv_of(c), over_tiles(PS[:, 4, :]), ALU.subtract).then_inc(centred, 1)
                    sum_squares(c, 0)
                    dve.wait_ge(inv_ready, 3 * c + 1)
                    dve.wait_ge(centred, 2 * c + 1)
                    nc.vector.tensor_tensor(conv_of(c), conv_of(c), over_tiles(inv[:, 0, :]), ALU.mult).then_inc(centred, 1)
                    return
                group, gains = (conv_of(c), 2 * CT) if part == 1 else (attn_of(c), 3 * CT)
                dve.wait_ge(inv_ready, 3 * c + part + 1)
                dve.wait_ge(loaded, LOADS)
                for i in range(CT):
                    nc.vector.scalar_tensor_tensor(group[:, i, :], group[:, i, :], cg[:, gains + i:gains + i + 1], inv[:, part, :],
                                                   ALU.mult, ALU.mult).then_inc(mix_ready, 1)

            def low_weights(first, last):
                for k in range(first, last):
                    dve.wait_ge(wh_ready, k + 1)
                    nc.vector.tensor_tensor(wl[:, k, :], xn[:, k % 3, :], wh[:, k, :].bitcast(F32), ALU.subtract).then_inc(wl_ready, 1)

            def low_mix(t):
                for half, src in enumerate(mix_tile(t)):
                    dve.wait_ge(mh_ready, 2 * t + half + 1)
                    at = lambda buf: buf[:, t % 2, half * CT:(half + 1) * CT, :]
                    nc.vector.tensor_tensor(at(ml), src, at(mh).bitcast(F32), ALU.subtract).then_inc(ml_ready, 1)

            def residual(t):
                dve.wait_ge(out_done, t + 1)
                dve.wait_ge(x_loaded[t % 3], 16 * (t // 3 + 1))
                b = 2 * (t % 2)
                nc.vector.tensor_tensor(h[:, t % 3, :].rearrange("p (b n) -> p b n", b=2), PS[:, b:b + 2, :],
                                        h[:, t % 3, :].rearrange("p (b n) -> p b n", b=2), ALU.add).then_inc(h_ready, 1)

            def norm(t):
                dve.wait_ge(rstd_ready, t + 1)
                dve.wait_ge(h_ready, t + 1)
                if t == 0:
                    dve.wait_ge(wl_ready, KD)
                if t >= 3:
                    dve.wait_ge(xn_stored[t % 3], 16 * (t // 3))
                    dve.wait_ge(tr_done, t - 2)
                nc.vector.scalar_tensor_tensor(xn[:, t % 3, :], h[:, t % 3, :], rstd[:, t:t + 1], g2[:, :], ALU.mult, ALU.mult).then_inc(xn_ready, 1)

            def route(t):
                i = t % 2
                dve.wait_ge(logit_done, t + 1)
                if t >= 2:
                    dve.wait_ge(exp_ready, t - 1)
                nc.vector.tensor_reduce(rt[:, i, 0:1], PS[:, 5, 0:E], AX.X, ALU.max, negate=True).then_inc(aff_ready, 1)
                dve.wait_ge(exp_ready, t + 1)
                nc.vector.reciprocal(rt[:, i, 2:3], rt[:, i, 1:2]).then_inc(aff_ready, 1)
                dve.wait_ge(aff_ready, 3 * t + 2)
                if t >= 2:
                    dve.wait_ge(affT_done, t - 1)
                nc.vector.tensor_scalar(aff[:, i, :], ex[:, i, :], rt[:, i, 2:3], None, ALU.mult).then_inc(aff_ready, 1)

            def keep_affinity(t):
                dve.wait_ge(affT_done, t + 1)
                dst = affP[:, t * P:(t + 1) * P] if t < PTILES else affS[:, (t - PTILES) * P:(t - PTILES + 1) * P]
                nc.vector.tensor_copy(dst, PS[0:E, 5, CHUNK // 2:CHUNK // 2 + P]).then_inc(affT_ready, 1)

            BESIDE = 4

            def top(vals, idx, a, first, last):
                a = a[:, :]
                for r in range(first, last):
                    v8, i8 = vals[:, 8 * r:8 * r + 8], idx[:, 8 * r:8 * r + 8]
                    own.wait(own.did(nc.vector.max(v8, a)))
                    own.wait(own.did(nc.vector.max_index(i8, v8, a)))
                    own.wait(own.did(nc.vector.match_replace(a, v8, a, NEG)))

            sum_tiles(conv_of(0), 0, MEAN)
            for part in range(3):
                if part:
                    sum_squares(0, part)
                chunk_norm(0, part)
                low_weights(*W_SPLIT[part])
            low_mix(0)
            for t in range(TILES + 3):
                ahead = norm_ahead(t)
                if split_early(t):
                    low_mix(t + 1)
                if ahead and ahead[1] == 0:
                    chunk_norm(*ahead)
                elif ahead:
                    sum_squares(*ahead)
                if t < TILES:
                    residual(t)
                if 3 <= t:
                    keep_affinity(t - 3)
                if ahead and ahead[1] > 0:
                    chunk_norm(*ahead)
                if t + 1 < TILES and not split_early(t):
                    low_mix(t + 1)
                if t < TILES:
                    norm(t)
                if 2 <= t < TILES + 2:
                    route(t - 2)
                if PTILES + 2 <= t < TILES:
                    top(valP, idxP, affP, BESIDE * (t - PTILES - 2), BESIDE * (t - PTILES - 1))
                if norm_ahead(t + 1) and norm_ahead(t + 1)[1] == 0:
                    sum_tiles(conv_of(norm_ahead(t + 1)[0]), norm_ahead(t + 1)[0], MEAN)
                if t == TILES - 1:
                    top(valP, idxP, affP, BESIDE * (TILES - PTILES - 2), CAP_P // 8 - 3)
                if t >= TILES:
                    top(valP, idxP, affP, CAP_P // 8 - 3 + t - TILES, CAP_P // 8 - 2 + t - TILES)
            dve.wait_ge(affT_ready, TILES)
            top(valS[:, 0, :], idxS, affS, 0, CAP_S // 8)
            nc.vector.tensor_copy(idxPf[:, :], idxP[:, :]).then_inc(topk_ready, 1)
            nc.vector.tensor_copy(idxSf[:, :], idxS[:, :]).then_inc(topk_ready, 1)
            nc.vector.tensor_copy(valS[:, 1, :], valS[:, 0, :]).then_inc(topk_ready, 1)
            dve.wait_ge(topkT_done, 1)
            own.did(nc.vector.tensor_copy(K.idxT_p[:, 0:E], PS[:, 5, 0:E]))
            own.did(nc.vector.tensor_copy(K.idxT_s[:, 0:E], PS[0:CAP_S, 5, E:2 * E]))
            own.did(nc.vector.tensor_copy(K.gateT_p[:, :], PS[:, 5, 2 * E:3 * E]))
            own.did(nc.vector.tensor_copy(K.gateT_s[:, :], PS[:, 5, 3 * E:4 * E]))

        @block.tensor
        def _(pe):
            def mean_of(c, which):
                pe.wait_ge(sum_ready, stat_no(c, which))
                nc.tensor.matmul(PS[:, 4, :], K.chan_mean[:, :], tile_sum[:, :], start=True, stop=True).then_inc(stat_done, 1)

            def first_mean(c):
                if c:
                    pe.wait_ge(ln_ready, 3 * c)
                mean_of(c, MEAN)

            def other_mean(c, n):
                if n == 0:
                    pe.wait_ge(centred, 2 * c + 1)
                else:
                    pe.wait_ge(ln_ready, 3 * c + n)
                mean_of(c, (VAR, MSC, MSA)[n])

            def transposes(t):
                pe.wait_ge(xn_ready, t + 1)
                if t:
                    pe.wait_ge(xnT_ready, t)
                for k in range(KD):
                    mm = nc.tensor.transpose(PS[:, 6 + k // 4, (k % 4) * P:(k % 4 + 1) * P], xn[:, t % 3, k * P:(k + 1) * P], K.ident[:, :])
                mm.then_inc(tr_done, 1)

            def logits(t):
                pe.wait_ge(xnT_ready, t + 1)
                if t:
                    pe.wait_ge(affT_ready, t)
                for k in range(KD):
                    mm = nc.tensor.matmul(PS[:, 5, 0:E], xnT[:, k, :], w_r[:, k, :], start=(k == 0), stop=(k == KD - 1))
                mm.then_inc(logit_done, 1)

            def turn_affinity(t):
                pe.wait_ge(aff_ready, 3 * t + 3)
                nc.tensor.transpose(PS[0:E, 5, CHUNK // 2:CHUNK // 2 + P], aff[:, t % 2, :], K.ident[:, :]).then_inc(affT_done, 1)

            def turn_p(t):
                pe.wait_ge(p_loaded[t % 2], 16 * (t // 2 + 1))
                if t == 0:
                    pe.wait_ge(xnT_ready, TILES - 1)
                if t == EARLY:
                    pe.wait_ge(xnT_ready, TILES)
                if t >= 2:
                    pe.wait_ge(pT_ready, t - 1)
                for k in range(2):
                    mm = nc.tensor.transpose(PS[:, 6 + t % 2, k * P:(k + 1) * P], p_sb[:, t % 2, k * P:(k + 1) * P], K.ident[:, :])
                mm.then_inc(pT_done, 1)

            def embeddings(first, last):
                turn_p(first)
                for t in range(first, last):
                    if t + 1 < last:
                        turn_p(t + 1)
                    pe.wait_ge(pT_ready, t + 1)
                    if t == 0:
                        pe.wait_ge(wpp_loaded, 16)
                        pe.wait_ge(h_ready, TILES)
                    if t >= 2:
                        pe.wait_ge(e_ready, 2 * (t - 1))
                    for k in range(2):
                        for half in range(2):
                            mm = nc.tensor.matmul(PS[:, 2 * (t % 2) + half, :], pT[:, t % 2, k, :], w_pp[:, k, half * CHUNK:(half + 1) * CHUNK],
                                                  start=(k == 0), stop=(k == 1))
                    mm.then_inc(e_done, 1)

            first_mean(0)
            for n in range(3):
                other_mean(0, n)
            pe.wait_ge(loaded, LOADS)
            for t in range(TILES + 3):
                c = t // CHUNK_TILES
                if t == TILES:
                    embeddings(0, EARLY)
                    pe.wait_ge(pT_ready, EARLY)
                ahead = norm_ahead(t)
                if ahead and ahead[1] == 0:
                    first_mean(c + 1)
                if t < TILES:
                    if t >= 2:
                        pe.wait_ge(h_ready, t - 1)
                    pe.wait_ge(ml_ready, 2 * (t + 1))
                    for k in range(KD):
                        if t == 0:
                            pe.wait_ge(wl_ready, k + 1)
                        for x, w in ((mh, wh), (mh, wl), (ml, wh)):
                            for half in range(2):
                                mm = nc.tensor.matmul(PS[:, 2 * (t % 2) + half, :], x[:, t % 2, k, :], w[:, k, half * CHUNK:(half + 1) * CHUNK],
                                                      start=(k == 0 and x is mh and w is wh), stop=(k == KD - 1 and x is ml))
                    mm.then_inc(out_done, 1)
                if 3 <= t:
                    turn_affinity(t - 3)
                if ahead:
                    other_mean(*ahead)
                if 1 <= t < TILES + 1:
                    transposes(t - 1)
                if 2 <= t < TILES + 2:
                    logits(t - 2)
            embeddings(EARLY, TILES)
            pe.wait_ge(topk_ready, 3)
            pe.wait_ge(affT_ready, TILES)
            small = K.ident[0:E, 0:E]
            nc.tensor.transpose(PS[:, 5, 0:E], idxPf[:, :], small)
            nc.tensor.transpose(PS[0:CAP_S, 5, E:2 * E], idxSf[:, :], small)
            nc.tensor.transpose(PS[:, 5, 2 * E:3 * E], valP[:, :], small)
            nc.tensor.transpose(PS[:, 5, 3 * E:4 * E], valS[:, :, :].rearrange("e a c -> e (a c)"), small).then_inc(topkT_done, 1)


def stage_experts(nc, K, io, sb, sem):
    RAW, HL = 6, 4
    NCH = 3 * FT // 2
    CC = 2048
    raw = sb("raw", [P, RAW, CC])
    wh, wl = sb("wh", [P, HL, CC], F32R), sb("wl", [P, HL, CC], F32R)
    xe_p, xe_s = sb("xe_p", [CAP_P, D]), sb("xe_s", [CAP_S, D])
    xhl = sb("xhl", [P, KD, 2, CAP], F32R)
    hhl = sb("hhl", [P, FT, 2 * CAP], F32R)
    HIGH, LOW_S, LOW_P, BOTH_S = slice(0, CAP), slice(CAP, CAP + CAP_S), slice(CAP + CAP_S, 2 * CAP), slice(CAP_P, CAP_P + 2 * CAP_S)
    gsum, usum, sg, hid = (sb(n, [P, 2, CAP]) for n in ("gsum", "usum", "sg", "hid"))
    y_p, y_s, y_low = sb("y_p", [CAP_P, D]), sb("y_s", [CAP_S, D]), sb("y_low", [CAP_S, D])
    ix_p, ix_s, sx_p, sx_s = sb("ix_p", [P, 1], U32), sb("ix_s", [CAP_S, 1], U32), sb("sx_p", [P, 1], U32), sb("sx_s", [CAP_S, 1], U32)
    gt_p, gt_s = sb("gt_p", [P, 1]), sb("gt_s", [P, 1])

    raw_loaded = [sem(f"raw_loaded{i}") for i in range(RAW)]
    high_ready = sem("high_ready")
    split_done = sem("split_done")
    down_used = sem("down_used")
    gathered_p, gathered_s = sem("gathered_p"), sem("gathered_s")
    index_ready, gates_ready, sindex_ready = sem("index_ready"), sem("gates_ready"), sem("sindex_ready")
    rows_asked = sem("rows_asked")
    xt_done, xh_ready, xl_ready = sem("xt_done"), sem("xh_ready"), sem("xl_ready")
    gate_done, up_done = sem("gate_done"), sem("up_done")
    gsum_ready, usum_ready = sem("gsum_ready"), sem("usum_ready")
    sg_ready, hid_ready, hh_ready, hl_ready = sem("sg_ready"), sem("hid_ready"), sem("hh_ready"), sem("hl_ready")
    yp_ready, ylow_ready, ys_ready = sem("yp_ready"), sem("ylow_ready"), sem("ys_ready")
    scat_p, scat_s = sem("scattered_p"), sem("scattered_s")
    PS = K.PS

    wg = io["w_gate"].rearrange("a e (k p) f -> (a e) p k f", p=P)
    wu = io["w_up"].rearrange("a e (k p) f -> (a e) p k f", p=P)
    wd = io["w_down"].rearrange("a e (k p) n -> (a e) p k n", p=P)

    def split_ready(eng, e, c):
        eng.wait_ge(split_done, e * NCH + (RAW + c + 1))

    with nc.Block() as block:

        @block.sync
        def _(sp):
            with sp.Fori(0, E) as e:
                for c in range(NCH):
                    sp.wait_ge(split_done, e * NCH + (c + 1))
                    dst = raw[:, c % RAW, :]
                    if c < FT:
                        src = (wg if c % 2 == 0 else wu)[bass.ds(e, 1), :, :, (c // 2) * 2 * P:(c // 2 + 1) * 2 * P].rearrange("e p k f -> (e p) k f")
                        dst = dst.rearrange("p (k f) -> p k f", k=KD)
                    else:
                        i = c - FT
                        src = wd[bass.ds(e, 1), :, 2 * i:2 * i + 2, :].rearrange("e p k n -> (e p) k n")
                        dst = dst.rearrange("p (k n) -> p k n", k=2)
                    sp.dma_start(dst, src).then_inc(raw_loaded[c % RAW], 16)
            sp.dma_start(K.w_pg[:, :, :], io["ple_gate_w"].rearrange("a (k p) n -> (a p) k n", p=P)).then_inc(K.wpg_loaded, 16)
            sp.wait_ge(scat_p, 16 * E)
            sp.wait_ge(scat_s, 16 * E)

        def loaded_wait(eng, e, c):
            eng.wait_ge(raw_loaded[c % RAW], e * (16 * NCH // RAW) + 16 * (c // RAW + 1))

        @block.gpsimd
        def _(pool):
            def gather(e, nth):
                nc.gpsimd.tensor_copy(ix_p[:, :], K.idxT_p[:, bass.ds(e, 1)]).then_inc(index_ready, 1)
                nc.gpsimd.tensor_copy(ix_s[:, :], K.idxT_s[:, bass.ds(e, 1)]).then_inc(index_ready, 1)
                pool.wait_ge(index_ready, nth * 2 + 2)
                pool.sem_inc(rows_asked, 1)
                nc.gpsimd.indirect_dma_start(xe_p[:, :], None, K.xn_p, bass.IndirectOffsetOnAxis(ap=ix_p[:, :], axis=0)).then_inc(gathered_p, 16)
                nc.gpsimd.indirect_dma_start(xe_s[:, :], None, K.xn_s, bass.IndirectOffsetOnAxis(ap=ix_s[:, :], axis=0)).then_inc(gathered_s, 16)

            def combine(f, nth):
                i = f % 2
                pool.wait_ge(sg_ready, nth + (f + 1))
                pool.wait_ge(usum_ready, nth + (f + 3))
                if f >= 2:
                    pool.wait_ge(hl_ready, 2 * nth + 2 * (f - 1))
                nc.gpsimd.tensor_tensor(hid[:, i, :], sg[:, i, :], usum[:, i, :], ALU.mult).then_inc(hid_ready, 1)

            def low_hid(f, nth):
                i = f % 2
                pool.wait_ge(hh_ready, nth + (f + 1))
                nc.gpsimd.tensor_tensor(hhl[:, f, LOW_P], hid[:, i, 0:CAP_P], hhl[:, f, 0:CAP_P].bitcast(F32), ALU.subtract).then_inc(hl_ready, 1)
                nc.gpsimd.tensor_tensor(hhl[:, f, LOW_S], hid[:, i, CAP_P:CAP], hhl[:, f, CAP_P:CAP].bitcast(F32), ALU.subtract).then_inc(hl_ready, 1)

            def body(e, first=False, last=False):
                for f in range(FT):
                    combine(f, e * FT)
                    if f:
                        low_hid(f - 1, e * FT)
                    if f == 1 and not first:
                        scatter(e - 1)
                    if f == 3 and not first:
                        pool.wait_ge(scat_p, e * 16)
                        pool.wait_ge(scat_s, e * 16)
                    if f == 3:
                        pool.wait_ge(yp_ready, e * 1 + 1)
                        pool.wait_ge(ys_ready, e * 1 + 1)
                        nc.gpsimd.tensor_copy(gt_p[:, :], K.gateT_p[:, bass.ds(e, 1)]).then_inc(gates_ready, 1)
                        nc.gpsimd.tensor_copy(gt_s[:, :], K.gateT_s[:, bass.ds(e, 1)]).then_inc(gates_ready, 1)
                    if f == 5 and not last:
                        pool.wait_ge(gathered_p, e * 16 + 16)
                        pool.wait_ge(gathered_s, e * 16 + 16)
                        pool.wait_ge(xt_done, e * 2 + 2)
                        gather(e + 1, e + 1)
                low_hid(FT - 1, e * FT)

            def scatter(e):
                nc.gpsimd.tensor_copy(sx_p[:, :], K.idxT_p[:, bass.ds(e, 1)]).then_inc(sindex_ready, 1)
                nc.gpsimd.tensor_copy(sx_s[:, :], K.idxT_s[:, bass.ds(e, 1)]).then_inc(sindex_ready, 1)
                pool.wait_ge(sindex_ready, e * 2 + 2)
                pool.wait_ge(yp_ready, e * 1 + 2)
                pool.sem_inc(rows_asked, 1)
                nc.gpsimd.indirect_dma_start(K.h_p, bass.IndirectOffsetOnAxis(ap=sx_p[:, :], axis=0), y_p[:, :], None,
                                             compute_op=ALU.add).then_inc(scat_p, 16)
                pool.wait_ge(ys_ready, e * 1 + 2)
                pool.sem_inc(rows_asked, 1)
                nc.gpsimd.indirect_dma_start(K.h_s, bass.IndirectOffsetOnAxis(ap=sx_s[:, :], axis=0), y_s[:, :], None,
                                             compute_op=ALU.add).then_inc(scat_s, 16)

            gather(0, 0)
            body(0, first=True)
            with pool.Fori(1, E - 1) as e:
                body(e)
            body(E - 1, last=True)
            pool.wait_ge(scat_p, 16 * (E - 1))
            pool.wait_ge(scat_s, 16 * (E - 1))
            scatter(E - 1)

        @block.scalar
        def _(act):
            act.sem_inc(yp_ready, 1)

            def high(e, c):
                loaded_wait(act, e, c)
                prev = c - HL
                if 0 <= prev < FT:
                    act.wait_ge(gate_done if prev % 2 == 0 else up_done, e * FT + (2 * (prev // 2) + 2))
                elif prev >= FT:
                    act.wait_ge(down_used, e * (FT // 2) + (prev - FT + 1))
                nc.scalar.copy(wh[:, c % HL, :], raw[:, c % RAW, :]).then_inc(high_ready, 1)

            def x_high(nth):
                for half in range(2):
                    act.wait_ge(xt_done, nth * 2 + (half + 1))
                    src = PS[:, 2 * half:2 * half + 2, 0:2 * CAP].rearrange("p b (k n) -> p b k n", k=2)
                    dst = xhl[:, 4 * half:4 * half + 4, 0, :].rearrange("p (b k) n -> p b k n", k=2)
                    nc.scalar.copy(dst, src).then_inc(xh_ready, 1)

            def gate_silu(e, f):
                i = f % 2
                act.wait_ge(gsum_ready, e * FT + (f + 3))
                if f >= 2:
                    act.wait_ge(hid_ready, e * FT + (f - 1))
                nc.scalar.activation(sg[:, i, :], gsum[:, i, :], ACT.Silu).then_inc(sg_ready, 1)

            def high_hid(e, f):
                i = f % 2
                act.wait_ge(hid_ready, e * FT + (f + 1))
                nc.scalar.copy(hhl[:, f, HIGH], hid[:, i, :]).then_inc(hh_ready, 1)

            def body(e, first=False, last=False):
                for fp in range(FT // 2):
                    for f in (2 * fp, 2 * fp + 1):
                        gate_silu(e, f)
                        if f:
                            high_hid(e, f - 1)
                    high(e, 2 * fp + 4)
                    high(e, 2 * fp + 5)
                high_hid(e, FT - 1)
                for c in range(FT + HL, NCH + (0 if last else HL)):
                    high(e, c)
                    if c == FT + HL + 1 and not last:
                        x_high(e + 1)
                act.wait_ge(down_used, e * (FT // 2) + FT // 2)
                act.wait_ge(gates_ready, e * 2 + 2)
                if not first:
                    act.wait_ge(scat_p, e * 16)
                nc.scalar.mul(y_p[:, :], PS[:, 4:6, :].rearrange("p b n -> p (b n)"), gt_p[:, 0:1]).then_inc(yp_ready, 1)
                act.wait_ge(ys_ready, e * 1 + 1)
                nc.scalar.mul(y_low[:, :], PS[CAP_S:P, 6:8, :].rearrange("p b n -> p (b n)"), gt_s[CAP_S:P, 0:1]).then_inc(ylow_ready, 1)

            high(0, 0)
            x_high(0)
            for c in range(1, HL):
                high(0, c)
            body(0, first=True)
            with act.Fori(1, E - 1) as e:
                body(e)
            body(E - 1, last=True)

        @block.vector
        def _(dve):
            dve.sem_inc(split_done, 2)
            dve.sem_inc(gsum_ready, 2)
            dve.sem_inc(usum_ready, 2)
            dve.sem_inc(ys_ready, 1)

            def low(e, c):
                dve.wait_ge(high_ready, e * NCH + (c + 1))
                nc.vector.tensor_tensor(wl[:, c % HL, :], raw[:, c % RAW, :], wh[:, c % HL, :].bitcast(F32), ALU.subtract).then_inc(split_done, 1)

            def x_low(nth):
                for half in range(2):
                    dve.wait_ge(xh_ready, nth * 2 + (half + 1))
                    src = PS[:, 2 * half:2 * half + 2, 0:2 * CAP].rearrange("p b (k n) -> p b k n", k=2)
                    at = lambda part: xhl[:, 4 * half:4 * half + 4, part, :].rearrange("p (b k) n -> p b k n", k=2)
                    nc.vector.tensor_tensor(at(1), src, at(0).bitcast(F32), ALU.subtract).then_inc(xl_ready, 1)

            def sums(e, f):
                i = f % 2
                for done, ready, dst, bank, read in ((gate_done, gsum_ready, gsum, i, sg_ready), (up_done, usum_ready, usum, 2 + i, hid_ready)):
                    dve.wait_ge(done, e * FT + (f + 1))
                    if f >= 2:
                        dve.wait_ge(read, e * FT + (f - 1))
                    nc.vector.tensor_reduce(dst[:, i, :], PS[:, bank, 0:2 * CAP].rearrange("p (a n) -> p n a", a=2), AX.X, ALU.add).then_inc(ready, 1)

            def body(e, first=False, last=False):
                for fp in range(FT // 2):
                    for f in (2 * fp, 2 * fp + 1):
                        sums(e, f)
                    low(e, 2 * fp + 4)
                    low(e, 2 * fp + 5)
                for c in range(FT + HL, NCH + (0 if last else HL)):
                    low(e, c)
                    if c == FT + HL + 1 and not last:
                        x_low(e + 1)
                dve.wait_ge(ylow_ready, e * 1 + 1)
                if not first:
                    dve.wait_ge(scat_s, e * 16)
                nc.vector.scalar_tensor_tensor(y_s[:, :], PS[0:CAP_S, 6:8, :].rearrange("p b n -> p (b n)"), gt_s[0:CAP_S, 0:1], y_low[:, :],
                                               ALU.mult, ALU.add).then_inc(ys_ready, 1)

            dve.wait_ge(gathered_p, 16)
            dve.wait_ge(gathered_s, 16)
            dve.sem_inc(split_done, RAW - 2)
            low(0, 0)
            x_low(0)
            for c in range(1, HL):
                low(0, c)
            body(0, first=True)
            with dve.Fori(1, E - 1) as e:
                body(e)
            body(E - 1, last=True)

        @block.tensor
        def _(pe):
            def turn(nth):
                pe.wait_ge(gathered_p, nth * 16 + 16)
                pe.wait_ge(gathered_s, nth * 16 + 16)
                pe.wait_ge(gsum_ready, nth * FT + 2)
                pe.wait_ge(usum_ready, nth * FT + 2)
                for k in range(KD):
                    b, o = k // 2, (k % 2) * CAP
                    nc.tensor.transpose(PS[:, b, o:o + CAP_P], xe_p[:, k * P:(k + 1) * P], K.ident[:, :])
                    mm = nc.tensor.transpose(PS[:, b, o + CAP_P:o + CAP], xe_s[:, k * P:(k + 1) * P], K.ident[0:CAP_S, 0:CAP_S])
                    if k % 4 == 3:
                        mm.then_inc(xt_done, 1)

            def gate_up(e, f):
                i, sub = f % 2, f % 2
                for part, (bank, free, done) in enumerate(((i, gsum_ready, gate_done), (2 + i, usum_ready, up_done))):
                    c = (f // 2) * 2 + part
                    if sub == 0:
                        split_ready(pe, e, c)
                    pe.wait_ge(free, e * FT + (f + 1))
                    hi = wh[:, c % HL, :].rearrange("p (k f) -> p k f", k=KD)
                    lo = wl[:, c % HL, :].rearrange("p (k f) -> p k f", k=KD)
                    for k in range(KD):
                        nc.tensor.matmul(PS[:, bank, 0:2 * CAP], hi[:, k, sub * P:(sub + 1) * P], xhl[:, k, :, :].rearrange("p a n -> p (a n)"),
                                         start=(k == 0), stop=False)
                        mm = nc.tensor.matmul(PS[:, bank, 0:CAP], lo[:, k, sub * P:(sub + 1) * P], xhl[:, k, 0, :],
                                              start=False, stop=(k == KD - 1))
                    mm.then_inc(done, 1)

            def down(e, f):
                c = FT + f // 2
                if f % 2 == 0:
                    split_ready(pe, e, c)
                pe.wait_ge(hl_ready, e * (2 * FT) + 2 * (f + 1))
                if f == 0:
                    pe.wait_ge(yp_ready, e * 1 + 1)
                    pe.wait_ge(ys_ready, e * 1 + 1)
                at = (f % 2) * D
                hi = [wh[:, c % HL, at + n * CHUNK:at + (n + 1) * CHUNK] for n in range(2)]
                lo = [wl[:, c % HL, at + n * CHUNK:at + (n + 1) * CHUNK] for n in range(2)]
                ph, pl, both = hhl[:, f, 0:CAP_P], hhl[:, f, LOW_P], hhl[:, f, BOTH_S]
                first, final = f == 0, f == FT - 1
                for n in range(2):
                    nc.tensor.matmul(PS[:, 4 + n, :], ph, hi[n], start=first, stop=False)
                for n in range(2):
                    nc.tensor.matmul(PS[:, 4 + n, :], ph, lo[n], start=False, stop=False)
                for n in range(2):
                    nc.tensor.matmul(PS[:, 4 + n, :], pl, hi[n], start=False, stop=final)
                for n in range(2):
                    nc.tensor.matmul(PS[:, 6 + n, :], both, hi[n], start=first, stop=False)
                for n in range(2):
                    mm = nc.tensor.matmul(PS[:, 6 + n, :], both, lo[n], start=False, stop=final)
                return mm

            def body(e, first=False, last=False):
                pe.wait_ge(xl_ready, e * 2 + 2)
                for f in range(FT):
                    gate_up(e, f)
                for f in range(FT):
                    mm = down(e, f)
                    if f % 2 == 1:
                        mm.then_inc(down_used, 1)
                    if f == 3 and not last:
                        turn(e + 1)

            turn(0)
            body(0, first=True)
            with pe.Fori(1, E - 1) as e:
                body(e)
            body(E - 1, last=True)


def stage_embed(nc, K, io, sb, sem):
    wh, wl = sb("pgh", [P, KD, D], F32R), sb("pgl", [P, KD, D], F32R)
    g3, bias = sb("g3", [P, D]), sb("bias", [P, D])
    H = 6
    h, e_in = sb("h5", [P, H, D]), sb("e_in", [P, 2, D])
    hn = sb("hn", [P, 2, D])
    nh, nl = sb("hnT_high", [P, 3, KD, P], F32R), sb("hnT_low", [P, 3, KD, P], F32R)
    pre, out = sb("pre", [P, 2, D]), sb("out5", [P, 2, D])
    sig = sb("sig", [P, D])
    ssq, ms, rstd = sb("ssq5", [P, TILES]), sb("ms5", [P, TILES]), sb("rstd5", [P, TILES])
    gain_loaded, bias_loaded = sem("gain5_loaded"), sem("bias_loaded")
    h_loaded = [sem(f"h5_loaded{i}") for i in range(H)]
    e_loaded = [sem(f"e5_loaded{i}") for i in range(2)]
    out_stored = [sem(f"out_stored{i}") for i in range(2)]
    ssq_ready, ms_ready, rstd_ready = sem("ssq5_ready"), sem("ms5_ready"), sem("rstd5_ready")
    wh_ready, wl_ready = sem("pgh_ready"), sem("pgl_ready")
    hn_ready, tr_done, high_ready, low_ready, gate_done = sem("hn_ready"), sem("tr5_done"), sem("nh_ready"), sem("nl_ready"), sem("gate5_done")
    pre_ready, sig_ready, prod_ready, out_ready = sem("pre_ready"), sem("sig5_ready"), sem("prod_ready"), sem("out_ready")
    PS = K.PS

    def turned():
        return PS[:, 6:8, :].rearrange("p b (k n) -> p (b k) n", k=4)

    with nc.Block() as block:

        @block.sync
        def _(sp):
            def load(t):
                if t >= H:
                    sp.wait_ge(out_ready, t - H + 1)
                sp.dma_start(h[:, t % H, :], K.h_rows(t)).then_inc(h_loaded[t % H], 16)

            load(0)
            sp.dma_start(g3[:, :], io["ple_norm_g"].partition_broadcast(P)).then_inc(gain_loaded, 16)
            for t in range(1, H):
                load(t)
            sp.dma_start(bias[:, :], io["ple_gate_b"].partition_broadcast(P)).then_inc(bias_loaded, 16)
            for t in range(TILES):
                if t >= 2:
                    sp.wait_ge(prod_ready, t - 1)
                sp.dma_start(e_in[:, t % 2, :], K.e_rows(t)).then_inc(e_loaded[t % 2], 16)
                if t >= 1:
                    sp.wait_ge(out_ready, t)
                    sp.dma_start(io["out_rows"](t - 1), out[:, (t - 1) % 2, :]).then_inc(out_stored[(t - 1) % 2], 16)
                    if t - 1 + H < TILES:
                        load(t - 1 + H)
            sp.wait_ge(out_ready, TILES)
            sp.dma_start(io["out_rows"](TILES - 1), out[:, (TILES - 1) % 2, :]).then_inc(out_stored[(TILES - 1) % 2], 16)
            for i in range(2):
                sp.wait_ge(out_stored[i], 16 * (TILES // 2))

        @block.gpsimd
        def _(pool):
            for t in range(TILES):
                pool.wait_ge(ssq_ready, t + 1)
                nc.gpsimd.tensor_scalar(ms[:, t:t + 1], ssq[:, t:t + 1], 1.0 / D, EPS, ALU.mult, ALU.add).then_inc(ms_ready, 1)
                pool.wait_ge(ms_ready, t + 1)
                nc.gpsimd.tensor_tensor(rstd[:, t:t + 1], ms[:, t:t + 1], K.minus_half[:, :], ALU.pow).then_inc(rstd_ready, 1)

        @block.scalar
        def _(act):
            def square(t):
                act.wait_ge(h_loaded[t % H], 16 * (t // H + 1))
                if t >= 2:
                    act.wait_ge(sig_ready, t - 1)
                nc.scalar.activation(pre[:, t % 2, :], h[:, t % H, :], ACT.Square, accum_out=ssq[:, t:t + 1]).then_inc(ssq_ready, 1)

            def high(t):
                act.wait_ge(tr_done, t + 1)
                if t >= 3:
                    act.wait_ge(gate_done, t - 2)
                nc.scalar.copy(nh[:, t % 3, :, :], turned()).then_inc(high_ready, 1)

            def sigmoid(t):
                act.wait_ge(pre_ready, t + 1)
                if t:
                    act.wait_ge(prod_ready, t)
                nc.scalar.activation(sig[:, :], pre[:, t % 2, :], ACT.Sigmoid).then_inc(sig_ready, 1)

            act.wait_ge(K.wpg_loaded, 16)
            for k in range(KD):
                nc.scalar.copy(wh[:, k, :], K.w_pg[:, k, :]).then_inc(wh_ready, 1)
                if k == 2:
                    square(0)
                    square(1)
                if k == 4:
                    high(0)
            high(1)
            for t in range(TILES):
                sigmoid(t)
                if t + 2 < TILES:
                    square(t + 2)
                    high(t + 2)

        @block.vector
        def _(dve):
            def norm(t):
                dve.wait_ge(rstd_ready, t + 1)
                if t >= 2:
                    dve.wait_ge(tr_done, t - 1)
                nc.vector.scalar_tensor_tensor(hn[:, t % 2, :], h[:, t % H, :], rstd[:, t:t + 1], g3[:, :], ALU.mult, ALU.mult).then_inc(hn_ready, 1)

            def low(t):
                dve.wait_ge(high_ready, t + 1)
                nc.vector.tensor_tensor(nl[:, t % 3, :, :], turned(), nh[:, t % 3, :, :].bitcast(F32), ALU.subtract).then_inc(low_ready, 1)

            def low_weights(k):
                dve.wait_ge(wh_ready, k + 1)
                nc.vector.tensor_tensor(wl[:, k, :], K.w_pg[:, k, :], wh[:, k, :].bitcast(F32), ALU.subtract).then_inc(wl_ready, 1)

            halves = lambda ap: ap.rearrange("p (b n) -> p b n", b=2)
            for k in range(KD):
                low_weights(k)
                if k == 2:
                    dve.wait_ge(gain_loaded, 16)
                    norm(0)
                    norm(1)
                if k == 4:
                    low(0)
            low(1)
            dve.wait_ge(bias_loaded, 16)
            for t in range(TILES):
                i = t % 2
                dve.wait_ge(gate_done, t + 1)
                dve.wait_ge(ssq_ready, t + 1)
                nc.vector.tensor_tensor(halves(pre[:, i, :]), PS[:, 2 * i:2 * i + 2, :], halves(bias[:, :]), ALU.add).then_inc(pre_ready, 1)
                if t + 2 < TILES:
                    norm(t + 2)
                dve.wait_ge(sig_ready, t + 1)
                dve.wait_ge(e_loaded[i], 16 * (t // 2 + 1))
                if t >= 2:
                    dve.wait_ge(out_stored[i], 16 * (t // 2))
                nc.vector.tensor_tensor(out[:, i, :], sig[:, :], e_in[:, i, :], ALU.mult).then_inc(prod_ready, 1)
                dve.wait_ge(prod_ready, t + 1)
                nc.vector.tensor_tensor(out[:, i, :], out[:, i, :], h[:, t % H, :], ALU.add).then_inc(out_ready, 1)
                if t + 2 < TILES:
                    low(t + 2)

        @block.tensor
        def _(pe):
            def turn(t):
                pe.wait_ge(hn_ready, t + 1)
                if t:
                    pe.wait_ge(low_ready, t)
                for k in range(KD):
                    mm = nc.tensor.transpose(PS[:, 6 + k // 4, (k % 4) * P:(k % 4 + 1) * P], hn[:, t % 2, k * P:(k + 1) * P], K.ident[:, :])
                mm.then_inc(tr_done, 1)

            turn(0)
            turn(1)
            for t in range(TILES):
                pe.wait_ge(low_ready, t + 1)
                if t >= 2:
                    pe.wait_ge(pre_ready, t - 1)
                b = 2 * (t % 2)
                for k in range(KD):
                    if t == 0:
                        pe.wait_ge(wl_ready, k + 1)
                    for x, w in ((nh, wh), (nh, wl), (nl, wh)):
                        for half in range(2):
                            mm = nc.tensor.matmul(PS[:, b + half, :], x[:, t % 3, k, :], w[:, k, half * CHUNK:(half + 1) * CHUNK],
                                                  start=(k == 0 and x is nh and w is wh), stop=(k == KD - 1 and x is nl))
                    if k == KD // 2 and 0 < t and t + 1 < TILES:
                        turn(t + 1)
                mm.then_inc(gate_done, 1)


def encoder_layer_kernel(nc, io, stages=5):
    K = Kept()

    def rows(prompt, sample):
        return lambda t: prompt[t * P:(t + 1) * P, :] if t < PTILES else sample[(t - PTILES) * P:(t - PTILES + 1) * P, :]

    io["x_rows"] = rows(io["x_prompt"][0], io["x_sample"][0])
    io["p_rows"] = rows(io["p_prompt"][0, 0], io["p_sample"][0, 0])
    io["out_rows"] = rows(io["y_prompt"][0], io["y_sample"][0])
    def scratch(name):
        return [nc.dram_tensor(f"{name}_rows_{g}", (t, D), F32, kind="Internal").ap() for g, t in (("p", T_PROMPT), ("s", T_SAMPLE))]

    K.h_p, K.h_s = scratch("h")
    K.xn_p, K.xn_s = scratch("xn")
    K.h_rows, K.xn_rows, K.e_rows = rows(K.h_p, K.h_s), rows(K.xn_p, K.xn_s), rows(*scratch("e"))

    with ExitStack() as whole:
        def alloc(stack):
            return lambda name, shape, dt=F32: stack.enter_context(nc.sbuf_tensor(name, shape, dt))

        def sem(name):
            return whole.enter_context(nc.semaphore(name))

        keep = alloc(whole)
        K.PS = whole.enter_context(nc.psum_tensor("PS", [P, 8, CHUNK], F32))
        K.ident, K.eps, K.minus_half = keep("ident", [P, P]), keep("eps", [P, 1]), keep("minus_half", [P, 1])
        K.idxT_p, K.idxT_s = keep("idxT_p", [P, E], U32), keep("idxT_s", [CAP_S, E], U32)
        K.gateT_p, K.gateT_s = keep("gateT_p", [P, E]), keep("gateT_s", [P, E])
        K.glu_cleared = sem("glu_cleared")
        with ExitStack() as mixers:
            part = alloc(mixers)
            K.qT, K.conv = part("qT", [P, QT, T_ALL]), part("conv", [P, CT, T_ALL])
            K.chan_mean = part("chan_mean", [P, P])
            K.pool_taps = sem("pool_taps")
            with ExitStack() as attention:
                part = alloc(attention)
                K.k_high, K.k_low = part("k_high", [P, KV, T_ALL], F32R), part("k_low", [P, KV, T_ALL], F32R)
                K.v_high, K.v_low = part("v_high", [P, TILES, KV, P], F32R), part("v_low", [P, TILES, KV, HD], F32R)
                K.conv_w = part("conv_w", [P, CT * (TAPS + 1)])
                K.head_ones, K.rot = part("head_ones", [P, P]), part("rot", [P, P])
                K.glu = part("glu", [P, CT, GLU_COLS])
                with ExitStack() as s:
                    stage_project(nc, K, io, alloc(s), sem)
                if stages >= 2:
                    with ExitStack() as s:
                        stage_attend(nc, K, io, alloc(s), sem)
            if stages >= 3:
                with ExitStack() as s:
                    stage_mix_route(nc, K, io, alloc(s), sem)
        K.w_pg, K.wpg_loaded = keep("w_pg", [P, KD, D]), sem("wpg_loaded")
        if stages >= 4:
            with ExitStack() as s:
                stage_experts(nc, K, io, alloc(s), sem)
        if stages >= 5:
            with ExitStack() as s:
                stage_embed(nc, K, io, alloc(s), sem)


def shape_constants():
    import numpy as np
    f = np.float32
    half = HD // 4
    freqs = (f(1.0) / (f(10000.0) ** (np.arange(0, HD // 2, 2, dtype=f) / f(HD // 2)))).astype(f)
    t = np.arange(T_PROMPT)
    ang = np.zeros((HD, T_PROMPT), f)
    for d in range(HD):
        pos = (t // 64 if d < HD // 2 else t % 64).astype(f)
        ang[d] = pos * freqs[d % half]
    two = lambda a: np.ascontiguousarray(np.concatenate([a, a], 0).astype(f))
    rot = np.zeros((P, P), f)
    for base in range(0, P, HD // 2):
        for i in range(half):
            rot[base + half + i, base + i] = -1.0
            rot[base + i, base + half + i] = 1.0
    head_ones = np.kron(np.eye(P // HD), np.full((HD, HD), 1.0 / HD)).astype(f)
    return dict(cos=two(np.cos(ang)), sin=two(np.sin(ang)), rot=rot, head_ones=head_ones, ident=np.eye(P, dtype=f),
                chan_mean=np.full((P, P), 1.0 / D_CONV, f), eps_col=np.full((P, 1), EPS, f))


def layouts(inputs):
    import numpy as np
    a = {n: np.ascontiguousarray(v) for n, v in inputs.items()}
    col = lambda v, k: np.ascontiguousarray(v.reshape(k, P).T)
    a["norm1_g"] = col(a["norm1_g"], KD)
    a["qk_gain"] = np.ascontiguousarray(np.stack([np.tile(a.pop("q_norm_g")[0], 2), np.tile(a.pop("k_norm_g")[0], 2)], 1))
    taps = np.concatenate([a.pop("conv_dw_w")[0], a.pop("conv_dw_b")], 0)
    a["conv_w"] = np.ascontiguousarray(taps.reshape(TAPS + 1, CT, P).transpose(2, 1, 0).reshape(P, CT * (TAPS + 1)))
    a["chan_gain"] = np.ascontiguousarray(np.concatenate([col(a.pop(n), CT) for n in ("conv_ln_g", "conv_ln_b", "conv_out_g", "attn_out_g")], 1))
    for n in ("norm2_g", "ple_norm_g", "ple_gate_b"):
        a[n] = a[n].reshape(D)
    return a | shape_constants()


def kernel(**inputs):
    import concourse.bacc as _bacc
    from concourse.bass_utils import run_bass_kernel_spmd as _run

    arrays = layouts(inputs)
    nc = _bacc.Bacc("TRN2", target_bir_lowering=False, num_devices=1)
    io = {name: nc.dram_tensor(f"in_{name}", a.shape, mybir.dt.from_np(a.dtype), kind="ExternalInput").ap()
          for name, a in arrays.items()}
    for name, t in (("y_prompt", T_PROMPT), ("y_sample", T_SAMPLE)):
        io[name] = nc.dram_tensor(f"out_{name}", (1, t, D), F32, kind="ExternalOutput").ap()
    encoder_layer_kernel(nc, io)
    r = _run(nc, [{f"in_{n}": a for n, a in arrays.items()}], core_ids=[0])
    return r.results[0]["out_y_prompt"], r.results[0]["out_y_sample"]
```
